# Optimizing a Trainium2 kernel written in Bass

```python
import jax, jax.numpy as jnp
from jax import lax
import numpy as np
import math

D_MODEL = 1024
BATCH = 1
SEQ = 512
DEPTH = 2

GRID_W = 64
CTX_LEN = 256
N_MIXERS = 2
N_FNET_LAYERS = (DEPTH + 1) // 2
N_RWKV_LAYERS = DEPTH // 2
N_VRES_LAYERS = N_RWKV_LAYERS - 1
FNET_GROUPS = 4
FNET_GROUP_DIM = D_MODEL // FNET_GROUPS
HEAD_SIZE = 64
N_HEADS = D_MODEL // HEAD_SIZE
D_DECAY_LORA = 64
D_AAA_LORA = 64
D_MV_LORA = 32
D_GATE_LORA = 128
N_DIRS = 2
N_EXPERTS = 16
D_EXPERT = 1024
CAPACITY_FACTOR = 2
NORM_EPS = 1e-6
LNX_EPS = 64e-5


def rmsnorm(h, g):
    hf = h.astype(jnp.float32)
    hf = hf * lax.rsqrt(jnp.mean(hf * hf, axis=-1, keepdims=True) + NORM_EPS)
    return (hf * g.astype(jnp.float32)).astype(h.dtype)

def adaln_params(cvec, w, b):
    return jnp.split(jax.nn.silu(cvec) @ w + b, 6, axis=-1)

def fourier_mix(h, w_o, b_o):
    bsz, t, _ = h.shape
    hg = h.astype(jnp.float32).reshape(bsz, t, FNET_GROUPS, FNET_GROUP_DIM)
    f = jnp.fft.fft2(hg, axes=(1, 3), norm='ortho').real
    return f.reshape(bsz, t, D_MODEL).astype(h.dtype) @ w_o + b_o

def qshift_grid(h):
    bsz, t, d = h.shape
    rows = t // GRID_W
    g = h.reshape(bsz, rows, GRID_W, d)
    q = d // 4
    left = jnp.pad(g[:, :, :-1, :q], ((0, 0), (0, 0), (1, 0), (0, 0)))
    right = jnp.pad(g[:, :, 1:, q:2 * q], ((0, 0), (0, 0), (0, 1), (0, 0)))
    up = jnp.pad(g[:, :-1, :, 2 * q:3 * q], ((0, 0), (1, 0), (0, 0), (0, 0)))
    down = jnp.pad(g[:, 1:, :, 3 * q:], ((0, 0), (0, 1), (0, 0), (0, 0)))
    return jnp.concatenate([left, right, up, down], axis=-1).reshape(bsz, t, d)

def shift_seq(h):
    half = h.shape[-1] // 2
    prev = jnp.pad(h[:, :-1, :half], ((0, 0), (1, 0), (0, 0)))
    nxt = jnp.pad(h[:, 1:, half:], ((0, 0), (0, 1), (0, 0)))
    return jnp.concatenate([prev, nxt], axis=-1)

def to_heads(t):
    return t.reshape(t.shape[0], t.shape[1], N_HEADS, HEAD_SIZE)

def rwkv_project(h, h_shift, mix, wr, wk, wv, w0, w1, w2, a0, a1, a2, g1, g2, k_k, k_a, v_first, vres):
    xx = h_shift - h
    xr, xw, xk, xv, xa, xg = [h + xx * mix[j] for j in range(6)]
    r = xr @ wr
    k = xk @ wk
    v = xv @ wv
    if vres is not None:
        v0, v1, v2 = vres
        v = v + (v_first - v) * jax.nn.sigmoid(v0 + (xv @ v1) @ v2)
    g = jax.nn.sigmoid(xg @ g1) @ g2
    kk = to_heads((k * k_k).astype(jnp.float32))
    kk = kk * lax.rsqrt(jnp.sum(kk * kk, axis=-1, keepdims=True) + 1e-12)
    kf = k.astype(jnp.float32)
    dirs = []
    for d in range(N_DIRS):
        wlog = (w0[d] + jnp.tanh(xw @ w1[d]) @ w2[d]).astype(jnp.float32)
        wlog = -jax.nn.softplus(-wlog) - 0.5
        decay = jnp.exp(-jnp.exp(wlog))
        a = jax.nn.sigmoid((a0[d] + (xa @ a1[d]) @ a2[d]).astype(jnp.float32))
        k_d = kf * (1.0 + (a - 1.0) * k_a.astype(jnp.float32))
        dirs.append((to_heads(decay), to_heads(k_d), to_heads(a)))
    return to_heads(r.astype(jnp.float32)), v, g, kk, dirs

def wkv_scan(r, decay, k, v, a_vec, b_vec, s0, reverse):
    def step(s, inp):
        r_t, w_t, k_t, v_t, a_t, b_t = inp
        sa = jnp.einsum('bhvk,bhk->bhv', s, a_t)
        s = s * w_t[:, :, None, :] + sa[..., None] * b_t[:, :, None, :] + v_t[..., None] * k_t[:, :, None, :]
        return s, jnp.einsum('bhvk,bhk->bhv', s, r_t)
    xs = tuple(jnp.swapaxes(t, 0, 1) for t in (r, decay, k, v, a_vec, b_vec))
    s_final, ys = lax.scan(step, s0, xs, reverse=reverse)
    return jnp.swapaxes(ys, 0, 1), s_final

def rwkv_output(y, r, v, g, k_dirs, r_k, lnx_w, lnx_b, wo, dtype):
    mu = jnp.mean(y, axis=-1, keepdims=True)
    var = jnp.mean(jnp.square(y - mu), axis=-1, keepdims=True)
    yn = (y - mu) * lax.rsqrt(var + LNX_EPS)
    bsz, t = y.shape[:2]
    yn = yn.reshape(bsz, t, D_MODEL) * lnx_w.astype(jnp.float32) + lnx_b.astype(jnp.float32)
    rk = r_k.astype(jnp.float32)
    bonus = sum(jnp.sum(r * k_d * rk, axis=-1, keepdims=True) for k_d in k_dirs) * v
    out = (yn + bonus.reshape(bsz, t, D_MODEL)).astype(dtype) * g
    return out @ wo

def ec_moe(h, router, wg, wu, wd):
    bsz, t, d = h.shape
    cap = CAPACITY_FACTOR * t // N_EXPERTS
    aff = jax.nn.softmax((h @ router).astype(jnp.float32), axis=-1)
    gates, idx = lax.top_k(jnp.swapaxes(aff, 1, 2), cap)
    xs = jax.vmap(lambda hb, ib: hb[ib])(h, idx)
    hid = jax.nn.silu(jnp.einsum('becd,edf->becf', xs, wg)) * jnp.einsum('becd,edf->becf', xs, wu)
    ys = jnp.einsum('becf,efd->becd', hid, wd) * gates[..., None].astype(h.dtype)
    return jax.vmap(lambda ib, yb: jnp.zeros((t, d), h.dtype).at[ib.reshape(-1)].add(yb.reshape(-1, d)))(idx, ys)

def first_inputs(seed: int = 0) -> dict:
    key = jax.random.key(seed)
    ks = iter(jax.random.split(key, 40))

    def nrm(shape, scale):
        return jax.random.normal(next(ks), shape, jnp.float32) * scale

    D = D_MODEL
    inv = D ** -0.5
    NR = N_RWKV_LAYERS
    NV = N_VRES_LAYERS
    return {
        'x': nrm((BATCH, SEQ, D), 1.0),
        'c': nrm((BATCH, D), 1.0),
        'ctx': nrm((BATCH, CTX_LEN, D), 1.0),
        'c_ctx': nrm((D,), 1.0),
        'ada_w': nrm((DEPTH, D, 6 * D), 0.5 * inv),
        'ada_b': nrm((DEPTH, 6 * D), 0.01),
        'norm_g': 1.0 + nrm((DEPTH, 2, D), 0.1),
        'fnet_wo': nrm((N_FNET_LAYERS, D, D), inv),
        'fnet_bo': nrm((N_FNET_LAYERS, D), 0.01),
        'rw_mix': jax.random.uniform(next(ks), (NR, 6, D), jnp.float32),
        'rw_wr': nrm((NR, D, D), inv),
        'rw_wk': nrm((NR, D, D), inv),
        'rw_wv': nrm((NR, D, D), inv),
        'rw_wo': nrm((NR, D, D), inv),
        'rw_w0': jax.random.uniform(next(ks), (NR, N_DIRS, D), jnp.float32, -6.0, 1.0),
        'rw_w1': nrm((NR, N_DIRS, D, D_DECAY_LORA), inv),
        'rw_w2': nrm((NR, N_DIRS, D_DECAY_LORA, D), 0.1),
        'rw_a0': nrm((NR, N_DIRS, D), 0.5),
        'rw_a1': nrm((NR, N_DIRS, D, D_AAA_LORA), inv),
        'rw_a2': nrm((NR, N_DIRS, D_AAA_LORA, D), 0.1),
        'rw_v0': nrm((NV, D), 0.5),
        'rw_v1': nrm((NV, D, D_MV_LORA), inv),
        'rw_v2': nrm((NV, D_MV_LORA, D), 0.1),
        'rw_g1': nrm((NR, D, D_GATE_LORA), inv),
        'rw_g2': nrm((NR, D_GATE_LORA, D), D_GATE_LORA ** -0.5),
        'rw_kk': 0.85 + nrm((NR, D), 0.1),
        'rw_ka': 1.0 + nrm((NR, D), 0.1),
        'rw_rk': nrm((NR, N_HEADS, HEAD_SIZE), 0.1),
        'rw_lnx_w': 1.0 + nrm((NR, D), 0.1),
        'rw_lnx_b': nrm((NR, D), 0.01),
        'moe_router': nrm((DEPTH, D, N_EXPERTS), inv),
        'moe_wg': nrm((DEPTH, N_EXPERTS, D, D_EXPERT), inv),
        'moe_wu': nrm((DEPTH, N_EXPERTS, D, D_EXPERT), inv),
        'moe_wd': nrm((DEPTH, N_EXPERTS, D_EXPERT, D), D_EXPERT ** -0.5),
        'final_g': 1.0 + nrm((D,), 0.1),
    }

def first_block(x, c, ctx, c_ctx, ada_w, ada_b, norm_g, fnet_wo, fnet_bo, rw_mix, rw_wr, rw_wk, rw_wv, rw_wo,
              rw_w0, rw_w1, rw_w2, rw_a0, rw_a1, rw_a2, rw_v0, rw_v1, rw_v2, rw_g1, rw_g2, rw_kk, rw_ka, rw_rk,
              rw_lnx_w, rw_lnx_b, moe_router, moe_wg, moe_wu, moe_wd, final_g):
    dtype = x.dtype
    v_first_x = None
    v_first_c = None
    for i in range(DEPTH):
        need_ctx = i < DEPTH - 1
        sh1x, sc1x, g1x, sh2x, sc2x, g2x = [m[:, None, :] for m in adaln_params(c, ada_w[i], ada_b[i])]
        sh1c, sc1c, g1c, sh2c, sc2c, g2c = adaln_params(c_ctx, ada_w[i], ada_b[i])
        hx = rmsnorm(x, norm_g[i, 0]) * (1.0 + sc1x) + sh1x
        if i % N_MIXERS == 0:
            fi = i // N_MIXERS
            x = x + g1x * fourier_mix(hx, fnet_wo[fi], fnet_bo[fi])
            if need_ctx:
                hc = rmsnorm(ctx, norm_g[i, 0]) * (1.0 + sc1c) + sh1c
                ctx = ctx + g1c * fourier_mix(hc, fnet_wo[fi], fnet_bo[fi])
        else:
            ri = i // N_MIXERS
            hc = rmsnorm(ctx, norm_g[i, 0]) * (1.0 + sc1c) + sh1c
            vres = None if ri == 0 else (rw_v0[ri - 1], rw_v1[ri - 1], rw_v2[ri - 1])
            prm = (rw_mix[ri], rw_wr[ri], rw_wk[ri], rw_wv[ri], rw_w0[ri], rw_w1[ri], rw_w2[ri],
                   rw_a0[ri], rw_a1[ri], rw_a2[ri], rw_g1[ri], rw_g2[ri], rw_kk[ri], rw_ka[ri])
            r_x, v_x, gt_x, kk_x, dirs_x = rwkv_project(hx, qshift_grid(hx), *prm, v_first_x, vres)
            r_c, v_c, gt_c, kk_c, dirs_c = rwkv_project(hc, shift_seq(hc), *prm, v_first_c, vres)
            if ri == 0:
                v_first_x, v_first_c = v_x, v_c
            vh_x = to_heads(v_x.astype(jnp.float32))
            vh_c = to_heads(v_c.astype(jnp.float32))
            s0 = jnp.zeros((x.shape[0], N_HEADS, HEAD_SIZE, HEAD_SIZE), jnp.float32)
            ys_x = []
            ys_c = []
            for d in range(N_DIRS):
                reverse = d == 1
                dec_c, k_c, a_c = dirs_c[d]
                yc_d, s_ctx = wkv_scan(r_c, dec_c, k_c, vh_c, -kk_c, kk_c * a_c, s0, reverse)
                dec_x, k_x, a_x = dirs_x[d]
                yx_d, _ = wkv_scan(r_x, dec_x, k_x, vh_x, -kk_x, kk_x * a_x, s_ctx, reverse)
                ys_x.append(yx_d)
                ys_c.append(yc_d)
            x = x + g1x * rwkv_output(ys_x[0] + ys_x[1], r_x, vh_x, gt_x, [dd[1] for dd in dirs_x],
                                      rw_rk[ri], rw_lnx_w[ri], rw_lnx_b[ri], rw_wo[ri], dtype)
            if need_ctx:
                ctx = ctx + g1c * rwkv_output(ys_c[0] + ys_c[1], r_c, vh_c, gt_c, [dd[1] for dd in dirs_c],
                                              rw_rk[ri], rw_lnx_w[ri], rw_lnx_b[ri], rw_wo[ri], dtype)
        hx = rmsnorm(x, norm_g[i, 1]) * (1.0 + sc2x) + sh2x
        x = x + g2x * ec_moe(hx, moe_router[i], moe_wg[i], moe_wu[i], moe_wd[i])
        if need_ctx:
            hc = rmsnorm(ctx, norm_g[i, 1]) * (1.0 + sc2c) + sh2c
            ctx = ctx + g2c * ec_moe(hc, moe_router[i], moe_wg[i], moe_wu[i], moe_wd[i])
    return rmsnorm(x, final_g)


CHUNK = 128
D_MIX = D_MODEL
GMLP_HEADS = 4
GMLP_HEAD_DIM = 64
GMLP_W = GMLP_HEADS * GMLP_HEAD_DIM
SSD_HEADS = 6
SSD_HEAD_DIM = 64
SSD_W = SSD_HEADS * SSD_HEAD_DIM
SSD_GROUPS = 2
SSD_STATE = 64
SSD_CONV = 4
SSD_XBC = SSD_W + 2 * SSD_GROUPS * SSD_STATE
MLA_HEADS = 6
MLA_NOPE = 64
MLA_ROPE = 32
MLA_V = 64
MLA_W = MLA_HEADS * MLA_V
MLA_Q_RANK = 384
MLA_KV_RANK = 256
ROPE_BASE = 10000.0
D_FF = 4 * D_MODEL
EPS = 1e-6
IN_WIDTHS = (2 * GMLP_W, SSD_W, SSD_XBC, SSD_HEADS, MLA_Q_RANK, MLA_KV_RANK, MLA_ROPE)
D_IN = sum(IN_WIDTHS)


def rmsnorm_2(x, g):
    xf = x.astype(jnp.float32)
    var = jnp.mean(xf * xf, axis=-1, keepdims=True)
    return (xf * lax.rsqrt(var + EPS)).astype(x.dtype) * g

def split_cols(proj):
    idx, acc = [], 0
    for w in IN_WIDTHS[:-1]:
        acc += w
        idx.append(acc)
    return jnp.split(proj, idx, axis=-1)

def rope_tables(S):
    half = MLA_ROPE // 2
    pos = jnp.arange(S, dtype=jnp.float32)
    inv_freq = jnp.power(ROPE_BASE, -jnp.arange(half, dtype=jnp.float32) / half)
    ang = pos[:, None] * inv_freq[None, :]
    return jnp.cos(ang), jnp.sin(ang)

def apply_rope(x, cos, sin):
    c = cos[None, :, None, :].astype(x.dtype)
    s = sin[None, :, None, :].astype(x.dtype)
    x1, x2 = jnp.split(x, 2, axis=-1)
    return jnp.concatenate([x1 * c - x2 * s, x2 * c + x1 * s], axis=-1)

def gmlp_mixer(uv, v_norm_g, w_s, b_s):
    Bsz, S, _ = uv.shape
    nc = S // CHUNK
    uv = jax.nn.gelu(uv)
    u, v = jnp.split(uv, 2, axis=-1)
    v = rmsnorm_2(v, v_norm_g).reshape(Bsz, nc, CHUNK, GMLP_HEADS, GMLP_HEAD_DIM)
    causal = jnp.tril(jnp.ones((CHUNK, CHUNK), dtype=w_s.dtype))
    mixed = jnp.einsum('hts,bcshd->bcthd', w_s * causal, v)
    mixed = mixed + b_s.T[None, None, :, :, None]
    return u * mixed.reshape(Bsz, S, GMLP_W)

def causal_depthwise_conv(x, w, b):
    K, C = w.shape
    out = lax.conv_general_dilated(
        x, w[:, None, :], window_strides=(1,), padding=((K - 1, 0),),
        dimension_numbers=('NWC', 'WIO', 'NWC'), feature_group_count=C)
    return out + b

def ssd_mixer(z, xbc, dt_raw, conv_w, conv_b, dt_bias, a_log, d_skip, norm_g):
    Bsz, S, _ = xbc.shape
    nc = S // CHUNK
    hpg = SSD_HEADS // SSD_GROUPS
    xbc = jax.nn.silu(causal_depthwise_conv(xbc, conv_w, conv_b))
    xs, Bm, Cm = jnp.split(xbc, [SSD_W, SSD_W + SSD_GROUPS * SSD_STATE], axis=-1)
    xs_c = xs.reshape(Bsz, nc, CHUNK, SSD_HEADS, SSD_HEAD_DIM)
    B_c = Bm.reshape(Bsz, nc, CHUNK, SSD_GROUPS, SSD_STATE)
    C_c = Cm.reshape(Bsz, nc, CHUNK, SSD_GROUPS, SSD_STATE)
    dt = jax.nn.softplus((dt_raw + dt_bias).astype(jnp.float32))
    A = -jnp.exp(a_log.astype(jnp.float32))
    dt_h = dt.reshape(Bsz, nc, CHUNK, SSD_HEADS).transpose(0, 1, 3, 2)
    a_h = jnp.cumsum(dt_h * A[None, None, :, None], axis=-1)
    causal = jnp.tril(jnp.ones((CHUNK, CHUNK), dtype=bool))
    seg = a_h[..., :, None] - a_h[..., None, :]
    decay = jnp.exp(jnp.where(causal, seg, -jnp.inf))
    cb = jnp.einsum('bctgn,bcsgn->bcgts', C_c, B_c)
    cb_h = jnp.repeat(cb, hpg, axis=2)
    w = cb_h * decay * dt_h[:, :, :, None, :]
    y_diag = jnp.einsum('bchts,bcshp->bcthp', w, xs_c)
    B_h = jnp.repeat(B_c, hpg, axis=3)
    C_h = jnp.repeat(C_c, hpg, axis=3)
    decay_to_end = jnp.exp(a_h[..., -1:] - a_h) * dt_h
    states = jnp.einsum('bchs,bcshn,bcshp->bchpn', decay_to_end, B_h, xs_c)
    chunk_decay = jnp.exp(a_h[..., -1])

    def step(h, inp):
        dec, st = inp
        return dec[:, :, None, None] * h + st, h

    h0 = jnp.zeros((Bsz, SSD_HEADS, SSD_HEAD_DIM, SSD_STATE), states.dtype)
    _, h_prev = lax.scan(step, h0, (chunk_decay.transpose(1, 0, 2), states.transpose(1, 0, 2, 3, 4)))
    h_prev = h_prev.transpose(1, 0, 2, 3, 4)
    y_off = jnp.einsum('bcthn,bchpn,bcht->bcthp', C_h, h_prev, jnp.exp(a_h))
    y = y_diag + y_off + xs_c * d_skip[:, None]
    y = y.reshape(Bsz, S, SSD_W).astype(z.dtype)
    yg = (y * jax.nn.silu(z)).reshape(Bsz, S, SSD_GROUPS, SSD_W // SSD_GROUPS)
    return rmsnorm_2(yg, norm_g.reshape(SSD_GROUPS, -1)).reshape(Bsz, S, SSD_W)

def causal_block_attention(q, k, v, scale):
    Bsz, S, H, Dqk = q.shape
    nq = S // CHUNK
    qb = q.reshape(Bsz, nq, CHUNK, H, Dqk).transpose(1, 0, 3, 2, 4)
    k_pos = jnp.arange(S)

    def one_block(args):
        q_blk, blk = args
        s = jnp.einsum('bhqd,bkhd->bhqk', q_blk, k).astype(jnp.float32) * scale
        q_pos = blk * CHUNK + jnp.arange(CHUNK)
        s = jnp.where(k_pos[None, :] <= q_pos[:, None], s, -jnp.inf)
        p = jax.nn.softmax(s, axis=-1).astype(v.dtype)
        return jnp.einsum('bhqk,bkhd->bqhd', p, v)

    out = lax.map(one_block, (qb, jnp.arange(nq)))
    return out.transpose(1, 0, 2, 3, 4).reshape(Bsz, S, H, v.shape[-1])

def mla_mixer(c_q, c_kv, k_rope_raw, q_norm_g, w_qb, kv_norm_g, w_kvb, cos, sin):
    Bsz, S, _ = c_q.shape
    q = (rmsnorm_2(c_q, q_norm_g) @ w_qb).reshape(Bsz, S, MLA_HEADS, MLA_NOPE + MLA_ROPE)
    kv = (rmsnorm_2(c_kv, kv_norm_g) @ w_kvb).reshape(Bsz, S, MLA_HEADS, MLA_NOPE + MLA_V)
    q_nope, q_rope = jnp.split(q, [MLA_NOPE], axis=-1)
    k_nope, v = jnp.split(kv, [MLA_NOPE], axis=-1)
    q_rope = apply_rope(q_rope, cos, sin)
    k_rope = apply_rope(k_rope_raw[:, :, None, :], cos, sin)
    q = jnp.concatenate([q_nope, q_rope], axis=-1)
    k = jnp.concatenate([k_nope, jnp.broadcast_to(k_rope, (Bsz, S, MLA_HEADS, MLA_ROPE))], axis=-1)
    scale = 1.0 / math.sqrt(MLA_NOPE + MLA_ROPE)
    out = causal_block_attention(q, k, v, scale)
    return out.reshape(Bsz, S, MLA_W)

def squared_relu_mlp(h, w1, w2):
    return jnp.square(jax.nn.relu(h @ w1)) @ w2

def second_inputs(seed: int = 0) -> dict:
    key = jax.random.key(seed)
    ks = jax.random.split(key, 21)

    def nrm(k, shape, scale):
        return jax.random.normal(k, shape, jnp.float32) * scale

    def gain(k, shape):
        return 1.0 + 0.02 * jax.random.normal(k, shape, jnp.float32)

    dt0 = jnp.exp(jax.random.uniform(ks[8], (DEPTH, SSD_HEADS), jnp.float32,
                                     math.log(1e-3), math.log(1e-1)))
    dt_bias = dt0 + jnp.log(-jnp.expm1(-dt0))
    a_log = jnp.log(jax.random.uniform(ks[9], (DEPTH, SSD_HEADS), jnp.float32, 1.0, 16.0))
    return {
        "x": nrm(ks[0], (BATCH, SEQ, D_MODEL), 1.0),
        "norm_mix_g": gain(ks[1], (DEPTH, D_MODEL)),
        "w_in": nrm(ks[2], (DEPTH, D_MODEL, D_IN), D_MODEL ** -0.5),
        "gmlp_v_norm_g": gain(ks[3], (DEPTH, GMLP_W)),
        "gmlp_w_s": nrm(ks[4], (DEPTH, GMLP_HEADS, CHUNK, CHUNK), CHUNK ** -0.5),
        "gmlp_b_s": gain(ks[5], (DEPTH, GMLP_HEADS, CHUNK)),
        "ssd_conv_w": nrm(ks[6], (DEPTH, SSD_CONV, SSD_XBC), SSD_CONV ** -0.5),
        "ssd_conv_b": nrm(ks[7], (DEPTH, SSD_XBC), 0.02),
        "ssd_dt_bias": dt_bias,
        "ssd_a_log": a_log,
        "ssd_d": 1.0 + 0.1 * jax.random.normal(ks[10], (DEPTH, SSD_HEADS), jnp.float32),
        "ssd_norm_g": gain(ks[11], (DEPTH, SSD_W)),
        "mla_q_norm_g": gain(ks[12], (DEPTH, MLA_Q_RANK)),
        "mla_w_qb": nrm(ks[13], (DEPTH, MLA_Q_RANK, MLA_HEADS * (MLA_NOPE + MLA_ROPE)), MLA_Q_RANK ** -0.5),
        "mla_kv_norm_g": gain(ks[14], (DEPTH, MLA_KV_RANK)),
        "mla_w_kvb": nrm(ks[15], (DEPTH, MLA_KV_RANK, MLA_HEADS * (MLA_NOPE + MLA_V)), MLA_KV_RANK ** -0.5),
        "w_out": nrm(ks[16], (DEPTH, D_MIX, D_MODEL), D_MIX ** -0.5),
        "norm_mlp_g": gain(ks[17], (DEPTH, D_MODEL)),
        "mlp_w1": nrm(ks[18], (DEPTH, D_MODEL, D_FF), D_MODEL ** -0.5),
        "mlp_w2": nrm(ks[19], (DEPTH, D_FF, D_MODEL), D_FF ** -0.5),
        "final_norm_g": gain(ks[20], (D_MODEL,)),
    }

def second_block(x, norm_mix_g, w_in, gmlp_v_norm_g, gmlp_w_s, gmlp_b_s, ssd_conv_w, ssd_conv_b,
              ssd_dt_bias, ssd_a_log, ssd_d, ssd_norm_g, mla_q_norm_g, mla_w_qb, mla_kv_norm_g,
              mla_w_kvb, w_out, norm_mlp_g, mlp_w1, mlp_w2, final_norm_g):
    S = x.shape[1]
    cos, sin = rope_tables(S)
    for l in range(DEPTH):
        h = rmsnorm_2(x, norm_mix_g[l])
        uv, z, xbc, dt_raw, c_q, c_kv, k_rope = split_cols(h @ w_in[l])
        y_a = gmlp_mixer(uv, gmlp_v_norm_g[l], gmlp_w_s[l], gmlp_b_s[l])
        y_b = ssd_mixer(z, xbc, dt_raw, ssd_conv_w[l], ssd_conv_b[l], ssd_dt_bias[l],
                        ssd_a_log[l], ssd_d[l], ssd_norm_g[l])
        y_c = mla_mixer(c_q, c_kv, k_rope, mla_q_norm_g[l], mla_w_qb[l], mla_kv_norm_g[l],
                        mla_w_kvb[l], cos, sin)
        mix = jnp.concatenate([y_a, y_b, y_c], axis=-1)
        x = x + mix @ w_out[l]
        x = x + squared_relu_mlp(rmsnorm_2(x, norm_mlp_g[l]), mlp_w1[l], mlp_w2[l])
    return rmsnorm_2(x, final_norm_g)


def setup_inputs(seed=0):
    out = dict(first_inputs(seed))
    for name, value in second_inputs(seed + 1).items():
        if name != "x":
            out[name + "_2"] = value
    return out


def reference(
    x, c, ctx, c_ctx, ada_w, ada_b, norm_g, fnet_wo, fnet_bo, rw_mix, rw_wr, rw_wk, rw_wv,
    rw_wo, rw_w0, rw_w1, rw_w2, rw_a0, rw_a1, rw_a2, rw_v0, rw_v1, rw_v2, rw_g1, rw_g2, rw_kk,
    rw_ka, rw_rk, rw_lnx_w, rw_lnx_b, moe_router, moe_wg, moe_wu, moe_wd, final_g, norm_mix_g_2,
    w_in_2, gmlp_v_norm_g_2, gmlp_w_s_2, gmlp_b_s_2, ssd_conv_w_2, ssd_conv_b_2, ssd_dt_bias_2,
    ssd_a_log_2, ssd_d_2, ssd_norm_g_2, mla_q_norm_g_2, mla_w_qb_2, mla_kv_norm_g_2,
    mla_w_kvb_2, w_out_2, norm_mlp_g_2, mlp_w1_2, mlp_w2_2, final_norm_g_2,
):
    x = first_block(
        x, c, ctx, c_ctx, ada_w, ada_b, norm_g, fnet_wo, fnet_bo, rw_mix, rw_wr, rw_wk, rw_wv,
        rw_wo, rw_w0, rw_w1, rw_w2, rw_a0, rw_a1, rw_a2, rw_v0, rw_v1, rw_v2, rw_g1, rw_g2,
        rw_kk, rw_ka, rw_rk, rw_lnx_w, rw_lnx_b, moe_router, moe_wg, moe_wu, moe_wd, final_g,
    )
    return second_block(
        x, norm_mix_g_2, w_in_2, gmlp_v_norm_g_2, gmlp_w_s_2, gmlp_b_s_2, ssd_conv_w_2,
        ssd_conv_b_2, ssd_dt_bias_2, ssd_a_log_2, ssd_d_2, ssd_norm_g_2, mla_q_norm_g_2,
        mla_w_qb_2, mla_kv_norm_g_2, mla_w_kvb_2, w_out_2, norm_mlp_g_2, mlp_w1_2, mlp_w2_2,
        final_norm_g_2,
    )


_drawn_inputs = setup_inputs


def setup_inputs(seed=0):
    import zlib

    import numpy as np

    out = dict(_drawn_inputs(seed))
    spreads = {}
    factors = {'ada_b': 3.055,
     'fnet_bo': 8.0,
     'rw_w1': 3.51,
     'rw_w2': 3.481,
     'rw_lnx_b': 8.0,
     'gmlp_v_norm_g_2': 8.0,
     'gmlp_b_s_2': 8.0,
     'ssd_conv_b_2': 2.832,
     'ssd_norm_g_2': 4.084,
     'mla_q_norm_g_2': 8.0,
     'mla_kv_norm_g_2': 8.0,
     'final_norm_g_2': 2.816}
    for name, (base, spread) in spreads.items():
        noise = np.random.default_rng([zlib.crc32(name.encode()), seed]).standard_normal(out[name].shape)
        drawn = base * np.exp(spread * noise) if base else spread * noise
        out[name] = __import__('jax').numpy.asarray(drawn.astype(out[name].dtype))
    for name, factor in factors.items():
        out[name] = (out[name] * factor).astype(out[name].dtype)
    return out
```

```python
import math
from contextlib import ExitStack

import numpy as np

import concourse.bass as bass
from concourse import mybir

F32 = mybir.dt.float32
ALU = mybir.AluOpType
ACT = mybir.ActivationFunctionType
AX = mybir.AxisListType.X

P = 128
D = 1024
KT = D // P
TX, TC = 512, 256
TA = TX + TC
SEGS = ((0, TX), (TX, TC))
XSEG = ((0, TX),)
NE = 16
CAPX, CAPC = 2 * TX // NE, 2 * TC // NE
SLOT = 2048
NSLOT = 8
CH = 64
NCHX, NCHC = TX // CH, TC // CH
NCH = NCHX + NCHC
LEVELS = 6
STREAMS = ("kk", "kka0", "kka1", "kd0", "kd1", "lw0", "lw1", "v", "r", "g")
VEC_PARTS = {}
STOP = None


def vec_layout():
    off, at = 0, {}
    for name, n in (
        ("norm_g", 32), ("fnet_bo", 8), ("mix", 48), ("w0", 16), ("a0", 16), ("kk", 8), ("ka", 8), ("rk", 8),
        ("lnw", 8), ("lnb", 8), ("final_g", 8), ("nmix", 16), ("nmlp", 16), ("fin2", 8), ("ada_b", 96),
        ("convw", 40), ("convb", 10), ("ssdg", 6), ("qg", 6), ("kvg", 4), ("ssdd", 6), ("c", 16), ("iop", 2), ("selc", 2),
    ):
        at[name] = off
        off += n
    return at, off


VEC, NVEC = vec_layout()


def weight_plan(a):
    plan = []

    def cols(name, src, width=256):
        n = src.shape[1]
        for i, c in enumerate(range(0, n, width)):
            plan.append((f"{name}.{i}", src[:, c:min(n, c + width)]))

    def ada(i):
        cols(f"ada{i}", a["ada_w"][i])

    def moe(i):
        plan.append((f"router{i}", a["moe_router"][i]))
        for e in range(NE) if i == 1 else ():
            for nm in ("g", "u", "d"):
                for r in range(2):
                    for n in range(2):
                        plan.append((f"w{nm}{i}.{e}.{r}.{n}",
                                     a[f"moe_w{nm}"][i, e, 512 * r:512 * r + 512, 512 * n:512 * n + 512]))
        for e in range(NE) if i == 0 else ():
            for b in range(4):
                plan.append((f"wg{i}.{e}.{b}", a["moe_wg"][i, e, :, 256 * b:256 * b + 256]))
                plan.append((f"wu{i}.{e}.{b}", a["moe_wu"][i, e, :, 256 * b:256 * b + 256]))
            for n in range(2):
                for r in range(2):
                    plan.append((f"wd{i}.{e}.{n}.{r}",
                                 a["moe_wd"][i, e, 512 * r:512 * r + 512, 512 * n:512 * n + 512]))

    ada(0)
    plan.append(("dftC", a["dftC"]))
    plan.append(("dftTc", a["dftTc"]))
    plan.append(("dftT.0", a["dftT"][:, 0:TX]))
    plan.append(("dftT.1", a["dftT"][:, TX:2 * TX]))
    cols("fwo", a["fnet_wo"][0])
    moe(0)
    ada(1)
    plan.append(("w1", a["w1cat"]))
    plan.append(("w2", a["w2cat"]))
    plan.append(("a1", a["a1cat"]))
    plan.append(("a2", a["a2cat"]))
    cols("wk", a["rw_wk"][0])
    cols("wv", a["rw_wv"][0])
    cols("wr", a["rw_wr"][0])
    plan.append(("g1", a["rw_g1"][0]))
    plan.append(("g2", a["rw_g2"][0]))
    for n in range(5):
        plan.append((f"hold.{n}", None))
    cols("wo", a["rw_wo"][0])
    moe(1)
    for l in range(2):
        w = a["w_in_2"][l]
        cols(f"i{l}.cq", w[:, 1542:1926])
        plan.append((f"i{l}.ckv", w[:, 1926:2182]))
        plan.append((f"i{l}.kr", a["krcat"][l]))
        plan.append((f"i{l}.qb", a["mla_w_qb_2"][l]))
        plan.append((f"i{l}.qs", a["qbsw"][l]))
        plan.append((f"i{l}.kvb", a["mla_w_kvb_2"][l]))
        plan.append((f"i{l}.v", w[:, 256:512]))
        plan.append((f"i{l}.u", w[:, 0:256]))
        plan.append((f"i{l}.dt", w[:, 1536:1542]))
        cols(f"i{l}.xbc", w[:, 896:1536])
        cols(f"i{l}.z", w[:, 512:896])
        cols(f"i{l}.wout", a["w_out_2"][l])
        cols(f"i{l}.m1", a["mlp_w1_2"][l])
        for n in range(2):
            for r in range(8):
                plan.append((f"i{l}.m2.{n}.{r}",
                             a["mlp_w2_2"][l, 512 * r:512 * r + 512, 512 * n:512 * n + 512]))
    return plan


def build(nc, a, out, table):
    marks = {}
    ctx = ExitStack()
    with ctx:
        def sb(name, shape):
            return ctx.enter_context(nc.sbuf_tensor(name, shape, F32))

        def semaphore(name):
            return ctx.enter_context(nc.semaphore(name))

        X = sb("X", [P, KT, TA])
        H = sb("H", [P, KT, TA])
        ring = sb("ring", [P, NSLOT, SLOT])
        vec = sb("vec", [P, NVEC])
        ident = sb("ident", [P, P])
        ones = sb("ones", [P, P])
        bones = sb("bones", [P, P])
        id64 = sb("id64", [P, 64])
        iota = sb("iota", [P, 64])
        eps = sb("eps", [P, 4])
        ada = sb("ada", [P, 48, 2])
        gsc = sb("gsc", [P, 2, KT, 2])
        csil = sb("csil", [P, KT, 32])
        small = sb("small", [P, 256])
        SCRW = 22900
        scr = sb("scr", [P, SCRW])
        ps = ctx.enter_context(nc.psum_tensor("ps", [P, 8, 512], F32))
        dram = {s: nc.dram_tensor(f"st_{s}", (NCH, P, KT, CH), F32).ap() for s in STREAMS}

        def S(off, *dims):
            n = int(np.prod(dims))
            assert off + n <= SCRW, (off, dims)
            t = scr[:, off:off + n]
            if len(dims) == 2:
                return t.rearrange("p (a b) -> p a b", b=dims[1])
            if len(dims) == 3:
                return t.rearrange("p (a b c) -> p a b c", b=dims[1], c=dims[2])
            if len(dims) == 4:
                return t.rearrange("p (a b c d) -> p a b c d", b=dims[1], c=dims[2], d=dims[3])
            return t

        sems = {
            "T": semaphore("tensor_done"), "V": semaphore("vector_done"),
            "A": semaphore("scalar_done"), "G": semaphore("pool_done"),
            "const": semaphore("constants_loaded"), "out": semaphore("output_stored"),
        }
        for i in range(NSLOT):
            sems[f"slot{i}"] = semaphore(f"weight_slot_{i}_loaded")
        for i in range(10):
            sems[f"st{i}"] = semaphore(f"stage_tile_{i}_stored")
        for i in range(2):
            sems[f"ld{i}"] = semaphore(f"chunk_buffer_{i}_loaded")
        sems["aux"] = semaphore("stage_constants_loaded")
        tensor_done, vector_done, scalar_done, pool_done = (sems[e] for e in "TVAG")
        inputs_in, constants_in, output_out = sems["const"], sems["aux"], sems["out"]
        count = dict.fromkeys(sems, 0)
        waited = {}

        def did(e, ins, name=None, by=1):
            count[e] += by
            if name is not None:
                assert name not in marks, name
                marks[name] = (e, count[e])

        def at(step):
            e, v = table.get(step, ("T", 1)) if not table else table[step]
            return sems[e], v

        def later(eng, step):
            e, v = table.get(step, ("T", 1)) if not table else table[step]
            fresh = waited.get((eng.engine, e), 0) < v
            if fresh:
                waited[eng.engine, e] = v
            return fresh

        def own(eng, e):
            waited[eng.engine, e] = count[e]
            return sems[e], count[e]

        def phase(eng, e, name):
            marks[f"ph.{name}.{e}"] = (e, count[e])
            for other in "TVAG":
                if other != e and table and table[f"ph.{name}.{other}"][1] > 0:
                    if later(eng, f"ph.{name}.{other}"):
                        eng.wait_ge(*at(f"ph.{name}.{other}"))

        owner = [None] * 8
        nbank = [0]

        def bank(pe, key):
            b = nbank[0] % 8
            nbank[0] += 1
            if owner[b] is not None:
                if later(pe, "free." + owner[b]):
                    pe.wait_ge(*at("free." + owner[b]))
            owner[b] = key
            marks["bank." + key] = ("bank", b)
            return ps[:, b, :]

        def tile(eng, key):
            if later(eng, key):
                eng.wait_ge(*at(key))
            return ps[:, table["bank." + key][1] if table else 0, :]

        plan = weight_plan(a)
        place = {name: (i % NSLOT, src.shape if src is not None else None) for i, (name, src) in enumerate(plan)}

        def weight(pe, name):
            if later(pe, "w." + name):
                pe.wait_ge(*at("w." + name))
            s, (rows, cols) = place[name]
            n = max(1, rows // P)
            return ring[0:min(P, rows), s, 0:n * cols].rearrange("p (k c) -> p k c", c=cols)

        block = ctx.enter_context(nc.Block())

        @block.sync
        def _(sp):
            def load(dst, src, name):
                did("const", sp.dma_start(dst, src).then_inc(inputs_in, 16), by=16)
            load(vec[:, :], a["vecs"], "c")
            load(ident[:, :], a["ident"], "c")
            load(bones[:, :], a["bones"], "c")
            load(id64[:, :], a["id64"], "c")
            load(iota[:, :], a["iota"], "c")
            load(X[:, :, 0:TX], a["xT"].rearrange("(k p) t -> p k t", p=P), "c")
            load(X[:, :, TX:TA], a["ctxT"].rearrange("(k p) t -> p k t", p=P), "c")
            marks["const"] = ("const", count["const"])
            for i, (name, src) in enumerate(plan):
                if STOP is not None and not table.get("wf." + name) and table:
                    break
                if src is None:
                    continue
                if i >= NSLOT:
                    if later(sp, "wf." + plan[i - NSLOT][0]):
                        sp.wait_ge(*at("wf." + plan[i - NSLOT][0]))
                rows, cols = src.shape
                n = max(1, rows // P)
                dst = ring[0:min(P, rows), i % NSLOT, 0:n * cols].rearrange("p (k c) -> p k c", c=cols)
                did(f"slot{i % NSLOT}", sp.dma_start(dst, src.rearrange("(k p) c -> p k c", p=min(P, rows))).then_inc(sems[f"slot{i % NSLOT}"], 16), "w." + name, by=16)
            if later(sp, "final"):
                sp.wait_ge(*at("final"))
            did("out", sp.dma_start(out.rearrange("(k p) t -> p k t", p=P), H[:, :, 0:TX]).then_inc(output_out, 16), by=16)
            sp.wait_ge(sems["out"], 16)

        V, A_, T_, G_ = "V", "A", "T", "G"

        def col(name, i):
            return vec[:, VEC[name] + i:VEC[name] + i + 1]

        def norm_scalar(act, tag, segs, n, shift):
            w = sum(s[1] for s in segs)
            rs = small_rs
            for k in range(KT):
                did(A_, act.activation(H[:, k, 0:w], X[:, k, 0:w], ACT.Square).then_inc(scalar_done, 1), f"{tag}.sq{k}")
            for s0, sn in segs:
                t = tile(act, f"{tag}.ss{s0}")
                did(A_, act.activation(rs[:, s0:s0 + sn], t[:, 0:sn], ACT.Sqrt, bias=eps[:, 0:1], scale=1.0 / D).then_inc(scalar_done, 1), f"free.{tag}.ss{s0}")
            if shift:
                for k in range(KT):
                    if later(act, f"{tag}.g{k}"):
                        act.wait_ge(*at(f"{tag}.g{k}"))
                    for i, (s0, sn) in enumerate(segs):
                        did(A_, act.activation(H[:, k, s0:s0 + sn], H[:, k, s0:s0 + sn], ACT.Identity,
                                               bias=ada[:, shift[0] + k, i:i + 1]).then_inc(scalar_done, 1))
                    marks[f"{tag}.h{k}"] = (A_, count[A_])

        def norm_tensor(pe, tag, segs):
            banks = [bank(pe, f"{tag}.ss{s0}") for s0, _ in segs]
            for k in range(KT):
                if later(pe, f"{tag}.sq{k}"):
                    pe.wait_ge(*at(f"{tag}.sq{k}"))
                for b, (s0, sn) in zip(banks, segs):
                    m = pe.matmul(b[:, 0:sn], ones[:, :], H[:, k, s0:s0 + sn], start=k == 0, stop=k == KT - 1)
                    if k == KT - 1:
                        did(T_, m.then_inc(tensor_done, 1), f"{tag}.ss{s0}")

        def norm_vector(dve, tag, segs, gain, shift):
            w = sum(s[1] for s in segs)
            rs = small_rs
            for step in [f"free.{tag}.ss{s0}" for s0, _ in segs]:
                if later(dve, step):
                    dve.wait_ge(*at(step))
            did(V, dve.reciprocal(rs[:, 0:w], rs[:, 0:w]).then_inc(vector_done, 1))
            dve.wait_ge(*own(dve, V))
            for k in range(KT):
                for i, (s0, sn) in enumerate(segs):
                    did(V, dve.scalar_tensor_tensor(H[:, k, s0:s0 + sn], X[:, k, s0:s0 + sn], gain(i, k),
                                                    rs[:, s0:s0 + sn], ALU.mult, ALU.mult).then_inc(vector_done, 1))
                marks[f"{tag}.{'g' if shift else 'h'}{k}"] = (V, count[V])

        small_rs = S(SCRW - TA, TA)

        AP_ = S(0, 2, 256)

        def ada_tensor(pe, i):
            def turn(blk):
                n = blk // 6
                if blk % 6 == 0:
                    ada_bank[0] = bank(pe, f"ada{i}.{n}")
                if later(pe, f"free.ad{i}.{blk}"):
                    pe.wait_ge(*at(f"free.ad{i}.{blk}"))
                for j in range(2):
                    m = 2 * (blk % 6) + j
                    ins = pe.matmul(ada_bank[0][:, 2 * m:2 * m + 2], AP_[:, blk % 2, j * P:j * P + P],
                                    vec[:, VEC["selc"]:VEC["selc"] + 2], start=True, stop=True)
                did(T_, ins.then_inc(tensor_done, 1), f"ada{i}.{n}" if blk % 6 == 5 else f"adt{i}.{blk}")
                if blk % 6 == 5:
                    marks[f"adt{i}.{blk}"] = (T_, count[T_])
            ada_bank = [None]
            if later(pe, "csil"):
                pe.wait_ge(*at("csil"))
            for blk in range(24):
                w = weight(pe, f"ada{i}.{blk}")
                b = bank(pe, f"ad{i}.{blk}")
                for half in range(2):
                    for c in range(4):
                        ins = pe.matmul(b[32 * c:32 * c + 32, 0:256], csil[:, 2 * c + half, :], w[:, 2 * c + half, :],
                                        start=half == 0, stop=half == 1)
                did(T_, ins.then_inc(tensor_done, 1), f"ad{i}.{blk}")
                marks[f"wf.ada{i}.{blk}"] = (T_, count[T_])
                if blk:
                    turn(blk - 1)
            turn(23)

        def ada_vector(dve, i):
            for blk in range(24):
                if blk >= 2:
                    if later(dve, f"adt{i}.{blk - 2}"):
                        dve.wait_ge(*at(f"adt{i}.{blk - 2}"))
                t = tile(dve, f"ad{i}.{blk}")
                did(V, dve.tensor_copy(AP_[:, blk % 2, :], t[:, 0:256]).then_inc(vector_done, 1), f"free.ad{i}.{blk}")
                if blk % 6 == 0 and blk:
                    part(dve, i, blk // 6 - 1)
            part(dve, i, 3)
            dve.wait_ge(*own(dve, V))
            for n in range(2):
                sc = ada[:, 24 * n + 8:24 * n + 16, :]
                g = vec[:, VEC["norm_g"] + 16 * i + 8 * n:VEC["norm_g"] + 16 * i + 8 * n + 8]
                did(V, dve.scalar_tensor_tensor(gsc[:, n, :, :], sc, 1.0,
                                                g.unsqueeze(2).to_broadcast([P, KT, 2]), ALU.add, ALU.mult).then_inc(vector_done, 1), f"gsc{i}.{n}")
            dve.wait_ge(*own(dve, V))

        def part(dve, i, n):
            t = tile(dve, f"ada{i}.{n}")
            o = VEC["ada_b"] + 48 * i + 12 * n
            did(V, dve.tensor_tensor(ada[:, 12 * n:12 * n + 12, :], t[:, 0:24].rearrange("p (m c) -> p m c", c=2),
                                     vec[:, o:o + 12].unsqueeze(2).to_broadcast([P, 12, 2]), ALU.add).then_inc(vector_done, 1), f"free.ada{i}.{n}")

        def linear_tensor(pe, tag, wname, rhs, segs, ready, mtiles=8, kt=KT, after=None):
            for m in range(mtiles):
                w = weight(pe, f"{wname}.{m // 2}")
                for s0, sn in segs:
                    b = bank(pe, f"{tag}.{m}.{s0}")
                    for k in range(kt):
                        if later(pe, ready(k)):
                            pe.wait_ge(*at(ready(k)))
                        ins = pe.matmul(b[:, 0:sn], w[:, k, (m % 2) * P:(m % 2) * P + P], rhs(k, s0, sn),
                                        start=k == 0, stop=k == kt - 1)
                    did(T_, ins.then_inc(tensor_done, 1), f"{tag}.{m}.{s0}")
                if m % 2 == 1 or m == mtiles - 1:
                    marks[f"wf.{wname}.{m // 2}"] = (T_, count[T_])

        def residual_vector(dve, tag, segs, gate=None):
            for m in range(KT):
                for i, (s0, sn) in enumerate(segs):
                    t = tile(dve, f"{tag}.{m}.{s0}")
                    x = X[:, m, s0:s0 + sn]
                    if gate is None:
                        ins = dve.tensor_tensor(x, t[:, 0:sn], x, ALU.add)
                    else:
                        ins = dve.scalar_tensor_tensor(x, t[:, 0:sn], ada[:, gate + m, i:i + 1], x, ALU.mult, ALU.add)
                    did(V, ins.then_inc(vector_done, 1), f"free.{tag}.{m}.{s0}")

        Z = S(0, 6, 4, 512)
        fb = small[:, 0:16].rearrange("p (k c) -> p k c", c=2)

        def fnet_tensor(pe):
            w = weight(pe, "dftC")
            for tt in range(6):
                for g in range(4):
                    b = bank(pe, f"f1.{tt}.{g}")
                    for k in range(2):
                        if later(pe, f"n0.h{2 * g + k}"):
                            pe.wait_ge(*at(f"n0.h{2 * g + k}"))
                        ins = pe.matmul(b, H[:, 2 * g + k, tt * P:tt * P + P], w[:, k, :], start=k == 0, stop=k == 1)
                    did(T_, ins.then_inc(tensor_done, 1), f"f1.{tt}.{g}")
            marks["wf.dftC"] = (T_, count[T_])
            for s0, sn, tts, ws in ((TX, TC, (4, 5), ("dftTc",)), (0, TX, (0, 1, 2, 3), ("dftT.0", "dftT.1"))):
                for d in range(KT):
                    b = bank(pe, f"f2.{d}.{s0}")
                    for cs in range(2):
                        w = weight(pe, ws[cs % len(ws)])
                        for n, tt in enumerate(tts):
                            if later(pe, f"free.f1.{tt}.{d // 2}"):
                                pe.wait_ge(*at(f"free.f1.{tt}.{d // 2}"))
                            rhs = w[:, n, cs * TC:cs * TC + TC] if len(ws) == 1 else w[:, n, :]
                            o = cs * 256 + (d % 2) * P
                            ins = pe.matmul(b[:, 0:sn], Z[:, tt, d // 2, o:o + P], rhs,
                                            start=cs == 0 and n == 0, stop=cs == 1 and n == len(tts) - 1)
                    did(T_, ins.then_inc(tensor_done, 1), f"f2.{d}.{s0}")
                for wn in ws:
                    marks["wf." + wn] = (T_, count[T_])
            linear_tensor(pe, "fo", "fwo", lambda k, s0, sn: H[:, k, s0:s0 + sn], SEGS, lambda k: f"free.f2.{k}.0")

        def fnet_scalar(act):
            for tt in range(6):
                for g in range(1, 4, 2):
                    t = tile(act, f"f1.{tt}.{g}")
                    did(A_, act.activation(Z[:, tt, g, :], t, ACT.Copy).then_inc(scalar_done, 1), f"free.f1.{tt}.{g}")

        def fnet_vector(dve):
            for tt in range(6):
                for g in range(0, 4, 2):
                    t = tile(dve, f"f1.{tt}.{g}")
                    did(V, dve.tensor_copy(Z[:, tt, g, :], t).then_inc(vector_done, 1), f"free.f1.{tt}.{g}")
            for s0, sn in (SEGS[1], SEGS[0]):
                for d in range(KT):
                    t = tile(dve, f"f2.{d}.{s0}")
                    did(V, dve.tensor_copy(H[:, d, s0:s0 + sn], t[:, 0:sn]).then_inc(vector_done, 1), f"free.f2.{d}.{s0}")
            bo = vec[:, VEC["fnet_bo"]:VEC["fnet_bo"] + 8].unsqueeze(2).to_broadcast([P, KT, 2])
            did(V, dve.tensor_tensor(fb, ada[:, 16:24, :], bo, ALU.mult).then_inc(vector_done, 1))
            dve.wait_ge(*own(dve, V))
            for k in range(KT):
                for i, (s0, sn) in enumerate(SEGS):
                    did(V, dve.tensor_scalar(X[:, k, s0:s0 + sn], X[:, k, s0:s0 + sn], fb[:, k, i:i + 1], None, ALU.add).then_inc(vector_done, 1))
            dve.wait_ge(*own(dve, V))
            residual_vector(dve, "fo", SEGS, 16)

        HT = S(0, 6, D)
        YSX = S(6144, 8, D)
        YSC = S(14336, 4, D)
        HID = S(18432, KT, 96)
        GM = S(19200, 6, 256)
        WORK = scr[0:NE, 19200:19200 + TA]
        AT = scr[0:NE, 20736:20736 + TA]
        AFF = S(21504, 6, NE)
        POST = S(21600, 6, NE)
        SIL = S(21696, 2, 96)
        MX = S(21888, 8)
        M8 = scr[0:NE, 21896:21904]
        POSM = scr[0:NE, SCRW - TA:SCRW]
        SMX = S(0, 8, TX)
        SMC = S(4096, 4, TC)
        AB = S(5120, 2, 512)
        sel = S(19200, 12, P)

        def XS(q):
            return H[:, :, :].rearrange("p k t -> p (k t)")[:, 3072 * q:3072 * q + 3072].rearrange(
                "p (k e c) -> p k e c", k=KT, c=96)

        def moe_segs(i):
            return SEGS if i == 0 else XSEG

        SIL1 = S(14336, 2, 512)
        HD1 = S(15360, 2, 512)
        HI1 = S(16384, 2, 512)

        def experts1_tensor(pe, gather):
            for e in range(NE):
                q = e // 4
                xs = XS(q % 2)
                for nm in ("g", "u"):
                    b = bank(pe, f"{nm}1.{e}")
                    for k in range(KT):
                        if later(pe, f"free.xs1.{q}.{k}"):
                            pe.wait_ge(*at(f"free.xs1.{q}.{k}"))
                        for n in range(2):
                            w = weight(pe, f"w{nm}1.{e}.{k // 4}.{n}")
                            ins = pe.matmul(b[64 * n:64 * n + 64, :], xs[:, k, e % 4, 0:64], w[:, k % 4, :],
                                            start=k == 0, stop=k == KT - 1)
                        if k == 3:
                            did(T_, ins.then_inc(tensor_done, 1))
                            for n in range(2):
                                marks[f"wf.w{nm}1.{e}.0.{n}"] = (T_, count[T_])
                    did(T_, ins.then_inc(tensor_done, 1), f"{nm}1.{e}")
                    for n in range(2):
                        marks[f"wf.w{nm}1.{e}.1.{n}"] = (T_, count[T_])
                if e % 4 == 0 and q < 3:
                    gather(q + 1)
                b = bank(pe, f"hx.{e}")
                if later(pe, f"hd.{e}"):
                    pe.wait_ge(*at(f"hd.{e}"))
                for f in range(4):
                    ins = pe.transpose(b[:, f * P:f * P + P], HD1[:, e % 2, f * P:f * P + P], ident[:, :])
                did(T_, ins.then_inc(tensor_done, 1), f"hx.{e}")
                b = bank(pe, f"y1.{e}")
                if later(pe, f"free.hx.{e}"):
                    pe.wait_ge(*at(f"free.hx.{e}"))
                for f in range(KT):
                    for n in range(2):
                        w = weight(pe, f"wd1.{e}.{f // 4}.{n}")
                        o = (f % 4) * P + 64 * (f // 4)
                        ins = pe.matmul(b[64 * n:64 * n + 64, :], HI1[:, e % 2, o:o + 64], w[:, f % 4, :],
                                        start=f == 0, stop=f == KT - 1)
                    if f == 3:
                        did(T_, ins.then_inc(tensor_done, 1))
                        for n in range(2):
                            marks[f"wf.wd1.{e}.0.{n}"] = (T_, count[T_])
                did(T_, ins.then_inc(tensor_done, 1), f"y1.{e}")
                for n in range(2):
                    marks[f"wf.wd1.{e}.1.{n}"] = (T_, count[T_])

        def experts1_scalar(act):
            for e in range(NE):
                t = tile(act, f"g1.{e}")
                if e >= 2:
                    if later(act, f"hd.{e - 2}"):
                        act.wait_ge(*at(f"hd.{e - 2}"))
                did(A_, act.activation(SIL1[:, e % 2, :], t, ACT.Silu).then_inc(scalar_done, 1), f"free.g1.{e}")
                t = tile(act, f"hx.{e}")
                if e >= 2:
                    if later(act, f"y1.{e - 2}"):
                        act.wait_ge(*at(f"y1.{e - 2}"))
                did(A_, act.activation(HI1[:, e % 2, :], t, ACT.Copy).then_inc(scalar_done, 1), f"free.hx.{e}")
                t = tile(act, f"y1.{e}")
                for n in range(2):
                    o = 64 * (e % 2)
                    did(A_, act.activation(YSX[o:o + 64, e // 2, 512 * n:512 * n + 512], t[64 * n:64 * n + 64, :], ACT.Copy).then_inc(scalar_done, 1))
                marks[f"free.y1.{e}"] = (A_, count[A_])
            marks[f"free.y1.{NE - 1}.1"] = (A_, count[A_])

        def experts1_vector(dve, onehot, take):
            for e in range(NE):
                if e % 4 == 0 and e < 12:
                    onehot(e // 4 + 1)
                t = tile(dve, f"u1.{e}")
                if later(dve, f"free.g1.{e}"):
                    dve.wait_ge(*at(f"free.g1.{e}"))
                if e >= 2:
                    if later(dve, f"hx.{e - 2}"):
                        dve.wait_ge(*at(f"hx.{e - 2}"))
                did(V, dve.tensor_tensor(HD1[:, e % 2, :], t, SIL1[:, e % 2, :], ALU.mult).then_inc(vector_done, 1), f"hd.{e}")
                marks[f"free.u1.{e}"] = (V, count[V])
                if e % 4 == 0 and e < 12:
                    take(e // 4 + 1)

        def moe_tensor(pe, i):
            segs = moe_segs(i)
            ntt = 6 if i == 0 else 4
            mx = 96 if i == 0 else 64
            w = weight(pe, f"router{i}")
            b = bank(pe, f"rt{i}")
            for tt in range(ntt):
                for k in range(KT):
                    if later(pe, f"m{i}.h{k}"):
                        pe.wait_ge(*at(f"m{i}.h{k}"))
                    ins = pe.matmul(b[:, tt * NE:tt * NE + NE], H[:, k, tt * P:tt * P + P], w[:, k, :],
                                    start=k == 0, stop=k == KT - 1)
            did(T_, ins.then_inc(tensor_done, 1), f"rt{i}")
            marks[f"wf.router{i}"] = (T_, count[T_])
            for tt in range(ntt):
                for half in range(2):
                    b = bank(pe, f"ht{i}.{tt}.{half}")
                    for k in range(4):
                        ins = pe.transpose(b[:, k * P:k * P + P], H[:, 4 * half + k, tt * P:tt * P + P], ident[:, :])
                    did(T_, ins.then_inc(tensor_done, 1), f"ht{i}.{tt}.{half}")
            if later(pe, f"aff{i}"):
                pe.wait_ge(*at(f"aff{i}"))
            for n, (s0, sn) in enumerate(segs):
                b = bank(pe, f"at{i}.{s0}")
                for tt in range(sn // P):
                    ins = pe.transpose(b[0:NE, tt * P:tt * P + P], AFF[:, s0 // P + tt, :], ident[:, :])
                did(T_, ins.then_inc(tensor_done, 1), f"at{i}.{s0}")
            if later(pe, f"posm{i}"):
                pe.wait_ge(*at(f"posm{i}"))
            b = bank(pe, f"pt{i}")
            for tt in range(ntt):
                ins = pe.transpose(b[:, tt * NE:tt * NE + NE], POSM[:, tt * P:tt * P + P], ident[0:NE, 0:NE])
            did(T_, ins.then_inc(tensor_done, 1), f"pt{i}")

            def gather(q):
                if later(pe, f"gm{i}.{q}"):
                    pe.wait_ge(*at(f"gm{i}.{q}"))
                for step in [f"free.ht{i}.{tt}.{hf}" for tt in range(ntt) for hf in range(2)]:
                    if later(pe, step):
                        pe.wait_ge(*at(step))
                for k in range(KT):
                    b = bank(pe, f"xs{i}.{q}.{k}")
                    for tt in range(4):
                        ins = pe.matmul(b[:, 0:256], HT[:, tt, k * P:k * P + P], GM[:, tt, :], start=tt == 0, stop=tt == 3)
                    if i == 0:
                        for tt in (4, 5):
                            ins = pe.matmul(b[:, 256:384], HT[:, tt, k * P:k * P + P], GM[:, tt, 0:128],
                                            start=tt == 4, stop=tt == 5)
                    did(T_, ins.then_inc(tensor_done, 1), f"xs{i}.{q}.{k}")

            gather(0)
            if i == 1:
                experts1_tensor(pe, gather)
            for e in range(NE) if i == 0 else ():
                q = e // 4
                xs = XS(q % 2)
                for f in range(KT):
                    b = bank(pe, f"gu{i}.{e}.{f}")
                    for n, wn in enumerate(("wg", "wu")):
                        w = weight(pe, f"{wn}{i}.{e}.{f // 2}")
                        for k in range(KT):
                            if later(pe, f"free.xs{i}.{q}.{k}"):
                                pe.wait_ge(*at(f"free.xs{i}.{q}.{k}"))
                            ins = pe.matmul(b[:, 128 * n:128 * n + mx], w[:, k, (f % 2) * P:(f % 2) * P + P],
                                            xs[:, k, e % 4, 0:mx], start=k == 0, stop=k == KT - 1)
                    did(T_, ins.then_inc(tensor_done, 1), f"gu{i}.{e}.{f}")
                    if f % 2 == 1:
                        for wn in ("wg", "wu"):
                            marks[f"wf.{wn}{i}.{e}.{f // 2}"] = (T_, count[T_])
                if e % 4 == 0 and q < 3:
                    gather(q + 1)
                for n in range(2):
                    b = bank(pe, f"y{i}.{e}.{n}")
                    for f in range(KT):
                        w = weight(pe, f"wd{i}.{e}.{n}.{f // 4}")
                        if later(pe, f"hid{i}.{e}.{f}"):
                            pe.wait_ge(*at(f"hid{i}.{e}.{f}"))
                        ins = pe.matmul(b[0:mx, :], HID[:, f, 0:mx], w[:, f % 4, :], start=f == 0, stop=f == KT - 1)
                        if f == 3:
                            did(T_, ins.then_inc(tensor_done, 1), f"wf.wd{i}.{e}.{n}.0")
                    did(T_, ins.then_inc(tensor_done, 1), f"y{i}.{e}.{n}")
                    marks[f"wf.wd{i}.{e}.{n}.1"] = (T_, count[T_])
            if later(pe, f"sel{i}"):
                pe.wait_ge(*at(f"sel{i}"))
            for j in range(8):
                for nm, src in (("pb", POSM), ("ab", AT)):
                    b = bank(pe, f"{nm}{i}.{j}")
                    did(T_, pe.matmul(b, sel[0:NE, j, :], src[:, 0:TX], start=True, stop=True).then_inc(tensor_done, 1), f"{nm}{i}.{j}")
            if i == 0:
                for j in range(4):
                    for nm, src in (("pb", POSM), ("ab", AT)):
                        b = bank(pe, f"{nm}{i}.c{j}")
                        did(T_, pe.matmul(b[:, 0:TC], sel[0:NE, 8 + j, :], src[:, TX:TA], start=True, stop=True).then_inc(tensor_done, 1), f"{nm}{i}.c{j}")
            if later(pe, f"free.y{i}.{NE - 1}.1"):
                pe.wait_ge(*at(f"free.y{i}.{NE - 1}.1"))
            for m in range(KT):
                for s0, sn in segs:
                    b = bank(pe, f"mo{i}.{m}.{s0}")
                    ys, sm, nj, pre = (YSX, SMX, 8, "") if s0 == 0 else (YSC, SMC, 4, "c")
                    for j in range(nj):
                        if later(pe, f"free.pb{i}.{pre}{j}"):
                            pe.wait_ge(*at(f"free.pb{i}.{pre}{j}"))
                        ins = pe.matmul(b[:, 0:sn], ys[:, j, m * P:m * P + P], sm[:, j, :], start=j == 0, stop=j == nj - 1)
                    did(T_, ins.then_inc(tensor_done, 1), f"mo{i}.{m}.{s0}")

        def moe_scalar(act, i):
            ntt = 6 if i == 0 else 4
            if later(act, f"lg{i}"):
                act.wait_ge(*at(f"lg{i}"))
            did(A_, act.activation(AFF[:, 0:ntt, :], AFF[:, 0:ntt, :], ACT.Exp).then_inc(scalar_done, 1), f"ex{i}")
            for tt in range(ntt):
                for half in range(2):
                    t = tile(act, f"ht{i}.{tt}.{half}")
                    did(A_, act.activation(HT[:, tt, 512 * half:512 * half + 512], t, ACT.Copy).then_inc(scalar_done, 1), f"free.ht{i}.{tt}.{half}")
            for s0, sn in moe_segs(i):
                t = tile(act, f"at{i}.{s0}")
                did(A_, act.activation(AT[:, s0:s0 + sn], t[0:NE, 0:sn], ACT.Copy).then_inc(scalar_done, 1), f"free.at{i}.{s0}")
            if i == 1:
                experts1_scalar(act)
            for e in range(NE) if i == 0 else ():
                mx = 96 if i == 0 else 64
                for f in range(KT):
                    t = tile(act, f"gu{i}.{e}.{f}")
                    n = e * KT + f
                    if n >= 2:
                        e0, f0 = divmod(n - 2, KT)
                        if later(act, f"hid{i}.{e0}.{f0}"):
                            act.wait_ge(*at(f"hid{i}.{e0}.{f0}"))
                    did(A_, act.activation(SIL[:, n % 2, 0:mx], t[:, 0:mx], ACT.Silu).then_inc(scalar_done, 1), f"sil{i}.{e}.{f}")
                for n in range(2):
                    t = tile(act, f"y{i}.{e}.{n}")
                    o = 64 * (e % 2)
                    did(A_, act.activation(YSX[o:o + 64, e // 2, 512 * n:512 * n + 512], t[0:64, :], ACT.Copy).then_inc(scalar_done, 1), None if i == 0 else f"free.y{i}.{e}.{n}")
                    if i == 0:
                        o = 32 * (e % 4)
                        did(A_, act.activation(YSC[o:o + 32, e // 4, 512 * n:512 * n + 512], t[64:96, :], ACT.Copy).then_inc(scalar_done, 1), f"free.y{i}.{e}.{n}")
            for pre, nj, w in (("", 8, TX), ("c", 4, TC)) if i == 0 else (("", 8, TX),):
                for j in range(nj):
                    t = tile(act, f"ab{i}.{pre}{j}")
                    n = j if pre == "" else 8 + j
                    if n >= 2:
                        if later(act, f"free.pb{i}.{('' if n - 2 < 8 else 'c')}{n - 2 if n - 2 < 8 else n - 10}"):
                            act.wait_ge(*at(f"free.pb{i}.{('' if n - 2 < 8 else 'c')}{n - 2 if n - 2 < 8 else n - 10}"))
                    did(A_, act.activation(AB[:, n % 2, 0:w], t[:, 0:w], ACT.Copy).then_inc(scalar_done, 1), f"free.ab{i}.{pre}{j}")

        def moe_vector(dve, i):
            segs = moe_segs(i)
            ntt = 6 if i == 0 else 4
            w = TA if i == 0 else TX
            t = tile(dve, f"rt{i}")[:, 0:ntt * NE].rearrange("p (t e) -> p t e", e=NE)
            did(V, dve.tensor_reduce(MX[:, 0:ntt], t, AX, ALU.max).then_inc(vector_done, 1))
            dve.wait_ge(*own(dve, V))
            did(V, dve.tensor_tensor(AFF[:, 0:ntt, :], t, MX[:, 0:ntt].unsqueeze(2).to_broadcast([P, ntt, NE]),
                                     ALU.subtract).then_inc(vector_done, 1), f"lg{i}")
            marks[f"free.rt{i}"] = marks[f"lg{i}"]
            if later(dve, f"ex{i}"):
                dve.wait_ge(*at(f"ex{i}"))
            did(V, dve.tensor_reduce(MX[:, 0:ntt], AFF[:, 0:ntt, :], AX, ALU.add).then_inc(vector_done, 1))
            dve.wait_ge(*own(dve, V))
            did(V, dve.reciprocal(MX[:, 0:ntt], MX[:, 0:ntt]).then_inc(vector_done, 1))
            dve.wait_ge(*own(dve, V))
            did(V, dve.tensor_tensor(AFF[:, 0:ntt, :], AFF[:, 0:ntt, :],
                                     MX[:, 0:ntt].unsqueeze(2).to_broadcast([P, ntt, NE]), ALU.mult).then_inc(vector_done, 1), f"aff{i}")
            for s0, sn in segs:
                if later(dve, f"free.at{i}.{s0}"):
                    dve.wait_ge(*at(f"free.at{i}.{s0}"))
                did(V, dve.tensor_copy(WORK[:, s0:s0 + sn], AT[:, s0:s0 + sn]).then_inc(vector_done, 1))
                dve.wait_ge(*own(dve, V))
                for r in range(2 * sn // NE // 8):
                    did(V, dve.max(M8, WORK[:, s0:s0 + sn]).then_inc(vector_done, 1))
                    dve.wait_ge(*own(dve, V))
                    did(V, dve.match_replace(WORK[:, s0:s0 + sn], M8, WORK[:, s0:s0 + sn], -1.0).then_inc(vector_done, 1))
                    dve.wait_ge(*own(dve, V))
            did(V, dve.tensor_scalar(WORK[:, 0:w], WORK[:, 0:w], 0.0, None, ALU.is_lt).then_inc(vector_done, 1))
            dve.wait_ge(*own(dve, V))
            for s0, sn in segs:
                did(V, dve.tensor_tensor_scan(POSM[:, s0:s0 + sn], ones[0:NE, 0:1].to_broadcast([NE, sn]),
                                              WORK[:, s0:s0 + sn], 0.0, ALU.mult, ALU.add).then_inc(vector_done, 1))
            dve.wait_ge(*own(dve, V))
            did(V, dve.tensor_tensor(POSM[:, 0:w], POSM[:, 0:w], WORK[:, 0:w], ALU.mult).then_inc(vector_done, 1))
            dve.wait_ge(*own(dve, V))
            did(V, dve.tensor_scalar(POSM[:, 0:w], POSM[:, 0:w], -1.0, None, ALU.add).then_inc(vector_done, 1), f"posm{i}")
            t = tile(dve, f"pt{i}")
            did(V, dve.tensor_copy(POST[:, 0:ntt, :], t[:, 0:ntt * NE].rearrange("p (t e) -> p t e", e=NE)).then_inc(vector_done, 1), f"free.pt{i}")
            dve.wait_ge(*own(dve, V))

            def onehot(q):
                if q:
                    if later(dve, f"xs{i}.{q - 1}.{KT - 1}"):
                        dve.wait_ge(*at(f"xs{i}.{q - 1}.{KT - 1}"))
                for tt in range(ntt):
                    c = CAPX if tt < 4 else CAPC
                    did(V, dve.tensor_tensor(
                        GM[:, tt, 0:4 * c].rearrange("p (e c) -> p e c", c=c),
                        iota[:, 0:c].unsqueeze(1).to_broadcast([P, 4, c]),
                        POST[:, tt, 4 * q:4 * q + 4].unsqueeze(2).to_broadcast([P, 4, c]), ALU.is_equal).then_inc(vector_done, 1))
                marks[f"gm{i}.{q}"] = (V, count[V])

            def take(q):
                xs = XS(q % 2)
                if q >= 2:
                    if later(dve, f"gu{i}.{4 * (q - 2) + 3}.{KT - 1}" if i == 0 else f"u1.{4 * (q - 2) + 3}"):
                        dve.wait_ge(*at(f"gu{i}.{4 * (q - 2) + 3}.{KT - 1}" if i == 0 else f"u1.{4 * (q - 2) + 3}"))
                else:
                    if later(dve, f"ht{i}.{ntt - 1}.1"):
                        dve.wait_ge(*at(f"ht{i}.{ntt - 1}.1"))
                for k in range(KT):
                    t = tile(dve, f"xs{i}.{q}.{k}")
                    did(V, dve.tensor_copy(xs[:, k, :, 0:64], t[:, 0:256].rearrange("p (e c) -> p e c", c=64)).then_inc(vector_done, 1), None if i == 0 else f"free.xs{i}.{q}.{k}")
                    if i == 0:
                        did(V, dve.tensor_copy(xs[:, k, :, 64:96], t[:, 256:384].rearrange("p (e c) -> p e c", c=32)).then_inc(vector_done, 1), f"free.xs{i}.{q}.{k}")

            onehot(0)
            take(0)
            mx = 96 if i == 0 else 64
            if i == 1:
                experts1_vector(dve, onehot, take)
            for e in range(NE) if i == 0 else ():
                if e % 4 == 0 and e < 12:
                    onehot(e // 4 + 1)
                for f in range(KT):
                    t = tile(dve, f"gu{i}.{e}.{f}")
                    if later(dve, f"sil{i}.{e}.{f}"):
                        dve.wait_ge(*at(f"sil{i}.{e}.{f}"))
                    if e and f == 0:
                        if later(dve, f"y{i}.{e - 1}.1"):
                            dve.wait_ge(*at(f"y{i}.{e - 1}.1"))
                    did(V, dve.tensor_tensor(HID[:, f, 0:mx], SIL[:, (e * KT + f) % 2, 0:mx], t[:, 128:128 + mx], ALU.mult).then_inc(vector_done, 1), f"hid{i}.{e}.{f}")
                    marks[f"free.gu{i}.{e}.{f}"] = (V, count[V])
                if e % 4 == 0 and e < 12:
                    take(e // 4 + 1)
            for pre, nj, sn, sm in (("", 8, TX, SMX), ("c", 4, TC, SMC)) if i == 0 else (("", 8, TX, SMX),):
                for j in range(nj):
                    t = tile(dve, f"pb{i}.{pre}{j}")
                    if later(dve, f"free.ab{i}.{pre}{j}"):
                        dve.wait_ge(*at(f"free.ab{i}.{pre}{j}"))
                    n = j if pre == "" else 8 + j
                    io = col("iop", 0 if pre == "" else 1)
                    did(V, dve.scalar_tensor_tensor(sm[:, j, :], t[:, 0:sn], io, AB[:, n % 2, 0:sn],
                                                    ALU.is_equal, ALU.mult).then_inc(vector_done, 1), f"free.pb{i}.{pre}{j}")
            for m in range(KT):
                for n, (s0, sn) in enumerate(segs):
                    t = tile(dve, f"mo{i}.{m}.{s0}")
                    x = X[:, m, s0:s0 + sn]
                    did(V, dve.scalar_tensor_tensor(x, t[:, 0:sn], ada[:, 40 + m, n:n + 1], x, ALU.mult, ALU.add).then_inc(vector_done, 1), f"free.mo{i}.{m}.{s0}")

        def moe_pool(pool, i):
            if later(pool, f"xs{i}.3.{KT - 1}"):
                pool.wait_ge(*at(f"xs{i}.3.{KT - 1}"))
            did("aux", pool.dma_start(sel[0:NE, :, :], a["sel"].rearrange("e (j p) -> e j p", p=P)).then_inc(constants_in, 16), f"sel{i}", by=16)

        XX = S(0, KT, TA)
        XJ = S(6144, KT, TA)
        ST = [S(12288 + TA * n, TA) for n in range(10)]
        LH = S(12288 + 10 * TA, 2, TA)
        SQ, RN, KS, AS0, AS1 = ST[5], ST[6], ST[7], ST[8], ST[9]
        HALF = float(math.exp(-0.5))
        order = (1, 4, 2, 3, 0, 5)
        last_mm = {}

        def jsegs(j):
            return XSEG if j in (0, 5) else SEGS

        def rw_tensor(pe):
            def xj(j):
                return lambda k, s0, sn: XJ[:, k, s0:s0 + sn]

            def down(tag, wn, j, last_name):
                w = weight(pe, wn)
                for s0, sn in jsegs(j):
                    b = bank(pe, f"{tag}.{s0}")
                    for k in range(KT):
                        if later(pe, f"xj{j}.{k}"):
                            pe.wait_ge(*at(f"xj{j}.{k}"))
                        ins = pe.matmul(b[:, 0:sn], w[:, k, :], XJ[:, k, s0:s0 + sn], start=k == 0, stop=k == KT - 1)
                    did(T_, ins.then_inc(tensor_done, 1), f"{tag}.{s0}")
                marks["wf." + wn] = (T_, count[T_])
                marks[f"xjfree{j}"] = (T_, count[T_])

            down("lw", "w1", 1, None)
            w = weight(pe, "w2")
            for d in range(2):
                for m in range(KT):
                    for s0, sn in SEGS:
                        if later(pe, "free.lw.0"):
                            pe.wait_ge(*at("free.lw.0"))
                        if later(pe, "free.lw.512"):
                            pe.wait_ge(*at("free.lw.512"))
                        b = bank(pe, f"zw{d}.{m}.{s0}")
                        did(T_, pe.matmul(b[:, 0:sn], w[64 * d:64 * d + 64, 0, m * P:m * P + P],
                                          LH[64 * d:64 * d + 64, 0, s0:s0 + sn], start=True, stop=True).then_inc(tensor_done, 1), f"zw{d}.{m}.{s0}")
            marks["wf.w2"] = (T_, count[T_])
            down("la", "a1", 4, None)
            wa = weight(pe, "a2")
            for m in range(KT):
                w = weight(pe, f"wk.{m // 2}")
                for s0, sn in SEGS:
                    b = bank(pe, f"k.{m}.{s0}")
                    for k in range(KT):
                        if later(pe, f"xj2.{k}"):
                            pe.wait_ge(*at(f"xj2.{k}"))
                        ins = pe.matmul(b[:, 0:sn], w[:, k, (m % 2) * P:(m % 2) * P + P], XJ[:, k, s0:s0 + sn],
                                        start=k == 0, stop=k == KT - 1)
                    did(T_, ins.then_inc(tensor_done, 1), f"k.{m}.{s0}")
                if m % 2:
                    marks[f"wf.wk.{m // 2}"] = (T_, count[T_])
                for d in range(2):
                    for s0, sn in SEGS:
                        if later(pe, "free.la.0"):
                            pe.wait_ge(*at("free.la.0"))
                        if later(pe, "free.la.512"):
                            pe.wait_ge(*at("free.la.512"))
                        b = bank(pe, f"a{d}.{m}.{s0}")
                        did(T_, pe.matmul(b[:, 0:sn], wa[64 * d:64 * d + 64, 0, m * P:m * P + P],
                                          LH[64 * d:64 * d + 64, 1, s0:s0 + sn], start=True, stop=True).then_inc(tensor_done, 1), f"a{d}.{m}.{s0}")
                if m == KT - 1:
                    marks["xjfree2"] = (T_, count[T_])
                for s0, sn in SEGS:
                    if later(pe, f"ksq.{m}"):
                        pe.wait_ge(*at(f"ksq.{m}"))
                    b = bank(pe, f"kn.{m}.{s0}")
                    did(T_, pe.matmul(b[:, 0:sn], bones[:, :], SQ[:, s0:s0 + sn], start=True, stop=True).then_inc(tensor_done, 1), f"kn.{m}.{s0}")
            marks["wf.a2"] = (T_, count[T_])
            for tag, wn, j in (("v", "wv", 3), ("r", "wr", 0)):
                linear_tensor(pe, tag, wn, xj(j), jsegs(j), lambda k, j=j: f"xj{j}.{k}")
                marks[f"xjfree{j}"] = (T_, count[T_])
            down("lg", "g1", 5, None)
            w = weight(pe, "g2")
            for m in range(KT):
                if later(pe, "free.lg.0"):
                    pe.wait_ge(*at("free.lg.0"))
                b = bank(pe, f"g.{m}.0")
                did(T_, pe.matmul(b, w[:, 0, m * P:m * P + P], LH[:, 0, 0:TX], start=True, stop=True).then_inc(tensor_done, 1), f"g.{m}.0")
            marks["wf.g2"] = (T_, count[T_])

        def rw_vector(dve):
            for step in [f"n1.h{k}" for k in range(KT)]:
                if later(dve, step):
                    dve.wait_ge(*at(step))

            def sub(k, o0, n, i0):
                did(V, dve.tensor_tensor(XX[:, k, o0:o0 + n], H[:, k, i0:i0 + n], H[:, k, o0:o0 + n], ALU.subtract).then_inc(vector_done, 1))

            def neg(out_, in_):
                did(V, dve.tensor_scalar(out_, in_, -1.0, None, ALU.mult).then_inc(vector_done, 1))
            for k in range(KT):
                hx = H[:, k, 0:TX].rearrange("p (r c) -> p r c", c=64)
                xx = XX[:, k, 0:TX].rearrange("p (r c) -> p r c", c=64)
                if k < 2:
                    did(V, dve.tensor_tensor(xx[:, :, 1:64], hx[:, :, 0:63], hx[:, :, 1:64], ALU.subtract).then_inc(vector_done, 1))
                    neg(xx[:, :, 0:1], hx[:, :, 0:1])
                elif k < 4:
                    did(V, dve.tensor_tensor(xx[:, :, 0:63], hx[:, :, 1:64], hx[:, :, 0:63], ALU.subtract).then_inc(vector_done, 1))
                    neg(xx[:, :, 63:64], hx[:, :, 63:64])
                elif k < 6:
                    sub(k, 64, TX - 64, 0)
                    neg(XX[:, k, 0:64], H[:, k, 0:64])
                else:
                    sub(k, 0, TX - 64, 64)
                    neg(XX[:, k, TX - 64:TX], H[:, k, TX - 64:TX])
                if k < 4:
                    sub(k, TX + 1, TC - 1, TX)
                    neg(XX[:, k, TX:TX + 1], H[:, k, TX:TX + 1])
                else:
                    sub(k, TX, TC - 1, TX + 1)
                    neg(XX[:, k, TA - 1:TA], H[:, k, TA - 1:TA])
            dve.wait_ge(*own(dve, V))

            def mix(n):
                j = order[n]
                if n:
                    if later(dve, f"xjfree{order[n - 1]}"):
                        dve.wait_ge(*at(f"xjfree{order[n - 1]}"))
                w = TX if j in (0, 5) else TA
                for k in range(KT):
                    did(V, dve.scalar_tensor_tensor(XJ[:, k, 0:w], XX[:, k, 0:w], col("mix", 8 * j + k), H[:, k, 0:w],
                                                    ALU.mult, ALU.add).then_inc(vector_done, 1), f"xj{j}.{k}")
            mix(0)
            for d in range(2):
                for m in range(KT):
                    s = (d * KT + m) % 4
                    if later(dve, f"zs{d}.{m}"):
                        dve.wait_ge(*at(f"zs{d}.{m}"))
                    did(V, dve.tensor_scalar(ST[s], ST[s], -HALF, None, ALU.mult).then_inc(vector_done, 1), f"lw{d}.{m}")
                    if d == 0 and m == 0:
                        mix(1)
            mix(2)
            for m in range(KT):
                if later(dve, f"ks.{m}"):
                    dve.wait_ge(*at(f"ks.{m}"))
                if m:
                    if later(dve, f"s.kk.{m - 1}"):
                        dve.wait_ge(*at(f"s.kk.{m - 1}"))
                else:
                    if later(dve, "s.lw1.4"):
                        dve.wait_ge(*at("s.lw1.4"))
                    if later(dve, "s.lw1.5"):
                        dve.wait_ge(*at("s.lw1.5"))
                    if later(dve, "s.lw1.6"):
                        dve.wait_ge(*at("s.lw1.6"))
                    if later(dve, "s.lw1.7"):
                        dve.wait_ge(*at("s.lw1.7"))
                did(V, dve.tensor_scalar(ST[0], KS, col("kk", m), None, ALU.mult).then_inc(vector_done, 1))
                dve.wait_ge(*own(dve, V))
                did(V, dve.tensor_tensor(SQ, ST[0], ST[0], ALU.mult).then_inc(vector_done, 1), f"ksq.{m}")
                if m:
                    for step in [f"s.{x}.{m - 1}" for x in ("kka0", "kka1", "kd0", "kd1")]:
                        if later(dve, step):
                            dve.wait_ge(*at(step))
                if later(dve, f"as.{m}"):
                    dve.wait_ge(*at(f"as.{m}"))
                for d, AS in ((0, AS0), (1, AS1)):
                    did(V, dve.tensor_scalar(ST[3 + d], AS, col("ka", m), small[:, 32 + m:33 + m], ALU.mult, ALU.add).then_inc(vector_done, 1))
                dve.wait_ge(*own(dve, V))
                for d in range(2):
                    did(V, dve.tensor_tensor(ST[3 + d], ST[3 + d], KS, ALU.mult).then_inc(vector_done, 1))
                if later(dve, f"rn.{m}"):
                    dve.wait_ge(*at(f"rn.{m}"))
                did(V, dve.reciprocal(RN, RN).then_inc(vector_done, 1))
                dve.wait_ge(*own(dve, V))
                did(V, dve.tensor_tensor(ST[0], ST[0], RN, ALU.mult).then_inc(vector_done, 1))
                dve.wait_ge(*own(dve, V))
                for d, AS in ((0, AS0), (1, AS1)):
                    did(V, dve.tensor_tensor(ST[1 + d], ST[0], AS, ALU.mult).then_inc(vector_done, 1))
                marks[f"kout.{m}"] = (V, count[V])
            mix(3)
            mix(4)
            mix(5)

        def rw_scalar(act):
            def lora(tag, row, func, segs):
                for s0, sn in segs:
                    t = tile(act, f"{tag}.{s0}")
                    did(A_, act.activation(LH[:, row, s0:s0 + sn], t[:, 0:sn], func).then_inc(scalar_done, 1), f"free.{tag}.{s0}")

            lora("lw", 0, ACT.Tanh, SEGS)
            for d in range(2):
                for m in range(KT):
                    n = d * KT + m
                    s = n % 4
                    if n >= 4:
                        if later(act, f"s.lw{(n - 4) // KT}.{(n - 4) % KT}"):
                            act.wait_ge(*at(f"s.lw{(n - 4) // KT}.{(n - 4) % KT}"))
                    for s0, sn in SEGS:
                        t = tile(act, f"zw{d}.{m}.{s0}")
                        did(A_, act.activation(ST[s][:, s0:s0 + sn], t[:, 0:sn], ACT.Sigmoid, bias=col("w0", 8 * d + m)).then_inc(scalar_done, 1), f"free.zw{d}.{m}.{s0}")
                    marks[f"zs{d}.{m}"] = (A_, count[A_])
            lora("la", 1, ACT.Copy, SEGS)
            for m in range(KT):
                if m:
                    if later(act, f"kout.{m - 1}"):
                        act.wait_ge(*at(f"kout.{m - 1}"))
                for s0, sn in SEGS:
                    t = tile(act, f"k.{m}.{s0}")
                    did(A_, act.activation(KS[:, s0:s0 + sn], t[:, 0:sn], ACT.Copy).then_inc(scalar_done, 1), f"free.k.{m}.{s0}")
                marks[f"ks.{m}"] = (A_, count[A_])
                for d, AS in ((0, AS0), (1, AS1)):
                    for s0, sn in SEGS:
                        t = tile(act, f"a{d}.{m}.{s0}")
                        did(A_, act.activation(AS[:, s0:s0 + sn], t[:, 0:sn], ACT.Sigmoid, bias=col("a0", 8 * d + m)).then_inc(scalar_done, 1), f"free.a{d}.{m}.{s0}")
                marks[f"as.{m}"] = (A_, count[A_])
                for s0, sn in SEGS:
                    t = tile(act, f"kn.{m}.{s0}")
                    did(A_, act.activation(RN[:, s0:s0 + sn], t[:, 0:sn], ACT.Sqrt, bias=eps[:, 2:3]).then_inc(scalar_done, 1), f"free.kn.{m}.{s0}")
                marks[f"rn.{m}"] = (A_, count[A_])
            if later(act, f"s.kd1.{KT - 1}"):
                act.wait_ge(*at(f"s.kd1.{KT - 1}"))
            if later(act, f"s.kd0.{KT - 1}"):
                act.wait_ge(*at(f"s.kd0.{KT - 1}"))
            if later(act, f"s.kka1.{KT - 1}"):
                act.wait_ge(*at(f"s.kka1.{KT - 1}"))
            if later(act, f"s.kka0.{KT - 1}"):
                act.wait_ge(*at(f"s.kka0.{KT - 1}"))
            if later(act, f"s.kk.{KT - 1}"):
                act.wait_ge(*at(f"s.kk.{KT - 1}"))
            n = 0
            for tag in ("v", "r", "g"):
                if tag == "g":
                    lora("lg", 0, ACT.Sigmoid, XSEG)
                for m in range(KT):
                    s = n % 4
                    if n >= 4:
                        if later(act, f"s.{'vrg'[(n - 4) // KT]}.{(n - 4) % KT}"):
                            act.wait_ge(*at(f"s.{'vrg'[(n - 4) // KT]}.{(n - 4) % KT}"))
                    for s0, sn in SEGS if tag == "v" else XSEG:
                        t = tile(act, f"{tag}.{m}.{s0}")
                        did(A_, act.activation(ST[s][:, s0:s0 + sn], t[:, 0:sn], ACT.Copy).then_inc(scalar_done, 1), f"free.{tag}.{m}.{s0}")
                    marks[f"{tag}o.{m}"] = (A_, count[A_])
                    n += 1

        def rw_pool(pool):
            def store(stream, m, s, w, after):
                if later(pool, after):
                    pool.wait_ge(*at(after))
                nch = w // CH
                did(f"st{s}", pool.dma_start(dram[stream][0:nch, :, m, :].rearrange("c p t -> p c t"),
                                             ST[s][:, 0:w].rearrange("p (c t) -> p c t", t=CH)).then_inc(sems[f"st{s}"], 16), f"s.{stream}.{m}", by=16)
            for d in range(2):
                for m in range(KT):
                    store(f"lw{d}", m, (d * KT + m) % 4, TA, f"lw{d}.{m}")
            for m in range(KT):
                for n, s in enumerate(("kk", "kka0", "kka1", "kd0", "kd1")):
                    store(s, m, n, TA, f"kout.{m}")
            n = 0
            for tag in ("v", "r", "g"):
                for m in range(KT):
                    store(tag, m, n % 4, TA if tag == "v" else TX, f"{tag}o.{m}")
                    n += 1
            for s in range(5):
                pool.wait_ge(sems[f"st{s}"], count[f"st{s}"])

        LD = H[:, :, :].rearrange("p k t -> p (k t)").rearrange("p (b s n) -> p b s n", b=2, s=6)
        off = 0

        def take_scr(*dims):
            nonlocal off
            t = S(off, *dims)
            off += int(np.prod(dims))
            return t
        YA = take_scr(KT, TX)
        EP, EN, EM, CS = (take_scr(512) for _ in range(4))
        BK = [take_scr(KT, 2, CH) for _ in range(2)]
        AR = [[take_scr(KT, 2, CH) for _ in range(2)],
              [X[:, :, TX + 128 * d:TX + 128 * d + 128].rearrange("p k (s t) -> p k s t", s=2) for d in range(2)]]

        def held(n, off, *dims):
            t = ring[:, place[f"hold.{n}"][0], off:off + int(np.prod(dims))]
            return t.rearrange("p (a b) -> p a b", b=dims[1])
        SC = [take_scr(NE, 128), held(0, 0, NE, 128)]
        NM4 = [take_scr(LEVELS * 8, CH), None]
        NM = [[NM4[0][:, 8 * l:8 * l + 8, :] for l in range(LEVELS)],
              [held(1 + l // 4, (l % 4) * 512, 8, CH) for l in range(LEVELS)]]
        XI, XT, GT, QB = ([take_scr(8, CH), held(3, 512 * n, 8, CH)] for n in range(4))
        BKT = [take_scr(NE, CH), held(2, 1024, NE, CH)]
        SV = [take_scr(NE, CH), held(4, 0, NE, CH)]
        ZS = [take_scr(8, CH) for _ in range(2)]
        MD = take_scr(2, 128)
        LM = take_scr(2, LEVELS * CH)
        RST = take_scr(512)
        PT = take_scr(4, 8)

        def units():
            for step in range(NCH):
                pair = []
                for d in range(2):
                    s = step - NCHC
                    if s < 0:
                        c = NCHX + (step if d == 0 else NCHC - 1 - step)
                    else:
                        c = s if d == 0 else NCHX - 1 - s
                    pair.append((2 * step + d, d, c, s >= 0, s < NCHX // 2))
                yield pair

        def rows(q):
            return slice(64 * q, 64 * q + 64)

        def odd(t, q):
            return t.rearrange("p (j q) c -> p j q c", q=2)[:, :, q, :]

        def pairs(t):
            return t[:, 0:256].rearrange("p (j c) -> p j c", c=CH)

        def wkv_pool(pool):
            did("aux", pool.dma_start(MD[:, :, :], a["md"].rearrange("p (d c) -> p d c", d=2)).then_inc(constants_in, 16), by=16)
            did("aux", pool.dma_start(LM[:, :, :], a["lm"].rearrange("p (d c) -> p d c", d=2)).then_inc(constants_in, 16), by=16)
            did("aux", pool.dma_start(RST, a["rst"]).then_inc(constants_in, 16), "wkvc", by=16)

            def loads(u, d, c, img, first):
                if u >= 2:
                    if later(pool, f"til{u - 2}"):
                        pool.wait_ge(*at(f"til{u - 2}"))
                    if later(pool, f"V{u - 2}.1"):
                        pool.wait_ge(*at(f"V{u - 2}.1"))
                names = (f"kd{d}", "v", "kk", f"kka{d}", f"lw{d}") + (("r",) if img else ())
                for n, s in enumerate(names):
                    did(f"ld{d}", pool.dma_start(LD[:, d, n, :], dram[s][c].rearrange("p k t -> p (k t)")).then_inc(sems[f"ld{d}"], 16), by=16)
                marks[f"ld{u}"] = (f"ld{d}", count[f"ld{d}"])
            steps = list(units())
            for un in steps[0]:
                loads(*un)
            if later(pool, "wkvc"):
                pool.wait_ge(*at("wkvc"))
            for n, pair in enumerate(steps):
                for l in range(LEVELS):
                    for u, d, c, img, first in pair:
                        if later(pool, f"sc{u}.3"):
                            pool.wait_ge(*at(f"sc{u}.3"))
                        for q in range(2):
                            did(G_, pool.tensor_tensor(
                                NM[d][l][rows(1 - q)], odd(SC[d][rows(1 - q)], q)[:, :, 0:CH],
                                LM[rows(1 - q), d, l * CH:l * CH + CH].unsqueeze(1).to_broadcast([64, 8, CH]), ALU.mult).then_inc(pool_done, 1))
                        marks[f"nm{u}.{l}"] = (G_, count[G_])
                    if n + 1 < len(steps) and l >= 4:
                        loads(*steps[n + 1][l - 4])

        def wkv_scalar(act):
            def exps(u, d, c, img, first):
                if u:
                    if later(act, f"til{u - 1}"):
                        act.wait_ge(*at(f"til{u - 1}"))
                if later(act, f"cs{u}"):
                    act.wait_ge(*at(f"cs{u}"))
                did(A_, act.activation(EM, EM, ACT.Exp).then_inc(scalar_done, 1))
                did(A_, act.activation(EN, CS, ACT.Exp, scale=-1.0).then_inc(scalar_done, 1))
                did(A_, act.activation(EP, CS, ACT.Exp).then_inc(scalar_done, 1), f"exps{u}")
            steps = list(units())
            exps(*steps[0][0])
            exps(*steps[0][1])
            for n, pair in enumerate(steps):
                for u, d, c, img, first in pair:
                    for q in range(2):
                        t = tile(act, f"T{u}.{q}")
                        did(A_, act.activation(odd(BKT[d], q), t.rearrange("p (h c) -> p h c", c=CH), ACT.Copy).then_inc(scalar_done, 1), f"free.T{u}.{q}")
                for l in range(1, LEVELS):
                    for u, d, c, img, first in pair:
                        for g in range(2):
                            t = tile(act, f"G{u}.{l}.{g}")
                            did(A_, act.activation(GT[d][:, 4 * g:4 * g + 4, :], pairs(t), ACT.Copy).then_inc(scalar_done, 1), f"free.G{u}.{l}.{g}")
                    if n + 1 < len(steps) and l in (2, 4):
                        exps(*steps[n + 1][l // 2 - 1])
                for u, d, c, img, first in pair:
                    for g in range(2):
                        t = tile(act, f"Q{u}.{g}")
                        did(A_, act.activation(QB[d][:, 4 * g:4 * g + 4, :], pairs(t), ACT.Copy).then_inc(scalar_done, 1), f"free.Q{u}.{g}")
                for u, d, c, img, first in pair:
                    for g in range(2):
                        t = pairs(tile(act, f"S{u}.{g}"))
                        for q in range(2):
                            did(A_, act.activation(odd(SV[d][rows(1 - q), 8 * g:8 * g + 8, :], q), t[rows(1 - q)], ACT.Copy).then_inc(scalar_done, 1))
                        marks[f"free.S{u}.{g}"] = (A_, count[A_])

        def wkv_vector(dve):
            did(V, dve.memset(ZS[0][:, :, :], 0.0).then_inc(vector_done, 1))
            did(V, dve.memset(ZS[1][:, :, :], 0.0).then_inc(vector_done, 1), "z0")
            if later(dve, "wkvc"):
                dve.wait_ge(*at("wkvc"))
            dve.wait_ge(*own(dve, V))

            def v3(t):
                return t.rearrange("p (j t) -> p j t", t=CH)

            def scan(u, d, c, img, first):
                if later(dve, f"ld{u}"):
                    dve.wait_ge(*at(f"ld{u}"))
                ld = LD[:, d]
                cs, lw = (CS, ld[:, 4, :]) if d == 0 else (CS[:, ::-1], ld[:, 4, ::-1])
                did(V, dve.tensor_tensor_scan(cs, RST, lw, 0.0, ALU.mult, ALU.add).then_inc(vector_done, 1))
                dve.wait_ge(*own(dve, V))
                did(V, dve.tensor_tensor(EM, CS, ld[:, 4, :], ALU.subtract).then_inc(vector_done, 1), f"cs{u}")

            def tildes(u, d, c, img, first):
                ld = LD[:, d]
                if later(dve, f"exps{u}"):
                    dve.wait_ge(*at(f"exps{u}"))
                if u >= 2:
                    if later(dve, f"T{u - 2}.1"):
                        dve.wait_ge(*at(f"T{u - 2}.1"))
                b, r = BK[d], AR[(u // 2) % 2][d]
                did(V, dve.scalar_tensor_tensor(r[:, :, 0, :], v3(ld[:, 2, :]), -1.0, v3(EM), ALU.mult, ALU.mult).then_inc(vector_done, 1))
                if img:
                    did(V, dve.tensor_tensor(r[:, :, 1, :], v3(ld[:, 5, :]), v3(EP), ALU.mult).then_inc(vector_done, 1))
                for q in range(2):
                    did(V, dve.tensor_tensor(b[rows(q), :, 1 - q, :], v3(ld[rows(q), 3, :]), v3(EN[rows(q)]), ALU.mult).then_inc(vector_done, 1))
                    did(V, dve.tensor_tensor(b[rows(q), :, q, :], v3(ld[rows(q), 0, :]), v3(EN[rows(q)]), ALU.mult).then_inc(vector_done, 1))
                e = CH - 1 if d == 0 else 0
                did(V, dve.tensor_copy(PT[:, u % 4, :], v3(EP)[:, :, e]).then_inc(vector_done, 1), f"til{u}")

            steps = list(units())
            for un in steps[0]:
                scan(*un)
                tildes(*un)
            idb = id64[:, :].unsqueeze(1).to_broadcast([P, 8, CH])
            for n, pair in enumerate(steps):
                for u, d, c, img, first in pair:
                    for b4 in range(4):
                        t = tile(dve, f"A{u}.{b4}").rearrange("p (h c) -> p h c", c=128)
                        w = 128 if img else CH
                        g, q = divmod(b4, 2)
                        did(V, dve.tensor_tensor(odd(SC[d][:, 8 * g:8 * g + 8, :], q)[:, :, 0:w], t[:, :, 0:w],
                                                 MD[:, d, 0:w].unsqueeze(1).to_broadcast([P, 4, w]), ALU.mult).then_inc(vector_done, 1), f"sc{u}.{b4}")
                        marks[f"free.A{u}.{b4}"] = (V, count[V])
                for u, d, c, img, first in pair:
                    for g in range(2):
                        t = tile(dve, f"V{u}.{g}")[0:64, :].rearrange("p (j q c) -> p j q c", q=2, c=CH)
                        for q in range(2):
                            did(V, dve.tensor_copy(odd(SV[d][rows(q), 8 * g:8 * g + 8, :], q), t[:, :, q, :]).then_inc(vector_done, 1))
                        marks[f"free.V{u}.{g}"] = (V, count[V])
                for u, d, c, img, first in pair:
                    if later(dve, f"nm{u}.0"):
                        dve.wait_ge(*at(f"nm{u}.0"))
                    did(V, dve.tensor_tensor(XI[d][:, :, :], NM[d][0], idb, ALU.add).then_inc(vector_done, 1), f"xi{u}.0.0")
                    marks[f"xi{u}.0.1"] = marks[f"xi{u}.0.0"]
                    for g in range(2):
                        t = pairs(tile(dve, f"G{u}.0.{g}"))
                        did(V, dve.tensor_tensor(XT[d][:, 4 * g:4 * g + 4, :], t, idb[:, 0:4, :], ALU.add).then_inc(vector_done, 1), f"xt{u}.0.{g}")
                        marks[f"free.G{u}.0.{g}"] = (V, count[V])
                for l in range(1, LEVELS):
                    for u, d, c, img, first in pair:
                        for g in range(2):
                            t = tile(dve, f"P{u}.{l}.{g}").rearrange("p (s j c) -> p s j c", s=2, c=CH)
                            x = XI[d][:, 4 * g:4 * g + 4, :]
                            did(V, dve.tensor_tensor(x, t[:, 0], x, ALU.add).then_inc(vector_done, 1), f"xi{u}.{l}.{g}")
                            if l < LEVELS - 1:
                                x = XT[d][:, 4 * g:4 * g + 4, :]
                                did(V, dve.tensor_tensor(x, t[:, 1], x, ALU.add).then_inc(vector_done, 1), f"xt{u}.{l}.{g}")
                            marks[f"free.P{u}.{l}.{g}"] = (V, count[V])
                    if n + 1 < len(steps):
                        if l in (1, 3):
                            scan(*steps[n + 1][l // 2])
                        if l in (2, 4):
                            tildes(*steps[n + 1][l // 2 - 1])
                if img:
                    for u, d, c, img, first in pair:
                        for g in range(2):
                            t = pairs(tile(dve, f"Y{u}.{g}"))
                            y = YA[:, 4 * g:4 * g + 4, c * CH:c * CH + CH]
                            ins = dve.tensor_copy(y, t) if first else dve.tensor_tensor(y, t, y, ALU.add)
                            did(V, ins.then_inc(vector_done, 1), f"free.Y{u}.{g}")
                for u, d, c, img, first in pair:
                    for g in range(2):
                        t = pairs(tile(dve, f"Z{u}.{g}"))
                        z = ZS[d][:, 4 * g:4 * g + 4, :]
                        did(V, dve.tensor_tensor(z, t, z, ALU.add).then_inc(vector_done, 1), f"free.Z{u}.{g}")
                dve.wait_ge(*own(dve, V))
                for u, d, c, img, first in pair:
                    z = ZS[d][:, :, :]
                    did(V, dve.tensor_tensor(z, z, PT[:, u % 4, :].unsqueeze(2).to_broadcast([P, 8, CH]), ALU.mult).then_inc(vector_done, 1), f"zn{u}")

        def wkv_tensor(pe):
            def each(g):
                return [(j, q, slice((j % 4) * CH, (j % 4) * CH + CH)) for j in range(4 * g, 4 * g + 4) for q in range(2)]

            for pair in units():
                for u, d, c, img, first in pair:
                    bk, ar = BK[d], AR[(u // 2) % 2][d]
                    if later(pe, f"til{u}"):
                        pe.wait_ge(*at(f"til{u}"))
                    if later(pe, "z0"):
                        pe.wait_ge(*at("z0"))
                    w = 128 if img else CH
                    for g in range(2):
                        for q in range(2):
                            b = bank(pe, f"A{u}.{2 * g + q}")
                            for n, j in enumerate(range(4 * g, 4 * g + 4)):
                                ins = pe.matmul(b[:, n * 128:n * 128 + w], bk[rows(q), j, :, :],
                                                ar[rows(q), j, :, :] if img else ar[rows(q), j, 0, :], start=True, stop=True)
                            did(T_, ins.then_inc(tensor_done, 1), f"A{u}.{2 * g + q}")
                for u, d, c, img, first in pair:
                    for q in range(2):
                        b = bank(pe, f"T{u}.{q}")
                        for j in range(8):
                            ins = pe.transpose(b[:, j * CH:j * CH + CH], BK[d][rows(q), j, :, :], ident[rows(q), rows(q)])
                        did(T_, ins.then_inc(tensor_done, 1), f"T{u}.{q}")
                for u, d, c, img, first in pair:
                    for g in range(2):
                        b = bank(pe, f"V{u}.{g}")
                        for j in range(4):
                            o = (4 * g + j) * CH
                            ins = pe.transpose(b[0:64, j * P:j * P + P], LD[:, d, 1, o:o + CH], ident[:, :])
                        did(T_, ins.then_inc(tensor_done, 1), f"V{u}.{g}")
                for l in range(LEVELS):
                    for u, d, c, img, first in pair:
                        if later(pe, f"nm{u}.{l}"):
                            pe.wait_ge(*at(f"nm{u}.{l}"))
                        for g in range(2):
                            b = bank(pe, f"G{u}.{l}.{g}")
                            if l:
                                if later(pe, f"xt{u}.{l - 1}.{g}"):
                                    pe.wait_ge(*at(f"xt{u}.{l - 1}.{g}"))
                            for j, q, o in each(g):
                                rhs = XT[d][rows(q), j, :] if l else id64[rows(q), :]
                                ins = pe.matmul(b[rows(q), o], NM[d][l][rows(q), j, :], rhs, start=True, stop=True)
                            did(T_, ins.then_inc(tensor_done, 1), f"G{u}.{l}.{g}")
                    if l == 0:
                        continue
                    for u, d, c, img, first in pair:
                        for g in range(2):
                            b = bank(pe, f"P{u}.{l}.{g}")
                            if later(pe, f"free.G{u}.{l}.{g}"):
                                pe.wait_ge(*at(f"free.G{u}.{l}.{g}"))
                            if later(pe, f"xi{u}.{l - 1}.{g}"):
                                pe.wait_ge(*at(f"xi{u}.{l - 1}.{g}"))
                            for j, q, o in each(g):
                                ins = pe.matmul(b[rows(q), o], GT[d][rows(q), j, :], XI[d][rows(q), j, :],
                                                start=True, stop=True)
                            if l < LEVELS - 1:
                                for j, q, o in each(g):
                                    ins = pe.matmul(b[rows(q), 256 + o.start:256 + o.stop], XI[d][rows(q), j, :],
                                                    GT[d][rows(q), j, :], start=True, stop=True)
                            did(T_, ins.then_inc(tensor_done, 1), f"P{u}.{l}.{g}")
                for u, d, c, img, first in pair:
                    ar = AR[(u // 2) % 2][d]
                    if later(pe, f"free.V{u}.0"):
                        pe.wait_ge(*at(f"free.V{u}.0"))
                    if later(pe, f"free.V{u}.1"):
                        pe.wait_ge(*at(f"free.V{u}.1"))
                    for step in [f"zn{u - 2}"] if u >= 2 else []:
                        if later(pe, step):
                            pe.wait_ge(*at(step))
                    for g in range(2):
                        b = bank(pe, f"Q{u}.{g}")
                        for j, q, o in each(g):
                            pe.matmul(b[rows(1 - q), o], ar[rows(q), j, 0, :], ZS[d][rows(q), j, :], start=True, stop=False)
                            ins = pe.matmul(b[rows(1 - q), o], SC[d][rows(q), 2 * j + q, 0:CH],
                                            SV[d][rows(q), 2 * j + q, :], start=False, stop=True)
                        did(T_, ins.then_inc(tensor_done, 1), f"Q{u}.{g}")
                for u, d, c, img, first in pair:
                    for g in range(2):
                        b = bank(pe, f"S{u}.{g}")
                        if later(pe, f"free.Q{u}.{g}"):
                            pe.wait_ge(*at(f"free.Q{u}.{g}"))
                        if later(pe, f"xi{u}.{LEVELS - 1}.{g}"):
                            pe.wait_ge(*at(f"xi{u}.{LEVELS - 1}.{g}"))
                        for j, q, o in each(g):
                            ins = pe.matmul(b[rows(q), o], XI[d][rows(q), j, :], QB[d][rows(q), j, :], start=True, stop=True)
                        did(T_, ins.then_inc(tensor_done, 1), f"S{u}.{g}")
                if img:
                    for u, d, c, img, first in pair:
                        ar = AR[(u // 2) % 2][d]
                        for g in range(2):
                            b = bank(pe, f"Y{u}.{g}")
                            if later(pe, f"free.S{u}.{g}"):
                                pe.wait_ge(*at(f"free.S{u}.{g}"))
                            for j, q, o in each(g):
                                pe.matmul(b[rows(q), o], ZS[d][rows(q), j, :], ar[rows(q), j, 1, :], start=True, stop=False)
                                ins = pe.matmul(b[rows(q), o], SV[d][:, 2 * j + q, :], SC[d][:, 2 * j + q, CH:2 * CH],
                                                start=False, stop=True)
                            did(T_, ins.then_inc(tensor_done, 1), f"Y{u}.{g}")
                for u, d, c, img, first in pair:
                    for g in range(2):
                        b = bank(pe, f"Z{u}.{g}")
                        if later(pe, f"free.S{u}.{g}"):
                            pe.wait_ge(*at(f"free.S{u}.{g}"))
                        if later(pe, f"free.T{u}.1"):
                            pe.wait_ge(*at(f"free.T{u}.1"))
                        for j, q, o in each(g):
                            ins = pe.matmul(b[rows(q), o], BKT[d][:, 2 * j + q, :], SV[d][:, 2 * j + q, :],
                                            start=True, stop=True)
                        did(T_, ins.then_inc(tensor_done, 1), f"Z{u}.{g}")
            for n in range(5):
                marks[f"wf.hold.{n}"] = (T_, count[T_])

        PL = [S(4096 + 2560 * b, 5, 512) for b in range(2)]
        PW = [S(9216 + 512 * n, 512) for n in range(5)]

        def post_pool(pool):
            for m in range(KT):
                if m >= 2:
                    if later(pool, f"yo.{m - 2}"):
                        pool.wait_ge(*at(f"yo.{m - 2}"))
                for n, s in enumerate(("r", "kd0", "kd1", "v", "g")):
                    did(f"ld{m % 2}", pool.dma_start(
                        PL[m % 2][:, n, :].rearrange("p (c t) -> p c t", t=CH),
                        dram[s][0:NCHX, :, m, :].rearrange("c p t -> p c t")).then_inc(sems[f"ld{m % 2}"], 16), by=16)
                marks[f"pl.{m}"] = (f"ld{m % 2}", count[f"ld{m % 2}"])

        def post_vector(dve):
            BS, YC, YQ, SD, BV = PW
            for m in range(KT):
                pl = PL[m % 2]
                y = YA[:, m, :]
                if later(dve, f"pl.{m}"):
                    dve.wait_ge(*at(f"pl.{m}"))
                did(V, dve.tensor_tensor(pl[:, 1, :], pl[:, 1, :], pl[:, 2, :], ALU.add).then_inc(vector_done, 1))
                dve.wait_ge(*own(dve, V))
                did(V, dve.scalar_tensor_tensor(BS, pl[:, 1, :], col("rk", m), pl[:, 0, :], ALU.mult, ALU.mult).then_inc(vector_done, 1), f"bs.{m}")
                t = tile(dve, f"mu.{m}")
                did(V, dve.scalar_tensor_tensor(YC, t, -1.0 / 64, y, ALU.mult, ALU.add).then_inc(vector_done, 1), f"free.mu.{m}")
                dve.wait_ge(*own(dve, V))
                did(V, dve.tensor_tensor(YQ, YC, YC, ALU.mult).then_inc(vector_done, 1), f"yq.{m}")
                t = tile(dve, f"bo.{m}")
                did(V, dve.tensor_tensor(BV, t, pl[:, 3, :], ALU.mult).then_inc(vector_done, 1), f"free.bo.{m}")
                if later(dve, f"free.va.{m}"):
                    dve.wait_ge(*at(f"free.va.{m}"))
                did(V, dve.reciprocal(SD, SD).then_inc(vector_done, 1))
                dve.wait_ge(*own(dve, V))
                did(V, dve.tensor_tensor(YC, YC, SD, ALU.mult).then_inc(vector_done, 1))
                dve.wait_ge(*own(dve, V))
                did(V, dve.tensor_scalar(YC, YC, col("lnw", m), col("lnb", m), ALU.mult, ALU.add).then_inc(vector_done, 1))
                dve.wait_ge(*own(dve, V))
                did(V, dve.tensor_tensor(YC, YC, BV, ALU.add).then_inc(vector_done, 1))
                dve.wait_ge(*own(dve, V))
                did(V, dve.tensor_tensor(y, YC, pl[:, 4, :], ALU.mult).then_inc(vector_done, 1), f"yo.{m}")
            residual_vector(dve, "wo", XSEG, 16)

        def post_scalar(act):
            for m in range(KT):
                t = tile(act, f"va.{m}")
                did(A_, act.activation(PW[3], t, ACT.Sqrt, bias=eps[:, 1:2], scale=1.0 / 64).then_inc(scalar_done, 1), f"free.va.{m}")

        def post_tensor(pe):
            def one(key, src, after=None):
                b = bank(pe, key)
                if after:
                    if later(pe, after):
                        pe.wait_ge(*at(after))
                did(T_, pe.matmul(b, bones[:, :], src, start=True, stop=True).then_inc(tensor_done, 1), key)
            for m in range(KT):
                one(f"mu.{m}", YA[:, m, :])
                one(f"bo.{m}", PW[0], f"bs.{m}")
                one(f"va.{m}", PW[2], f"yq.{m}")
            linear_tensor(pe, "wo", "wo", lambda k, s0, sn: YA[:, k, s0:s0 + sn], XSEG, lambda k: f"yo.{k}")

        MIX = S(0, KT, TX)
        CQ = S(4096, 3, TX)
        CKV = S(5632, 2, TX)
        QT = S(6656, 6, TX)
        KTT = S(9728, 6, TX)
        VT = S(12800, 4, 384)
        PB = S(14336, 2, 512)
        PTT = S(15360, 2, 512)
        TR = S(16384, 2, 512)
        TQ = S(17408, 5, 512)
        RC = S(19968, 2, 512)
        KW = S(20992, 512)
        NEG = S(21504, P)
        AST = S(21632, 4, 24)
        SCALE = 1.0 / math.sqrt(96.0)
        HR = slice(64, 96)
        ORDER = [(h, i) for h in range(6) for i in range(4)]

        def mla_pool(pool, l):
            did("aux", pool.dma_start(TR[HR, :, :], a["rope"].rearrange("p (s t) -> p s t", s=2)).then_inc(constants_in, 16), by=16)
            did("aux", pool.dma_start(NEG, a["neg"]).then_inc(constants_in, 16), f"mlac{l}", by=16)

        def mla_tensor(pe, l):
            t0 = f"i{l}."
            hk = f"n2{l}"
            for m in range(3):
                w = weight(pe, f"{t0}cq.{m // 2}")
                b = bank(pe, f"{t0}cq{m}")
                for k in range(KT):
                    if later(pe, f"{hk}.h{k}"):
                        pe.wait_ge(*at(f"{hk}.h{k}"))
                    ins = pe.matmul(b, w[:, k, (m % 2) * P:(m % 2) * P + P], H[:, k, 0:TX], start=k == 0, stop=k == KT - 1)
                did(T_, ins.then_inc(tensor_done, 1), f"{t0}cq{m}")
                if m:
                    marks[f"wf.{t0}cq.{m // 2}"] = (T_, count[T_])
            marks[f"wf.{t0}cq.0"] = marks[f"wf.{t0}cq.0"] if f"wf.{t0}cq.0" in marks else (T_, count[T_])
            w = weight(pe, f"{t0}ckv")
            for m in range(2):
                b = bank(pe, f"{t0}ckv{m}")
                for k in range(KT):
                    ins = pe.matmul(b, w[:, k, m * P:m * P + P], H[:, k, 0:TX], start=k == 0, stop=k == KT - 1)
                did(T_, ins.then_inc(tensor_done, 1), f"{t0}ckv{m}")
            marks[f"wf.{t0}ckv"] = (T_, count[T_])
            w = weight(pe, f"{t0}kr")
            for s in range(2):
                b = bank(pe, f"{t0}kr{s}")
                for k in range(KT):
                    ins = pe.matmul(b[HR, :], w[:, k, 32 * s:32 * s + 32], H[:, k, 0:TX], start=k == 0, stop=k == KT - 1)
                did(T_, ins.then_inc(tensor_done, 1), f"{t0}kr{s}")
            marks[f"wf.{t0}kr"] = (T_, count[T_])
            for nm, n in (("cq", 3), ("ckv", 2)):
                b = bank(pe, f"{t0}s{nm}")
                for m in range(n):
                    if later(pe, f"{t0}q{nm}{m}"):
                        pe.wait_ge(*at(f"{t0}q{nm}{m}"))
                    ins = pe.matmul(b, ones[:, :], TQ[:, m + (3 if nm == "ckv" else 0), :], start=m == 0, stop=m == n - 1)
                did(T_, ins.then_inc(tensor_done, 1), f"{t0}s{nm}")
            w = weight(pe, f"{t0}qb")
            w2 = weight(pe, f"{t0}qs")
            for h in range(6):
                b = bank(pe, f"{t0}q{h}")
                b2 = bank(pe, f"{t0}qw{h}")
                if later(pe, f"{t0}ncq"):
                    pe.wait_ge(*at(f"{t0}ncq"))
                for k in range(3):
                    ins = pe.matmul(b[0:96, :], w[:, k, 96 * h:96 * h + 96], CQ[:, k, :], start=k == 0, stop=k == 2)
                did(T_, ins.then_inc(tensor_done, 1), f"{t0}q{h}")
                for k in range(3):
                    ins = pe.matmul(b2[HR, :], w2[:, k, 32 * h:32 * h + 32], CQ[:, k, :], start=k == 0, stop=k == 2)
                did(T_, ins.then_inc(tensor_done, 1), f"{t0}qw{h}")
            marks[f"wf.{t0}qb"] = (T_, count[T_])
            marks[f"wf.{t0}qs"] = (T_, count[T_])
            w = weight(pe, f"{t0}kvb")
            if later(pe, f"{t0}nckv"):
                pe.wait_ge(*at(f"{t0}nckv"))
            for h in range(6):
                b = bank(pe, f"{t0}k{h}")
                for k in range(2):
                    ins = pe.matmul(b[0:64, :], w[:, k, 128 * h:128 * h + 64], CKV[:, k, :], start=k == 0, stop=k == 1)
                did(T_, ins.then_inc(tensor_done, 1), f"{t0}k{h}")
            for tt in range(4):
                b = bank(pe, f"{t0}vt{tt}")
                for k in range(2):
                    rhs = w[:, k, :].rearrange("p (h s c) -> p h s c", s=2, c=64)[:, :, 1, :]
                    ins = pe.matmul(b[:, 0:384].rearrange("p (h c) -> p h c", c=64), CKV[:, k, tt * P:tt * P + P], rhs,
                                    start=k == 0, stop=k == 1)
                did(T_, ins.then_inc(tensor_done, 1), f"{t0}vt{tt}")
            marks[f"wf.{t0}kvb"] = (T_, count[T_])

            def score(n):
                h, i = ORDER[n]
                if later(pe, f"{t0}qt{h}"):
                    pe.wait_ge(*at(f"{t0}qt{h}"))
                if later(pe, f"{t0}kt{h}"):
                    pe.wait_ge(*at(f"{t0}kt{h}"))
                if later(pe, f"mlac{l}"):
                    pe.wait_ge(*at(f"mlac{l}"))
                b = bank(pe, f"{t0}sc{n}")
                w = (i + 1) * P
                pe.matmul(b[:, 0:w], QT[0:96, h, i * P:i * P + P], KTT[0:96, h, 0:w], start=True, stop=False)
                did(T_, pe.matmul(b[:, i * P:w], ident[:, :], NEG, start=False, stop=True).then_inc(tensor_done, 1), f"{t0}sc{n}")

            def turn(n):
                h, i = ORDER[n]
                if later(pe, f"{t0}pn{n}"):
                    pe.wait_ge(*at(f"{t0}pn{n}"))
                b = bank(pe, f"{t0}pt{n}")
                for j in range(i + 1):
                    ins = pe.transpose(b[:, j * P:j * P + P], PB[:, n % 2, j * P:j * P + P], ident[:, :])
                did(T_, ins.then_inc(tensor_done, 1), f"{t0}pt{n}")

            def value(n):
                h, i = ORDER[n]
                if later(pe, f"free.{t0}pt{n}"):
                    pe.wait_ge(*at(f"free.{t0}pt{n}"))
                if later(pe, f"free.{t0}vt3"):
                    pe.wait_ge(*at(f"free.{t0}vt3"))
                b = bank(pe, f"{t0}o{n}")
                for j in range(i + 1):
                    ins = pe.matmul(b[rows(h % 2), 0:P], VT[:, j, 64 * h:64 * h + 64], PTT[:, n % 2, j * P:j * P + P],
                                    start=j == 0, stop=j == i)
                did(T_, ins.then_inc(tensor_done, 1), f"{t0}o{n}")
            N = len(ORDER)
            for n in range(N + 2):
                if n < N:
                    score(n)
                if 1 <= n <= N:
                    turn(n - 1)
                if n >= 2:
                    value(n - 2)

        def mla_scalar(act, l):
            t0 = f"i{l}."
            for nm, n, o in (("cq", 3, CQ), ("ckv", 2, CKV)):
                for m in range(n):
                    t = tile(act, f"{t0}{nm}{m}")
                    did(A_, act.activation(o[:, m, :], t, ACT.Copy).then_inc(scalar_done, 1), f"{t0}c{nm}{m}")
                    did(A_, act.activation(TQ[:, m + (3 if nm == "ckv" else 0), :], t, ACT.Square).then_inc(scalar_done, 1), f"{t0}q{nm}{m}")
                    marks[f"free.{t0}{nm}{m}"] = (A_, count[A_])
            for nm, n, c in (("cq", 384, 0), ("ckv", 256, 1)):
                t = tile(act, f"{t0}s{nm}")
                did(A_, act.activation(RC[:, c, :], t, ACT.Sqrt, bias=eps[:, 0:1], scale=1.0 / n).then_inc(scalar_done, 1), f"free.{t0}s{nm}")
            for h in range(6):
                t = tile(act, f"{t0}k{h}")
                did(A_, act.activation(KTT[0:64, h, :], t[0:64, :], ACT.Copy).then_inc(scalar_done, 1), f"free.{t0}k{h}")
            for tt in range(4):
                t = tile(act, f"{t0}vt{tt}")
                did(A_, act.activation(VT[:, tt, :], t[:, 0:384], ACT.Copy).then_inc(scalar_done, 1), f"free.{t0}vt{tt}")

            def soft(n):
                h, i = ORDER[n]
                w = (i + 1) * P
                t = tile(act, f"{t0}sc{n}")
                if later(act, f"{t0}mx{n}"):
                    act.wait_ge(*at(f"{t0}mx{n}"))
                if n >= 2:
                    if later(act, f"{t0}pt{n - 2}"):
                        act.wait_ge(*at(f"{t0}pt{n - 2}"))
                did(A_, act.activation(PB[:, n % 2, 0:w], t[:, 0:w], ACT.Exp, bias=AST[:, 1, n:n + 1], scale=SCALE,
                                       accum_out=AST[:, 2, n:n + 1]).then_inc(scalar_done, 1), f"free.{t0}sc{n}")

            def turned(n):
                h, i = ORDER[n]
                w = (i + 1) * P
                t = tile(act, f"{t0}pt{n}")
                if n >= 2:
                    if later(act, f"{t0}o{n - 2}"):
                        act.wait_ge(*at(f"{t0}o{n - 2}"))
                did(A_, act.activation(PTT[:, n % 2, 0:w], t[:, 0:w], ACT.Copy).then_inc(scalar_done, 1), f"free.{t0}pt{n}")
            N = len(ORDER)
            for n in range(N + 1):
                if n < N:
                    soft(n)
                if n >= 1:
                    turned(n - 1)

        def mla_vector(dve, l):
            t0 = f"i{l}."
            if later(dve, f"mlac{l}"):
                dve.wait_ge(*at(f"mlac{l}"))
            for s in range(2):
                t = tile(dve, f"{t0}kr{s}")
                did(V, dve.tensor_tensor(TQ[HR, s, :] if False else KTT[HR, s, :], t[HR, :], TR[HR, s, :], ALU.mult).then_inc(vector_done, 1), f"free.{t0}kr{s}")
            dve.wait_ge(*own(dve, V))
            did(V, dve.tensor_tensor(KW[HR, :], KTT[HR, 0, :], KTT[HR, 1, :], ALU.add).then_inc(vector_done, 1))
            dve.wait_ge(*own(dve, V))
            did(V, dve.tensor_copy(KTT[HR, :, :], KW[HR, :].unsqueeze(1).to_broadcast([32, 6, TX])).then_inc(vector_done, 1))
            for nm, n, c, o, g in (("cq", 3, 0, CQ, "qg"), ("ckv", 2, 1, CKV, "kvg")):
                if later(dve, f"free.{t0}s{nm}"):
                    dve.wait_ge(*at(f"free.{t0}s{nm}"))
                did(V, dve.reciprocal(RC[:, c, :], RC[:, c, :]).then_inc(vector_done, 1))
                dve.wait_ge(*own(dve, V))
                for m in range(n):
                    if later(dve, f"{t0}c{nm}{m}"):
                        dve.wait_ge(*at(f"{t0}c{nm}{m}"))
                    did(V, dve.scalar_tensor_tensor(o[:, m, :], o[:, m, :], col(g, n * l + m), RC[:, c, :],
                                                    ALU.mult, ALU.mult).then_inc(vector_done, 1))
                marks[f"{t0}n{nm}"] = (V, count[V])
            for h in range(6):
                t = tile(dve, f"{t0}q{h}")
                did(V, dve.tensor_copy(QT[0:64, h, :], t[0:64, :]).then_inc(vector_done, 1))
                did(V, dve.tensor_tensor(QT[HR, h, :], t[HR, :], TR[HR, 0, :], ALU.mult).then_inc(vector_done, 1), f"free.{t0}q{h}")
                t = tile(dve, f"{t0}qw{h}")
                if h:
                    dve.wait_ge(*own(dve, V))
                did(V, dve.tensor_tensor(KW[HR, :], t[HR, :], TR[HR, 1, :], ALU.mult).then_inc(vector_done, 1), f"free.{t0}qw{h}")
                dve.wait_ge(*own(dve, V))
                did(V, dve.tensor_tensor(QT[HR, h, :], QT[HR, h, :], KW[HR, :], ALU.add).then_inc(vector_done, 1), f"{t0}qt{h}")
            for h in range(6):
                marks[f"{t0}kt{h}"] = (A_, 0)
            N = len(ORDER)

            def mx(n):
                h, i = ORDER[n]
                w = (i + 1) * P
                t = tile(dve, f"{t0}sc{n}")
                did(V, dve.tensor_reduce(AST[:, 0, n:n + 1], t[:, 0:w], AX, ALU.max).then_inc(vector_done, 1))
                dve.wait_ge(*own(dve, V))
                did(V, dve.tensor_scalar(AST[:, 1, n:n + 1], AST[:, 0, n:n + 1], -SCALE, None, ALU.mult).then_inc(vector_done, 1), f"{t0}mx{n}")

            def norm(n):
                h, i = ORDER[n]
                w = (i + 1) * P
                if later(dve, f"free.{t0}sc{n}"):
                    dve.wait_ge(*at(f"free.{t0}sc{n}"))
                did(V, dve.reciprocal(AST[:, 3, n:n + 1], AST[:, 2, n:n + 1]).then_inc(vector_done, 1))
                dve.wait_ge(*own(dve, V))
                did(V, dve.tensor_scalar(PB[:, n % 2, 0:w], PB[:, n % 2, 0:w], AST[:, 3, n:n + 1], None, ALU.mult).then_inc(vector_done, 1), f"{t0}pn{n}")

            def outv(n):
                h, i = ORDER[n]
                t = tile(dve, f"{t0}o{n}")
                did(V, dve.tensor_copy(MIX[rows(h % 2), 5 + h // 2, i * P:i * P + P], t[rows(h % 2), 0:P]).then_inc(vector_done, 1), f"free.{t0}o{n}")
            for n in range(N + 2):
                if n < N:
                    mx(n)
                    norm(n)
                if n >= 2:
                    outv(n - 2)

        UU = S(4096, 2, TX)
        VG = S(5120, 4, 256)
        VN = S(6144, 4, 256)
        WST = S(7168, 4, P)
        GBC = S(7680, 256)
        GB = S(7936, 2, P)
        CAUS = S(8192, P)
        VS = S(8320, 2, 4)
        GSQ = S(8328, 256)

        def gmlp_pool(pool, l):
            did("aux", pool.dma_start(WST, a["wsT"][l].rearrange("h s t -> s h t")).then_inc(constants_in, 16), by=16)
            did("aux", pool.dma_start(GBC, a["vng"][l]).then_inc(constants_in, 16), by=16)
            did("aux", pool.dma_start(GB, a["gbs"][l].rearrange("p (m t) -> p m t", t=P)).then_inc(constants_in, 16), by=16)
            did("aux", pool.dma_start(CAUS, a["caus"]).then_inc(constants_in, 16), f"gmc{l}", by=16)

        def gmlp_tensor(pe, l):
            t0 = f"i{l}."
            w = weight(pe, f"{t0}v")
            for tt in range(4):
                b = bank(pe, f"{t0}gv{tt}")
                for k in range(KT):
                    ins = pe.matmul(b[:, 0:256], H[:, k, tt * P:tt * P + P], w[:, k, :], start=k == 0, stop=k == KT - 1)
                did(T_, ins.then_inc(tensor_done, 1), f"{t0}gv{tt}")
            marks[f"wf.{t0}v"] = (T_, count[T_])
            w = weight(pe, f"{t0}u")
            for m in range(2):
                b = bank(pe, f"{t0}gu{m}")
                for k in range(KT):
                    ins = pe.matmul(b, w[:, k, m * P:m * P + P], H[:, k, 0:TX], start=k == 0, stop=k == KT - 1)
                did(T_, ins.then_inc(tensor_done, 1), f"{t0}gu{m}")
            marks[f"wf.{t0}u"] = (T_, count[T_])
            if later(pe, f"{t0}wst"):
                pe.wait_ge(*at(f"{t0}wst"))
            if later(pe, f"{t0}vn"):
                pe.wait_ge(*at(f"{t0}vn"))
            for m in range(2):
                b = bank(pe, f"{t0}gm{m}")
                for q in range(2):
                    h = 2 * m + q
                    for c in range(4):
                        ins = pe.matmul(b[rows(q), c * P:c * P + P], VN[:, c, 64 * h:64 * h + 64], WST[:, h, :],
                                        start=True, stop=True)
                did(T_, ins.then_inc(tensor_done, 1), f"{t0}gm{m}")

        def gmlp_scalar(act, l):
            t0 = f"i{l}."
            for tt in range(4):
                t = tile(act, f"{t0}gv{tt}")
                did(A_, act.activation(VG[:, tt, :], t[:, 0:256], ACT.Gelu_apprx_tanh).then_inc(scalar_done, 1), f"free.{t0}gv{tt}")
            for m in range(2):
                t = tile(act, f"{t0}gu{m}")
                did(A_, act.activation(UU[:, m, :], t, ACT.Gelu_apprx_tanh).then_inc(scalar_done, 1), f"free.{t0}gu{m}")
            if later(act, f"{t0}vs"):
                act.wait_ge(*at(f"{t0}vs"))
            did(A_, act.activation(VS[:, 1, :], VS[:, 0, :], ACT.Sqrt, bias=eps[:, 0:1], scale=1.0 / 256).then_inc(scalar_done, 1), f"{t0}vsq")

        def gmlp_vector(dve, l):
            t0 = f"i{l}."
            if later(dve, f"gmc{l}"):
                dve.wait_ge(*at(f"gmc{l}"))
            did(V, dve.tensor_tensor(WST[:, :, :], WST[:, :, :], CAUS.unsqueeze(1).to_broadcast([P, 4, P]), ALU.mult).then_inc(vector_done, 1), f"{t0}wst")
            for tt in range(4):
                if later(dve, f"free.{t0}gv{tt}"):
                    dve.wait_ge(*at(f"free.{t0}gv{tt}"))
                if tt:
                    dve.wait_ge(*own(dve, V))
                did(V, dve.scalar_tensor_tensor(GSQ, VG[:, tt, :], 1.0, VG[:, tt, :], ALU.mult, ALU.mult,
                                                accum_out=VS[:, 0, tt:tt + 1]).then_inc(vector_done, 1))
            marks[f"{t0}vs"] = (V, count[V])
            if later(dve, f"{t0}vsq"):
                dve.wait_ge(*at(f"{t0}vsq"))
            did(V, dve.reciprocal(VS[:, 1, :], VS[:, 1, :]).then_inc(vector_done, 1))
            dve.wait_ge(*own(dve, V))
            for tt in range(4):
                did(V, dve.scalar_tensor_tensor(VN[:, tt, :], VG[:, tt, :], VS[:, 1, tt:tt + 1], GBC, ALU.mult, ALU.mult).then_inc(vector_done, 1))
            marks[f"{t0}vn"] = (V, count[V])
            for m in range(2):
                t = tile(dve, f"{t0}gm{m}").rearrange("p (c t) -> p c t", t=P)
                mm = MIX[:, m, :].rearrange("p (c t) -> p c t", t=P)
                did(V, dve.tensor_tensor(mm, t, GB[:, m, :].unsqueeze(1).to_broadcast([P, 4, P]), ALU.add).then_inc(vector_done, 1), f"free.{t0}gm{m}")
                dve.wait_ge(*own(dve, V))
                if later(dve, f"free.{t0}gu{m}"):
                    dve.wait_ge(*at(f"free.{t0}gu{m}"))
                did(V, dve.tensor_tensor(MIX[:, m, :], MIX[:, m, :], UU[:, m, :], ALU.mult).then_inc(vector_done, 1))

        SZ = S(4096, 3, TX)
        RAW = S(5632, 5, TX)
        XBC = S(8192, 5, TX)
        TOK = S(10752, 4, 512)
        XW = S(12800, 24, 64)
        ABS = S(14336, 6, TX)
        WW = S(17408, 6, TX)
        RG = S(17408, 2, TX)
        YQ = S(18432, 3, TX)
        CB = S(20480, 2, 512)
        HS = S(12800, 4, 192)
        DTW = [scr[0:6, 5632 + 512 * n:6144 + 512 * n] for n in range(5)]
        SEL6 = scr[0:6, 8192 - 2560:8192 - 2560 + 768]
        AC2 = S(21504, 2, 24)
        DEC = S(21552, 2, 24)
        STT_ = S(21600, 192)
        SM6 = small[0:6, 64:68]
        CAU2 = S(21792, P)
        SE = S(5632 + 2560 - 1024, 2, 512)

        def ssd_pool(pool, l):
            did("aux", pool.dma_start(SM6, a["sm6"]).then_inc(constants_in, 16), by=16)
            did("aux", pool.dma_start(CAU2, a["caus"]).then_inc(constants_in, 16), by=16)
            did("aux", pool.dma_start(small[0:6, 72:74], a["sm6"][:, 0:2]).then_inc(constants_in, 16), f"ssc{l}", by=16)
            if later(pool, f"i{l}.sdt"):
                pool.wait_ge(*at(f"i{l}.sdt"))
            did("aux", pool.dma_start(H[0:6, 0, 0:768], a["sel6"]).then_inc(constants_in, 16), by=16)
            did("aux", pool.dma_start(H[0:6, 1, 0:512], a["rst128"]).then_inc(constants_in, 16), f"ssd2{l}", by=16)

        HF = H[:, :, :].rearrange("p k t -> p (k t)")
        DT = [HF[0:6, 2 * TA + 512 * n:2 * TA + 512 * n + 512] for n in range(5)]
        SELH = HF[0:6, 0:768].rearrange("p (h c) -> p h c", c=P)
        RS6 = HF[0:6, TA:TA + 512]
        SEH = HF[:, 5120:6144].rearrange("p (b n) -> p b n", b=2)

        def ssd_tensor(pe, l):
            t0 = f"i{l}."
            w = weight(pe, f"{t0}dt")
            b = bank(pe, f"{t0}dt")
            for k in range(KT):
                ins = pe.matmul(b[0:6, :], w[:, k, :], H[:, k, 0:TX], start=k == 0, stop=k == KT - 1)
            did(T_, ins.then_inc(tensor_done, 1), f"{t0}dt")
            marks[f"wf.{t0}dt"] = (T_, count[T_])
            for nm, n in (("xbc", 5), ("z", 3)):
                for m in range(n):
                    w = weight(pe, f"{t0}{nm}.{m // 2}")
                    b = bank(pe, f"{t0}{nm}{m}")
                    for k in range(KT):
                        ins = pe.matmul(b, w[:, k, (m % 2) * P:(m % 2) * P + P], H[:, k, 0:TX], start=k == 0, stop=k == KT - 1)
                    did(T_, ins.then_inc(tensor_done, 1), f"{t0}{nm}{m}")
                    if m % 2 or m == n - 1:
                        marks[f"wf.{t0}{nm}.{m // 2}"] = (T_, count[T_])
            marks[f"{t0}sdt"] = (T_, count[T_])
            if later(pe, f"ssd2{l}"):
                pe.wait_ge(*at(f"ssd2{l}"))
            if later(pe, f"{t0}ac"):
                pe.wait_ge(*at(f"{t0}ac"))
            for h in range(6):
                b = bank(pe, f"{t0}ab{h}")
                did(T_, pe.matmul(b, SELH[:, h, :], DT[4], start=True, stop=True).then_inc(tensor_done, 1), f"{t0}ab{h}")
            b = bank(pe, f"{t0}tk")
            for n, src in enumerate((DT[4], DT[3])):
                for c in range(4):
                    o = 24 * n + 6 * c
                    ins = pe.transpose(b[:, o:o + 6], src[:, c * P:c * P + P], ident[0:6, 0:6])
            did(T_, ins.then_inc(tensor_done, 1), f"{t0}tk")
            for c in range(4):
                b = bank(pe, f"{t0}tok{c}")
                for m in range(4):
                    if later(pe, f"{t0}xc{m}"):
                        pe.wait_ge(*at(f"{t0}xc{m}"))
                    ins = pe.transpose(b[:, m * P:m * P + P], XBC[:, m, c * P:c * P + P], ident[:, :])
                did(T_, ins.then_inc(tensor_done, 1), f"{t0}tok{c}")
            if later(pe, f"{t0}xc4"):
                pe.wait_ge(*at(f"{t0}xc4"))
            for g in range(2):
                b = bank(pe, f"{t0}cb{g}")
                for c in range(4):
                    ins = pe.matmul(b[:, c * P:c * P + P], XBC[rows(g), 3, c * P:c * P + P], XBC[rows(g), 4, c * P:c * P + P],
                                    start=True, stop=True)
                did(T_, ins.then_inc(tensor_done, 1), f"{t0}cb{g}")
            for c in range(4):
                b = bank(pe, f"{t0}st{c}")
                if later(pe, f"{t0}xw"):
                    pe.wait_ge(*at(f"{t0}xw"))
                for g in range(2):
                    ins = pe.matmul(b[rows(g), 0:192], TOK[:, c, 384 + 64 * g:448 + 64 * g], XW[:, 6 * c + 3 * g:6 * c + 3 * g + 3, :],
                                    start=True, stop=True)
                did(T_, ins.then_inc(tensor_done, 1), f"{t0}st{c}")
            for m in range(3):
                b = bank(pe, f"{t0}ya{m}")
                for q in range(2):
                    h = 2 * m + q
                    if later(pe, f"{t0}w{h}"):
                        pe.wait_ge(*at(f"{t0}w{h}"))
                    for c in range(4):
                        ins = pe.matmul(b[rows(q), c * P:c * P + P], TOK[:, c, 64 * h:64 * h + 64], WW[:, h, c * P:c * P + P],
                                        start=True, stop=True)
                did(T_, ins.then_inc(tensor_done, 1), f"{t0}ya{m}")
                b = bank(pe, f"{t0}yo{m}")
                if later(pe, f"{t0}hs"):
                    pe.wait_ge(*at(f"{t0}hs"))
                for q in range(2):
                    h = 2 * m + q
                    g = h // 3
                    for c in range(4):
                        ins = pe.matmul(b[rows(q), c * P:c * P + P], HS[rows(g), c, 64 * (h % 3):64 * (h % 3) + 64],
                                        XBC[rows(g), 4, c * P:c * P + P], start=True, stop=True)
                did(T_, ins.then_inc(tensor_done, 1), f"{t0}yo{m}")
            if later(pe, f"{t0}yq"):
                pe.wait_ge(*at(f"{t0}yq"))
            b = bank(pe, f"{t0}sg0")
            pe.matmul(b, ones[:, :], YQ[:, 0, :], start=True, stop=False)
            did(T_, pe.matmul(b, ones[0:64, :], YQ[0:64, 1, :], start=False, stop=True).then_inc(tensor_done, 1), f"{t0}sg0")
            b = bank(pe, f"{t0}sg1")
            pe.matmul(b, ones[:, :], YQ[:, 2, :], start=True, stop=False)
            did(T_, pe.matmul(b, ones[64:128, :], YQ[64:128, 1, :], start=False, stop=True).then_inc(tensor_done, 1), f"{t0}sg1")

        def ssd_scalar(act, l):
            t0 = f"i{l}."
            if later(act, f"{t0}ady"):
                act.wait_ge(*at(f"{t0}ady"))
            did(A_, act.activation(DTB(l)[1], DTB(l)[1], ACT.Exp, scale=-1.0).then_inc(scalar_done, 1))
            act.wait_ge(*own(act, A_))
            did(A_, act.activation(DTB(l)[1], DTB(l)[1], ACT.Ln, bias=1.0).then_inc(scalar_done, 1))
            if later(act, f"ssc{l}"):
                act.wait_ge(*at(f"ssc{l}"))
            did(A_, act.activation(small[0:6, 70:71], SM6[:, 2 + l:3 + l], ACT.Exp).then_inc(scalar_done, 1), f"{t0}ln")
            for m in range(5):
                if later(act, f"{t0}cv{m}"):
                    act.wait_ge(*at(f"{t0}cv{m}"))
                did(A_, act.activation(XBC[:, m, :], XBC[:, m, :], ACT.Silu).then_inc(scalar_done, 1), f"{t0}xc{m}")
            for m in range(3):
                t = tile(act, f"{t0}z{m}")
                did(A_, act.activation(SZ[:, m, :], t, ACT.Silu).then_inc(scalar_done, 1), f"free.{t0}z{m}")
            for h in range(6):
                t = tile(act, f"{t0}ab{h}")
                did(A_, act.activation(ABS[:, h, :], t, ACT.Copy).then_inc(scalar_done, 1), f"free.{t0}ab{h}")
            for c in range(4):
                t = tile(act, f"{t0}tok{c}")
                did(A_, act.activation(TOK[:, c, :], t, ACT.Copy).then_inc(scalar_done, 1), f"free.{t0}tok{c}")
            if later(act, f"{t0}dc"):
                act.wait_ge(*at(f"{t0}dc"))
            did(A_, act.activation(DEC[:, :, :], DEC[:, :, :], ACT.Exp).then_inc(scalar_done, 1), f"{t0}dce")
            for h in range(6):
                if later(act, f"{t0}sg_{h}"):
                    act.wait_ge(*at(f"{t0}sg_{h}"))
                if h >= 2:
                    if later(act, f"{t0}w{h - 2}"):
                        act.wait_ge(*at(f"{t0}w{h - 2}"))
                did(A_, act.activation(SEH[:, h % 2, :], WW[:, h, :], ACT.Exp).then_inc(scalar_done, 1), f"{t0}se{h}")
            for h in range(6):
                did(A_, act.activation(ABS[:, h, :], ABS[:, h, :], ACT.Exp).then_inc(scalar_done, 1), f"{t0}ea{h}")
            for g in range(2):
                t = tile(act, f"{t0}sg{g}")
                did(A_, act.activation(RG[:, g, :], t, ACT.Sqrt, bias=eps[:, 0:1], scale=1.0 / 192).then_inc(scalar_done, 1), f"free.{t0}sg{g}")

        def DTB(l):
            return [scr[0:6, 17408 + 512 * n:17920 + 512 * n] for n in range(2)]

        def ssd_vector(dve, l):
            t0 = f"i{l}."
            y0, y1 = DTB(l)
            if later(dve, f"ssc{l}"):
                dve.wait_ge(*at(f"ssc{l}"))
            t = tile(dve, f"{t0}dt")
            did(V, dve.tensor_scalar(y0, t[0:6, :], SM6[:, l:l + 1], None, ALU.add).then_inc(vector_done, 1), f"free.{t0}dt")
            dve.wait_ge(*own(dve, V))
            did(V, dve.scalar_tensor_tensor(y1, y0, -1.0, y0, ALU.mult, ALU.max).then_inc(vector_done, 1), f"{t0}ady")
            for m in range(5):
                t = tile(dve, f"{t0}xbc{m}")
                did(V, dve.tensor_copy(RAW[:, m, :], t).then_inc(vector_done, 1), f"free.{t0}xbc{m}")
                dve.wait_ge(*own(dve, V))
                cw = [col("convw", 20 * l + 5 * j + m) for j in range(4)]
                did(V, dve.tensor_scalar(XBC[:, m, :], RAW[:, m, :], cw[3], col("convb", 5 * l + m), ALU.mult, ALU.add).then_inc(vector_done, 1))
                for j in (2, 1, 0):
                    s = 3 - j
                    dve.wait_ge(*own(dve, V))
                    did(V, dve.scalar_tensor_tensor(XBC[:, m, s:TX], RAW[:, m, 0:TX - s], cw[j], XBC[:, m, s:TX],
                                                    ALU.mult, ALU.add).then_inc(vector_done, 1))
                marks[f"{t0}cv{m}"] = (V, count[V])
            if later(dve, f"{t0}ln"):
                dve.wait_ge(*at(f"{t0}ln"))
            if later(dve, f"{t0}sdt"):
                dve.wait_ge(*at(f"{t0}sdt"))
            if later(dve, f"ssd2{l}"):
                dve.wait_ge(*at(f"ssd2{l}"))
            did(V, dve.scalar_tensor_tensor(DT[3], y0, 0.0, y1, ALU.max, ALU.add).then_inc(vector_done, 1))
            dve.wait_ge(*own(dve, V))
            did(V, dve.tensor_scalar(DT[0], DT[3], small[0:6, 70:71], -1.0, ALU.mult, ALU.mult).then_inc(vector_done, 1))
            dve.wait_ge(*own(dve, V))
            did(V, dve.tensor_tensor_scan(DT[4], RS6, DT[0], 0.0, ALU.mult, ALU.add).then_inc(vector_done, 1), f"{t0}ac")
            t = tile(dve, f"{t0}tk")
            did(V, dve.tensor_copy(AC2[:, :, :], t[:, 0:48].rearrange("p (n c) -> p n c", n=2)).then_inc(vector_done, 1), f"free.{t0}tk")
            for step in [f"free.{t0}ab{h}" for h in range(6)]:
                if later(dve, step):
                    dve.wait_ge(*at(step))
            dve.wait_ge(*own(dve, V))
            ends = ABS[:, :, :].rearrange("p h (c t) -> p c h t", t=P)[:, :, :, P - 1]
            a2 = AC2[:, 0, :].rearrange("p (c h) -> p c h", h=6)
            did(V, dve.tensor_tensor(DEC[:, 0, :].rearrange("p (c h) -> p c h", h=6), ends, a2, ALU.subtract).then_inc(vector_done, 1))
            did(V, dve.tensor_copy(DEC[:, 1, :].rearrange("p (c h) -> p c h", h=6), ends).then_inc(vector_done, 1), f"{t0}dc")
            for g in range(2):
                t = tile(dve, f"{t0}cb{g}")
                did(V, dve.tensor_tensor(CB[:, g, :].rearrange("p (c t) -> p c t", t=P), t.rearrange("p (c t) -> p c t", t=P),
                                         CAU2.unsqueeze(1).to_broadcast([P, 4, P]), ALU.mult).then_inc(vector_done, 1), f"free.{t0}cb{g}")
            if later(dve, f"{t0}dce"):
                dve.wait_ge(*at(f"{t0}dce"))
            did(V, dve.tensor_tensor(DEC[:, 0, :], DEC[:, 0, :], AC2[:, 1, :], ALU.mult).then_inc(vector_done, 1))
            dve.wait_ge(*own(dve, V))
            if later(dve, f"free.{t0}tok3"):
                dve.wait_ge(*at(f"free.{t0}tok3"))
            for c in range(4):
                did(V, dve.tensor_tensor(XW[:, 6 * c:6 * c + 6, :], TOK[:, c, 0:384].rearrange("p (h c) -> p h c", c=64),
                                         DEC[:, 0, 6 * c:6 * c + 6].unsqueeze(2).to_broadcast([P, 6, 64]), ALU.mult).then_inc(vector_done, 1))
            marks[f"{t0}xw"] = (V, count[V])
            for h in range(6):
                for c in range(4):
                    did(V, dve.tensor_scalar(WW[:, h, c * P:c * P + P], ABS[:, h, c * P:c * P + P],
                                             AC2[:, 0, 6 * c + h:6 * c + h + 1], 0.0, ALU.subtract, ALU.min).then_inc(vector_done, 1))
                marks[f"{t0}sg_{h}"] = (V, count[V])
            for h in range(6):
                if later(dve, f"{t0}se{h}"):
                    dve.wait_ge(*at(f"{t0}se{h}"))
                for c in range(4):
                    did(V, dve.scalar_tensor_tensor(WW[:, h, c * P:c * P + P], CB[:, h // 3, c * P:c * P + P],
                                                    AC2[:, 1, 6 * c + h:6 * c + h + 1], SEH[:, h % 2, c * P:c * P + P],
                                                    ALU.mult, ALU.mult).then_inc(vector_done, 1))
                marks[f"{t0}w{h}"] = (V, count[V])
            if later(dve, f"{t0}st3"):
                dve.wait_ge(*at(f"{t0}st3"))
            did(V, dve.memset(HS[:, 0, :], 0.0).then_inc(vector_done, 1))
            dve.wait_ge(*own(dve, V))
            for c in range(4):
                t = tile(dve, f"{t0}st{c}")
                if c == 3:
                    did(V, dve.tensor_copy(STT_[:, 0:1], t[:, 0:1]).then_inc(vector_done, 1), f"free.{t0}st{c}")
                    continue
                for g in range(2):
                    dd = DEC[rows(g), 1, 6 * c + 3 * g:6 * c + 3 * g + 3].unsqueeze(2).to_broadcast([64, 3, 64])
                    did(V, dve.tensor_tensor(STT_[rows(g), :].rearrange("p (h c) -> p h c", c=64),
                                             HS[rows(g), c, :].rearrange("p (h c) -> p h c", c=64), dd, ALU.mult).then_inc(vector_done, 1))
                dve.wait_ge(*own(dve, V))
                did(V, dve.tensor_tensor(HS[:, c + 1, :], t[:, 0:192], STT_, ALU.add).then_inc(vector_done, 1), f"free.{t0}st{c}")
                dve.wait_ge(*own(dve, V))
            marks[f"{t0}hs"] = (V, count[V])
            for m in range(3):
                to = tile(dve, f"{t0}yo{m}")
                ta = tile(dve, f"{t0}ya{m}")
                y = MIX[:, 2 + m, :]
                for q in range(2):
                    if later(dve, f"{t0}ea{2 * m + q}"):
                        dve.wait_ge(*at(f"{t0}ea{2 * m + q}"))
                    did(V, dve.tensor_tensor(MIX[rows(q), 2 + m, :], to[rows(q), :], ABS[rows(q), 2 * m + q, :], ALU.mult).then_inc(vector_done, 1))
                marks[f"free.{t0}yo{m}"] = (V, count[V])
                dve.wait_ge(*own(dve, V))
                did(V, dve.tensor_tensor(y, ta, y, ALU.add).then_inc(vector_done, 1), f"free.{t0}ya{m}")
                dve.wait_ge(*own(dve, V))
                did(V, dve.scalar_tensor_tensor(y, XBC[:, m, :], col("ssdd", 3 * l + m), y, ALU.mult, ALU.add).then_inc(vector_done, 1))
                dve.wait_ge(*own(dve, V))
                did(V, dve.tensor_tensor(y, y, SZ[:, m, :], ALU.mult).then_inc(vector_done, 1), f"{t0}yg{m}")
            if later(dve, f"{t0}yo2"):
                dve.wait_ge(*at(f"{t0}yo2"))
            dve.wait_ge(*own(dve, V))
            for m in range(3):
                did(V, dve.tensor_tensor(YQ[:, m, :], MIX[:, 2 + m, :], MIX[:, 2 + m, :], ALU.mult).then_inc(vector_done, 1))
            marks[f"{t0}yq"] = (V, count[V])
            if later(dve, f"free.{t0}sg0"):
                dve.wait_ge(*at(f"free.{t0}sg0"))
            if later(dve, f"free.{t0}sg1"):
                dve.wait_ge(*at(f"free.{t0}sg1"))
            did(V, dve.reciprocal(RG[:, :, :], RG[:, :, :]).then_inc(vector_done, 1))
            dve.wait_ge(*own(dve, V))
            for m, rr, g in ((0, slice(0, P), 0), (1, rows(0), 0), (1, rows(1), 1), (2, slice(0, P), 1)):
                did(V, dve.scalar_tensor_tensor(MIX[rr, 2 + m, :], MIX[rr, 2 + m, :],
                                                vec[rr, VEC["ssdg"] + 3 * l + m:VEC["ssdg"] + 3 * l + m + 1],
                                                RG[rr, g, :], ALU.mult, ALU.mult).then_inc(vector_done, 1))
            marks[f"{t0}mix"] = (V, count[V])

        HB = S(0, 32, TX)
        RL = S(16384, 2, TX)

        def mlp_tensor(pe, l):
            t0 = f"i{l}."
            linear_tensor(pe, f"{t0}m1", f"{t0}m1", lambda k, s0, sn: H[:, k, s0:s0 + sn], XSEG,
                          lambda k: f"n3{l}.h{k}", mtiles=32)
            for n in range(2):
                banks = [bank(pe, f"{t0}m2.{4 * n + m}.0") for m in range(4)]
                for r in range(8):
                    w = weight(pe, f"{t0}m2.{n}.{r}")
                    for m in range(4):
                        for f in range(4):
                            if later(pe, f"{t0}hb{4 * r + f}"):
                                pe.wait_ge(*at(f"{t0}hb{4 * r + f}"))
                            ins = pe.matmul(banks[m], w[:, f, m * P:m * P + P], HB[:, 4 * r + f, :],
                                            start=r == 0 and f == 0, stop=r == 7 and f == 3)
                        if r == 7:
                            did(T_, ins.then_inc(tensor_done, 1), f"{t0}m2.{4 * n + m}.0")
                    if r < 7:
                        did(T_, ins.then_inc(tensor_done, 1))
                    marks[f"wf.{t0}m2.{n}.{r}"] = (T_, count[T_])

        def mlp_scalar(act, l):
            t0 = f"i{l}."
            for f in range(32):
                t = tile(act, f"{t0}m1.{f}.0")
                if f >= 2:
                    if later(act, f"{t0}hb{f - 2}"):
                        act.wait_ge(*at(f"{t0}hb{f - 2}"))
                did(A_, act.activation(RL[:, f % 2, :], t, ACT.Relu).then_inc(scalar_done, 1), f"free.{t0}m1.{f}.0")

        def mlp_vector(dve, l):
            t0 = f"i{l}."
            for f in range(32):
                if later(dve, f"free.{t0}m1.{f}.0"):
                    dve.wait_ge(*at(f"free.{t0}m1.{f}.0"))
                did(V, dve.tensor_tensor(HB[:, f, :], RL[:, f % 2, :], RL[:, f % 2, :], ALU.mult).then_inc(vector_done, 1), f"{t0}hb{f}")
            residual_vector(dve, f"{t0}m2", XSEG)

        def stages():
            names = ["ada0", "n0", "fnet", "m0", "moe0", "ada1", "n1", "rw", "wkv", "post", "m1", "moe1", "fg"]
            for l in range(2):
                names += [f"n2{l}", f"mla{l}", f"gmlp{l}", f"ssd{l}", f"wout{l}", f"n3{l}", f"mlp{l}"]
            names = names[:names.index(STOP) + 1] if STOP else names
            return names + ["end"]

        def vgain(name, i):
            return lambda s, k: col(name, 8 * i + k)

        def again(n):
            return lambda s, k: gsc[:, n, k, s:s + 1]

        @block.tensor
        def _(pe):
            if later(pe, "const"):
                pe.wait_ge(*at("const"))
            for st in stages():
                if st in ("ada0", "ada1"):
                    ada_tensor(pe, int(st[3]))
                elif st in ("n0", "m0", "n1"):
                    norm_tensor(pe, st, SEGS)
                elif st == "m1" or st == "fg" or st[:2] in ("n2", "n3") or st == "end":
                    norm_tensor(pe, st, XSEG)
                elif st == "fnet":
                    fnet_tensor(pe)
                elif st[:3] == "moe":
                    moe_tensor(pe, int(st[3]))
                elif st == "rw":
                    rw_tensor(pe)
                elif st == "wkv":
                    wkv_tensor(pe)
                elif st == "post":
                    post_tensor(pe)
                elif st[:3] == "mla":
                    mla_tensor(pe, int(st[3]))
                elif st[:4] == "gmlp":
                    gmlp_tensor(pe, int(st[4]))
                elif st[:3] == "ssd":
                    ssd_tensor(pe, int(st[3]))
                elif st[:4] == "wout":
                    l = int(st[4])
                    linear_tensor(pe, f"wo{l}", f"i{l}.wout", lambda k, s0, sn: MIX[:, k, s0:s0 + sn], XSEG,
                                  lambda k: f"i{l}.mix")
                elif st[:3] == "mlp":
                    mlp_tensor(pe, int(st[3]))
                if st not in ("ada0", "ada1", "end"):
                    phase(pe, T_, st)

        @block.vector
        def _(dve):
            did(V, dve.memset(csil[:, :, :], 0.0).then_inc(vector_done, 1))
            did(V, dve.memset(ones[:, :], 1.0).then_inc(vector_done, 1))
            did(V, dve.memset(eps[:, 0:1], 1e-6).then_inc(vector_done, 1))
            did(V, dve.memset(eps[:, 1:2], 64e-5).then_inc(vector_done, 1))
            did(V, dve.memset(eps[:, 2:3], 1e-12).then_inc(vector_done, 1), "eps")
            if later(dve, "const"):
                dve.wait_ge(*at("const"))
            did(V, dve.tensor_scalar(small[:, 32:40], vec[:, VEC["ka"]:VEC["ka"] + 8], -1.0, 1.0, ALU.mult, ALU.add).then_inc(vector_done, 1))
            for st in stages():
                if st in ("ada0", "ada1"):
                    ada_vector(dve, int(st[3]))
                elif st in ("n0", "m0", "n1"):
                    norm_vector(dve, st, SEGS, again(0 if st[0] == "n" else 1), True)
                elif st == "m1":
                    norm_vector(dve, st, XSEG, again(1), True)
                elif st == "fg":
                    norm_vector(dve, st, XSEG, vgain("final_g", 0), False)
                    dve.wait_ge(*own(dve, V))
                    for k in range(KT):
                        did(V, dve.tensor_copy(X[:, k, 0:TX], H[:, k, 0:TX]).then_inc(vector_done, 1))
                elif st[:2] == "n2":
                    norm_vector(dve, st, XSEG, vgain("nmix", int(st[2])), False)
                elif st[:2] == "n3":
                    norm_vector(dve, st, XSEG, vgain("nmlp", int(st[2])), False)
                elif st == "end":
                    if STOP is None:
                        norm_vector(dve, st, XSEG, vgain("fin2", 0), False)
                    else:
                        if later(dve, "end.sq7"):
                            dve.wait_ge(*at("end.sq7"))
                        if later(dve, "end.ss0"):
                            dve.wait_ge(*at("end.ss0"))
                        did(V, dve.tensor_copy(H[:, :, 0:TX], X[:, :, 0:TX]).then_inc(vector_done, 1))
                    marks["final"] = (V, count[V])
                elif st == "fnet":
                    fnet_vector(dve)
                elif st[:3] == "moe":
                    moe_vector(dve, int(st[3]))
                elif st == "rw":
                    rw_vector(dve)
                elif st == "wkv":
                    wkv_vector(dve)
                elif st == "post":
                    post_vector(dve)
                elif st[:3] == "mla":
                    mla_vector(dve, int(st[3]))
                elif st[:4] == "gmlp":
                    gmlp_vector(dve, int(st[4]))
                elif st[:3] == "ssd":
                    ssd_vector(dve, int(st[3]))
                elif st[:4] == "wout":
                    residual_vector(dve, f"wo{st[4]}", XSEG)
                elif st[:3] == "mlp":
                    mlp_vector(dve, int(st[3]))
                if st not in ("ada0", "ada1", "end"):
                    phase(dve, V, st)
                    dve.wait_ge(*own(dve, V))

        @block.scalar
        def _(act):
            if later(act, "const"):
                act.wait_ge(*at("const"))
            if later(act, "eps"):
                act.wait_ge(*at("eps"))
            did(A_, act.activation(csil[:, :, 0:2], vec[:, VEC["c"]:VEC["c"] + 16].rearrange("p (k c) -> p k c", c=2),
                                   ACT.Silu).then_inc(scalar_done, 1), "csil")
            for st in stages():
                if st in ("n0", "m0", "n1"):
                    norm_scalar(act, st, SEGS, KT, (0,) if st[0] == "n" else (24,))
                elif st == "m1":
                    norm_scalar(act, st, XSEG, KT, (24,))
                elif st == "fg" or st[:2] in ("n2", "n3") or st == "end":
                    norm_scalar(act, st, XSEG, KT, None)
                elif st == "fnet":
                    fnet_scalar(act)
                elif st[:3] == "moe":
                    moe_scalar(act, int(st[3]))
                elif st == "rw":
                    rw_scalar(act)
                elif st == "wkv":
                    wkv_scalar(act)
                elif st == "post":
                    post_scalar(act)
                elif st[:3] == "mla":
                    mla_scalar(act, int(st[3]))
                elif st[:4] == "gmlp":
                    gmlp_scalar(act, int(st[4]))
                elif st[:3] == "ssd":
                    ssd_scalar(act, int(st[3]))
                elif st[:3] == "mlp":
                    mlp_scalar(act, int(st[3]))
                if st not in ("ada0", "ada1", "end"):
                    phase(act, A_, st)
                    act.wait_ge(*own(act, A_))

        @block.gpsimd
        def _(pool):
            for st in stages():
                if st[:3] == "moe":
                    moe_pool(pool, int(st[3]))
                elif st == "rw":
                    rw_pool(pool)
                elif st == "wkv":
                    wkv_pool(pool)
                elif st == "post":
                    post_pool(pool)
                elif st[:3] == "mla":
                    mla_pool(pool, int(st[3]))
                elif st[:4] == "gmlp":
                    gmlp_pool(pool, int(st[4]))
                elif st[:3] == "ssd":
                    ssd_pool(pool, int(st[3]))
                if st not in ("ada0", "ada1", "end"):
                    phase(pool, G_, st)
                    if count[G_]:
                        pool.wait_ge(*own(pool, G_))
    return marks


def feature_cols(v):
    v = np.asarray(v)
    v = v.reshape(-1, v.shape[-1] // P, P)
    return v.transpose(2, 0, 1).reshape(P, -1)


def constants():
    f = np.float32
    c = {}

    def dft(n):
        ang = 2 * np.pi * (np.outer(np.arange(n), np.arange(n)) % n) / n
        return np.cos(ang) / np.sqrt(n), np.sin(ang) / np.sqrt(n)
    cs, sn = dft(256)
    c["dftC"] = np.concatenate([cs, sn], 1)
    c["dftTc"] = np.concatenate([cs, -sn], 1)
    cs, sn = dft(TX)
    c["dftT"] = np.concatenate([cs, -sn], 1)
    c["ident"] = np.eye(P)
    i = np.arange(P)
    c["bones"] = (i[:, None] // 64 == i[None] // 64)
    c["id64"] = (i[:, None] % 64 == np.arange(64)[None])
    c["iota"] = np.tile(np.arange(64), (P, 1))
    e = np.arange(NE)[:, None, None]
    pair = 2 * np.arange(8)[None, :, None] + (i // 64)[None, None]
    four = 4 * np.arange(4)[None, :, None] + (i // 32)[None, None]
    c["sel"] = np.concatenate([(e == pair), (e == four)], 1).reshape(NE, -1)
    s, t = np.arange(64)[:, None], np.arange(64)[None]
    md, lm = [], []
    for d in range(2):
        strict, incl = (s < t, s <= t) if d == 0 else (s > t, s >= t)
        md.append(np.tile(np.concatenate([strict, incl], 1), (2, 1)))
        for l in range(LEVELS):
            lo, hi = (s >> l, t >> l) if d == 0 else (t >> l, s >> l)
            lm.append(np.tile((lo % 2 == 0) & (hi == lo + 1), (2, 1)))
    c["md"] = np.concatenate(md, 1)
    c["lm"] = np.concatenate(lm, 1)
    c["rst"] = np.tile((np.arange(512) % 64 != 0), (P, 1))
    c["rst128"] = np.tile((np.arange(512) % 128 != 0), (6, 1))
    c["neg"] = np.where(i[None] <= i[:, None], 0.0, -1e30)
    c["caus"] = (i[:, None] <= i[None])
    c["sel6"] = (np.arange(6)[:, None, None] == np.arange(6)[None, :, None]) * np.ones((1, 1, P))
    c["sel6"] = c["sel6"].reshape(6, -1)
    inv = np.power(np.float32(10000.0), -np.arange(16, dtype=f) / np.float32(16))
    ang = np.arange(TX, dtype=f)[None] * inv[:, None].astype(f)
    co, si = np.cos(ang.astype(np.float64)), np.sin(ang.astype(np.float64))
    c["rope"] = np.concatenate([np.concatenate([co, co], 0), np.concatenate([-si, si], 0)], 1)
    c["iop"] = np.stack([i % 64, i % 32], 1)
    c["selc"] = np.stack([i % 32 == 0, i % 32 == 1], 1)
    return {k: np.ascontiguousarray(v, dtype=f) for k, v in c.items()}


def layout(x):
    c = constants()
    n = {k: np.asarray(v) for k, v in x.items()}
    parts = {
        "norm_g": feature_cols(n["norm_g"].reshape(4, D)), "fnet_bo": feature_cols(n["fnet_bo"]),
        "mix": feature_cols(n["rw_mix"][0]), "w0": feature_cols(n["rw_w0"][0]), "a0": feature_cols(n["rw_a0"][0]),
        "kk": feature_cols(n["rw_kk"]), "ka": feature_cols(n["rw_ka"]), "rk": feature_cols(n["rw_rk"].reshape(1, D)),
        "lnw": feature_cols(n["rw_lnx_w"]), "lnb": feature_cols(n["rw_lnx_b"]), "final_g": feature_cols(n["final_g"][None]),
        "nmix": feature_cols(n["norm_mix_g_2"]), "nmlp": feature_cols(n["norm_mlp_g_2"]),
        "fin2": feature_cols(n["final_norm_g_2"][None]), "ada_b": feature_cols(n["ada_b"]),
        "convw": feature_cols(n["ssd_conv_w_2"].reshape(8, 640)), "convb": feature_cols(n["ssd_conv_b_2"]),
        "ssdg": feature_cols(n["ssd_norm_g_2"]), "qg": feature_cols(n["mla_q_norm_g_2"]),
        "kvg": feature_cols(n["mla_kv_norm_g_2"]), "ssdd": feature_cols(np.repeat(n["ssd_d_2"], 64, axis=1)),
        "c": np.stack([feature_cols(n["c"]), feature_cols(n["c_ctx"][None])], 2).reshape(P, 16), "iop": c.pop("iop"), "selc": c.pop("selc"),
    }
    vecs = np.zeros((P, NVEC), np.float32)
    for k, v in parts.items():
        vecs[:, VEC[k]:VEC[k] + v.shape[1]] = v
    w_in, qb = n["w_in_2"], n["mla_w_qb_2"].reshape(2, 384, 6, 96)
    kr = w_in[:, :, 2182:2214]
    arrays = {
        "vecs": vecs, "xT": n["x"][0].T, "ctxT": n["ctx"][0].T,
        "w1cat": n["rw_w1"][0].transpose(1, 0, 2).reshape(D, P), "a1cat": n["rw_a1"][0].transpose(1, 0, 2).reshape(D, P),
        "w2cat": n["rw_w2"][0].reshape(P, D), "a2cat": n["rw_a2"][0].reshape(P, D),
        "krcat": np.concatenate([kr, kr[:, :, 16:], kr[:, :, :16]], 2),
        "qbsw": np.concatenate([qb[..., 80:96], qb[..., 64:80]], 3).reshape(2, 384, 192),
        "wsT": n["gmlp_w_s_2"].transpose(0, 1, 3, 2),
        "vng": np.repeat(n["gmlp_v_norm_g_2"][:, None, :], P, axis=1),
        "gbs": np.repeat(n["gmlp_b_s_2"].reshape(2, 2, 2, 128).transpose(0, 2, 1, 3).reshape(2, 2, 256), 64, axis=1),
        "sm6": np.concatenate([n["ssd_dt_bias_2"].T, n["ssd_a_log_2"].T], 1),
    }
    for k in ("ada_w", "fnet_wo", "rw_wr", "rw_wk", "rw_wv", "rw_wo", "rw_g1", "rw_g2", "moe_router", "moe_wg",
              "moe_wu", "moe_wd", "w_in_2", "mla_w_qb_2", "mla_w_kvb_2", "w_out_2", "mlp_w1_2", "mlp_w2_2"):
        arrays[k] = n[k]
    arrays.update(c)
    return {k: np.ascontiguousarray(v) for k, v in arrays.items()}


def kernel(**inputs):
    import concourse.bacc as bacc
    from concourse.bass_utils import run_bass_kernel_spmd

    arrays = layout(inputs)
    table = {}
    for _ in range(2):
        nc = bacc.Bacc("TRN2", target_bir_lowering=False, num_devices=1)
        aps = {k: nc.dram_tensor(f"in_{k}", v.shape, mybir.dt.from_np(v.dtype), kind="ExternalInput").ap()
               for k, v in arrays.items()}
        out = nc.dram_tensor("outT", (D, TX), F32, kind="ExternalOutput").ap()
        table = build(nc, aps, out, table)
    r = run_bass_kernel_spmd(nc, [{f"in_{k}": v for k, v in arrays.items()}], core_ids=[0])
    return np.ascontiguousarray(r.results[0]["outT"].T)[None]
```

```python
import math
from contextlib import ExitStack

import numpy as np

import concourse.bass as bass
from concourse import mybir

F32 = mybir.dt.float32
F32R = mybir.dt.float32r
ALU = mybir.AluOpType
ACT = mybir.ActivationFunctionType
AX = mybir.AxisListType.X

P = 128
D = 1024
KT = D // P
TX, TC = 512, 256
TA = TX + TC
SEGS = ((0, TX), (TX, TC))
XSEG = ((0, TX),)
NE = 16
CAPX, CAPC = 2 * TX // NE, 2 * TC // NE
SLOT = 2048
NSLOT = 8
CH = 64
NCHX, NCHC = TX // CH, TC // CH
NCH = NCHX + NCHC
LEVELS = 6
STREAMS = ("kk", "kka0", "kka1", "kd0", "kd1", "lw0", "lw1", "v", "r", "g")
VEC_PARTS = {}
STOP = None


def vec_layout():
    off, at = 0, {}
    for name, n in (
        ("norm_g", 32), ("fnet_bo", 8), ("mix", 48), ("w0", 16), ("a0", 16), ("kk", 8), ("ka", 8), ("rk", 8),
        ("lnw", 8), ("lnb", 8), ("final_g", 8), ("nmix", 16), ("nmlp", 16), ("fin2", 8), ("ada_b", 96),
        ("convw", 40), ("convb", 10), ("ssdg", 6), ("qg", 6), ("kvg", 4), ("ssdd", 6), ("c", 16), ("iop", 2), ("selc", 2),
    ):
        at[name] = off
        off += n
    return at, off


VEC, NVEC = vec_layout()


def weight_plan(a):
    plan = []

    def cols(name, src, width=256):
        n = src.shape[1]
        for i, c in enumerate(range(0, n, width)):
            plan.append((f"{name}.{i}", src[:, c:min(n, c + width)]))

    def ada(i):
        cols(f"ada{i}", a["ada_w"][i])

    def moe(i):
        plan.append((f"router{i}", a["moe_router"][i]))

        def part(nm, e):
            for r in range(2):
                for n in range(2):
                    plan.append((f"w{nm}{i}.{e}.{r}.{n}",
                                 a[f"moe_w{nm}"][i, e, 512 * r:512 * r + 512, 512 * n:512 * n + 512]))
        for e in range(NE):
            part("g", e)
            if e:
                part("d", e - 1)
            part("u", e)
        part("d", NE - 1)

    ada(0)
    plan.append(("dftC", a["dftC"]))
    plan.append(("dftTc", a["dftTc"]))
    plan.append(("dftT.0", a["dftT"][:, 0:TX]))
    plan.append(("dftT.1", a["dftT"][:, TX:2 * TX]))
    cols("fwo", a["fnet_wo"][0])
    moe(0)
    ada(1)
    plan.append(("w1", a["w1cat"]))
    plan.append(("w2", a["w2cat"]))
    plan.append(("a1", a["a1cat"]))
    plan.append(("a2", a["a2cat"]))
    cols("wk", a["rw_wk"][0])
    cols("wv", a["rw_wv"][0])
    cols("wr", a["rw_wr"][0])
    plan.append(("g1", a["rw_g1"][0]))
    plan.append(("g2", a["rw_g2"][0]))
    for n in range(5):
        plan.append((f"hold.{n}", None))
    cols("wo", a["rw_wo"][0])
    moe(1)
    for l in range(2):
        w = a["w_in_2"][l]
        cols(f"i{l}.cq", w[:, 1542:1926])
        plan.append((f"i{l}.ckv", w[:, 1926:2182]))
        plan.append((f"i{l}.kr", a["krcat"][l]))
        plan.append((f"i{l}.qb", a["mla_w_qb_2"][l]))
        plan.append((f"i{l}.qs", a["qbsw"][l]))
        plan.append((f"i{l}.kvb", a["mla_w_kvb_2"][l]))
        plan.append((f"i{l}.v", w[:, 256:512]))
        plan.append((f"i{l}.u", w[:, 0:256]))
        plan.append((f"i{l}.dt", w[:, 1536:1542]))
        cols(f"i{l}.xbc", w[:, 896:1536])
        cols(f"i{l}.z", w[:, 512:896])
        cols(f"i{l}.wout", a["w_out_2"][l])
        for half in range(2):
            for i in range(8 * half, 8 * half + 8):
                plan.append((f"i{l}.m1.{i}", a["mlp_w1_2"][l, :, 256 * i:256 * i + 256]))
            for n in range(2):
                for r in range(4 * half, 4 * half + 4):
                    plan.append((f"i{l}.m2.{n}.{r}",
                                 a["mlp_w2_2"][l, 512 * r:512 * r + 512, 512 * n:512 * n + 512]))
    return plan


def build(nc, a, out, table):
    marks = {}
    ctx = ExitStack()
    with ctx:
        def sb(name, shape):
            return ctx.enter_context(nc.sbuf_tensor(name, shape, F32))

        def semaphore(name):
            return ctx.enter_context(nc.semaphore(name))

        def both(name, shape):
            with nc.sbuf_tensor(name, shape, F32) as plain:
                pass
            return plain, ctx.enter_context(nc.sbuf_tensor(name + "_rounded", shape, F32R))

        X, X_r = both("X", [P, KT, TA])
        H, H_r = both("H", [P, KT, TA])
        ring, ring_r = both("ring", [P, NSLOT, SLOT])
        vec = sb("vec", [P, NVEC])
        ident = sb("ident", [P, P])
        ones = sb("ones", [P, P])
        bones = sb("bones", [P, P])
        id64 = sb("id64", [P, 64])
        iota = sb("iota", [P, 64])
        eps = sb("eps", [P, 4])
        ada = sb("ada", [P, 48, 2])
        gsc = sb("gsc", [P, 2, KT, 2])
        csil = sb("csil", [P, KT, 32])
        small = sb("small", [P, 256])
        SCRW = 22900
        scr, scr_r = both("scr", [P, SCRW])
        ps = ctx.enter_context(nc.psum_tensor("ps", [P, 8, 512], F32))
        dram = {s: nc.dram_tensor(f"st_{s}", (P, KT, TA), F32).ap() for s in STREAMS}

        def S(off, *dims, of=scr):
            n = int(np.prod(dims))
            assert off + n <= SCRW, (off, dims)
            t = of[:, off:off + n]
            if len(dims) == 2:
                return t.rearrange("p (a b) -> p a b", b=dims[1])
            if len(dims) == 3:
                return t.rearrange("p (a b c) -> p a b c", b=dims[1], c=dims[2])
            if len(dims) == 4:
                return t.rearrange("p (a b c d) -> p a b c d", b=dims[1], c=dims[2], d=dims[3])
            return t

        sems = {
            "T": semaphore("tensor_done"), "V": semaphore("vector_done"),
            "A": semaphore("scalar_done"), "G": semaphore("pool_done"),
            "const": semaphore("constants_loaded"), "out": semaphore("output_stored"),
        }
        for i in range(NSLOT):
            sems[f"slot{i}"] = semaphore(f"weight_slot_{i}_loaded")
        for i in range(5):
            sems[f"st{i}"] = semaphore(f"stage_tile_{i}_stored_by_pool")
            sems[f"sa{i}"] = semaphore(f"stage_tile_{i}_stored_by_scalar")
        for i in range(2):
            sems[f"ld{i}"] = semaphore(f"chunk_buffer_{i}_loaded")
        sems["aux"] = semaphore("stage_constants_loaded")
        tensor_done, vector_done, scalar_done, pool_done = (sems[e] for e in "TVAG")
        inputs_in, constants_in, output_out = sems["const"], sems["aux"], sems["out"]
        count = dict.fromkeys(sems, 0)
        waited = {}

        def did(e, ins, name=None, by=1):
            count[e] += by
            if name is not None:
                assert name not in marks, name
                marks[name] = (e, count[e])

        def at(step):
            e, v = table.get(step, ("T", 1)) if not table else table[step]
            return sems[e], v

        def later(eng, step):
            e, v = table.get(step, ("T", 1)) if not table else table[step]
            fresh = waited.get((eng.engine, e), 0) < v
            if fresh:
                waited[eng.engine, e] = v
            return fresh

        def own(eng, e):
            waited[eng.engine, e] = count[e]
            return sems[e], count[e]

        def phase(eng, e, name):
            marks[f"ph.{name}.{e}"] = (e, count[e])
            for other in "TVAG":
                if other != e and table and table[f"ph.{name}.{other}"][1] > 0:
                    if later(eng, f"ph.{name}.{other}"):
                        eng.wait_ge(*at(f"ph.{name}.{other}"))

        owner = [None] * 8
        nbank = [0]

        def bank(pe, key):
            b = nbank[0] % 8
            nbank[0] += 1
            if owner[b] is not None:
                if later(pe, "free." + owner[b]):
                    pe.wait_ge(*at("free." + owner[b]))
            owner[b] = key
            marks["bank." + key] = ("bank", b)
            return ps[:, b, :]

        def tile(eng, key):
            if later(eng, key):
                eng.wait_ge(*at(key))
            return ps[:, table["bank." + key][1] if table else 0, :]

        plan = weight_plan(a)
        place = {name: (i % NSLOT, src.shape if src is not None else None) for i, (name, src) in enumerate(plan)}

        def weight(pe, name, of=ring):
            if later(pe, "w." + name):
                pe.wait_ge(*at("w." + name))
            s, (rows, cols) = place[name]
            n = max(1, rows // P)
            return of[0:min(P, rows), s, 0:n * cols].rearrange("p (k c) -> p k c", c=cols)

        block = ctx.enter_context(nc.Block())

        @block.sync
        def _(sp):
            def load(dst, src, name):
                did("const", sp.dma_start(dst, src).then_inc(inputs_in, 16), by=16)
            load(vec[:, :], a["vecs"], "c")
            load(ident[:, :], a["ident"], "c")
            load(bones[:, :], a["bones"], "c")
            load(id64[:, :], a["id64"], "c")
            load(iota[:, :], a["iota"], "c")
            load(X[:, :, 0:TX], a["xT"].rearrange("(k p) t -> p k t", p=P), "c")
            load(X[:, :, TX:TA], a["ctxT"].rearrange("(k p) t -> p k t", p=P), "c")
            marks["const"] = ("const", count["const"])
            for i, (name, src) in enumerate(plan):
                if STOP is not None and not table.get("wf." + name) and table:
                    break
                if src is None:
                    continue
                if i >= NSLOT:
                    if later(sp, "wf." + plan[i - NSLOT][0]):
                        sp.wait_ge(*at("wf." + plan[i - NSLOT][0]))
                rows, cols = src.shape
                n = max(1, rows // P)
                dst = ring[0:min(P, rows), i % NSLOT, 0:n * cols].rearrange("p (k c) -> p k c", c=cols)
                did(f"slot{i % NSLOT}", sp.dma_start(dst, src.rearrange("(k p) c -> p k c", p=min(P, rows))).then_inc(sems[f"slot{i % NSLOT}"], 16), "w." + name, by=16)
            if later(sp, "final"):
                sp.wait_ge(*at("final"))
            did("out", sp.dma_start(out.rearrange("(k p) t -> p k t", p=P), H[:, :, 0:TX]).then_inc(output_out, 16), by=16)
            sp.wait_ge(sems["out"], 16)

        V, A_, T_, G_ = "V", "A", "T", "G"

        def col(name, i):
            return vec[:, VEC[name] + i:VEC[name] + i + 1]

        NEXT = {"moe0": "n1", "post": "m1", "moe1": "fg", "wout0": "n30", "mlp0": "n21", "wout1": "n31", "mlp1": "end"}
        EARLY = list(NEXT.values()) if STOP is None else list(NEXT.values())[:-1]

        def residual_scalar(act, tag, segs, norm, tiles=range(KT)):
            w = sum(s[1] for s in segs)
            for m in tiles if norm in EARLY else ():
                if later(act, f"{tag}.x{m}"):
                    act.wait_ge(*at(f"{tag}.x{m}"))
                did(A_, act.activation(H[:, m, 0:w], X[:, m, 0:w], ACT.Square).then_inc(scalar_done, 1), f"{norm}.sq{m}")

        def norm_sum(dve, norm, k, w):
            if later(dve, f"{norm}.sq{k}"):
                dve.wait_ge(*at(f"{norm}.sq{k}"))
            if later(dve, f"{norm}.sq0"):
                dve.wait_ge(*at(f"{norm}.sq0"))
            did(V, dve.tensor_tensor(H[:, 0, 0:w], H[:, 0, 0:w], H[:, k, 0:w], ALU.add).then_inc(vector_done, 1))
            dve.wait_ge(*own(dve, V))
            if k == KT - 1:
                marks[f"{norm}.sum"] = (V, count[V])

        def norm_scalar(act, tag, segs, n, shift):
            w = sum(s[1] for s in segs)
            rs = small_rs
            for k in range(KT) if tag not in EARLY else ():
                did(A_, act.activation(H[:, k, 0:w], X[:, k, 0:w], ACT.Square).then_inc(scalar_done, 1), f"{tag}.sq{k}")
            for s0, sn in segs:
                t = tile(act, f"{tag}.ss{s0}")
                did(A_, act.activation(rs[:, s0:s0 + sn], t[:, 0:sn], ACT.Sqrt, bias=eps[:, 0:1], scale=1.0 / D).then_inc(scalar_done, 1), f"free.{tag}.ss{s0}")
            if shift:
                for k in range(KT):
                    if later(act, f"{tag}.g{k}"):
                        act.wait_ge(*at(f"{tag}.g{k}"))
                    for i, (s0, sn) in enumerate(segs):
                        did(A_, act.activation(H[:, k, s0:s0 + sn], H[:, k, s0:s0 + sn], ACT.Identity,
                                               bias=ada[:, shift[0] + k, i:i + 1]).then_inc(scalar_done, 1))
                    marks[f"{tag}.h{k}"] = (A_, count[A_])

        def norm_tensor(pe, tag, segs):
            if later(pe, f"{tag}.sum"):
                pe.wait_ge(*at(f"{tag}.sum"))
            for s0, sn in segs:
                b = bank(pe, f"{tag}.ss{s0}")
                did(T_, pe.matmul(b[:, 0:sn], ones[:, :], H[:, 0, s0:s0 + sn], start=True, stop=True).then_inc(tensor_done, 1), f"{tag}.ss{s0}")

        def norm_vector(dve, tag, segs, gain, shift):
            w = sum(s[1] for s in segs)
            rs = small_rs
            for k in range(1, KT) if tag not in EARLY else ():
                norm_sum(dve, tag, k, w)
            for step in [f"free.{tag}.ss{s0}" for s0, _ in segs]:
                if later(dve, step):
                    dve.wait_ge(*at(step))
            did(V, dve.reciprocal(rs[:, 0:w], rs[:, 0:w]).then_inc(vector_done, 1))
            dve.wait_ge(*own(dve, V))
            for k in range(KT):
                for i, (s0, sn) in enumerate(segs):
                    did(V, dve.scalar_tensor_tensor(H[:, k, s0:s0 + sn], X[:, k, s0:s0 + sn], gain(i, k),
                                                    rs[:, s0:s0 + sn], ALU.mult, ALU.mult).then_inc(vector_done, 1))
                marks[f"{tag}.{'g' if shift else 'h'}{k}"] = (V, count[V])

        small_rs = S(SCRW - TA, TA)

        AP_ = S(0, 2, 256)

        def ada_tensor(pe, i):
            def turn(blk):
                n = blk // 6
                if blk % 6 == 0:
                    ada_bank[0] = bank(pe, f"ada{i}.{n}")
                if later(pe, f"free.ad{i}.{blk}"):
                    pe.wait_ge(*at(f"free.ad{i}.{blk}"))
                for j in range(2):
                    m = 2 * (blk % 6) + j
                    ins = pe.matmul(ada_bank[0][:, 2 * m:2 * m + 2], AP_[:, blk % 2, j * P:j * P + P],
                                    vec[:, VEC["selc"]:VEC["selc"] + 2], start=True, stop=True)
                did(T_, ins.then_inc(tensor_done, 1), f"ada{i}.{n}" if blk % 6 == 5 else f"adt{i}.{blk}")
                if blk % 6 == 5:
                    marks[f"adt{i}.{blk}"] = (T_, count[T_])
            ada_bank = [None]
            if later(pe, "csil"):
                pe.wait_ge(*at("csil"))
            for blk in range(24):
                w = weight(pe, f"ada{i}.{blk}")
                b = bank(pe, f"ad{i}.{blk}")
                for half in range(2):
                    for c in range(4):
                        ins = pe.matmul(b[32 * c:32 * c + 32, 0:256], csil[:, 2 * c + half, :], w[:, 2 * c + half, :],
                                        start=half == 0, stop=half == 1)
                did(T_, ins.then_inc(tensor_done, 1), f"ad{i}.{blk}")
                marks[f"wf.ada{i}.{blk}"] = (T_, count[T_])
                if blk:
                    turn(blk - 1)
            turn(23)

        def ada_vector(dve, i):
            for blk in range(24):
                if blk >= 2:
                    if later(dve, f"adt{i}.{blk - 2}"):
                        dve.wait_ge(*at(f"adt{i}.{blk - 2}"))
                t = tile(dve, f"ad{i}.{blk}")
                did(V, dve.tensor_copy(AP_[:, blk % 2, :], t[:, 0:256]).then_inc(vector_done, 1), f"free.ad{i}.{blk}")
                if blk % 6 == 0 and blk:
                    part(dve, i, blk // 6 - 1)
            part(dve, i, 3)
            dve.wait_ge(*own(dve, V))
            for n in range(2):
                sc = ada[:, 24 * n + 8:24 * n + 16, :]
                g = vec[:, VEC["norm_g"] + 16 * i + 8 * n:VEC["norm_g"] + 16 * i + 8 * n + 8]
                did(V, dve.scalar_tensor_tensor(gsc[:, n, :, :], sc, 1.0,
                                                g.unsqueeze(2).to_broadcast([P, KT, 2]), ALU.add, ALU.mult).then_inc(vector_done, 1), f"gsc{i}.{n}")
            dve.wait_ge(*own(dve, V))

        def part(dve, i, n):
            t = tile(dve, f"ada{i}.{n}")
            o = VEC["ada_b"] + 48 * i + 12 * n
            did(V, dve.tensor_tensor(ada[:, 12 * n:12 * n + 12, :], t[:, 0:24].rearrange("p (m c) -> p m c", c=2),
                                     vec[:, o:o + 12].unsqueeze(2).to_broadcast([P, 12, 2]), ALU.add).then_inc(vector_done, 1), f"free.ada{i}.{n}")

        def linear_tensor(pe, tag, wname, rhs, segs, ready, mtiles=8, kt=KT, after=None):
            for m in range(mtiles):
                w = weight(pe, f"{wname}.{m // 2}")
                for s0, sn in segs:
                    b = bank(pe, f"{tag}.{m}.{s0}")
                    for k in range(kt):
                        if later(pe, ready(k)):
                            pe.wait_ge(*at(ready(k)))
                        ins = pe.matmul(b[:, 0:sn], w[:, k, (m % 2) * P:(m % 2) * P + P], rhs(k, s0, sn),
                                        start=k == 0, stop=k == kt - 1)
                    did(T_, ins.then_inc(tensor_done, 1), f"{tag}.{m}.{s0}")
                if m % 2 == 1 or m == mtiles - 1:
                    marks[f"wf.{wname}.{m // 2}"] = (T_, count[T_])

        def residual_vector(dve, tag, segs, gate=None, norm=None, tiles=range(KT)):
            w = sum(s[1] for s in segs)
            for m in tiles:
                for i, (s0, sn) in enumerate(segs):
                    t = tile(dve, f"{tag}.{m}.{s0}")
                    x = X[:, m, s0:s0 + sn]
                    if gate is None:
                        ins = dve.tensor_tensor(x, t[:, 0:sn], x, ALU.add)
                    else:
                        ins = dve.scalar_tensor_tensor(x, t[:, 0:sn], ada[:, gate + m, i:i + 1], x, ALU.mult, ALU.add)
                    did(V, ins.then_inc(vector_done, 1), f"free.{tag}.{m}.{s0}")
                marks[f"{tag}.x{m}"] = (V, count[V])
                if norm in EARLY and m >= 2:
                    norm_sum(dve, norm, m - 1, w)
            if norm in EARLY and KT - 1 in tiles:
                norm_sum(dve, norm, KT - 1, w)

        Z = S(0, 6, 4, 512)
        fb = small[:, 0:16].rearrange("p (k c) -> p k c", c=2)

        def fnet_tensor(pe):
            w = weight(pe, "dftC")
            for tt in range(6):
                for g in range(4):
                    b = bank(pe, f"f1.{tt}.{g}")
                    for k in range(2):
                        if later(pe, f"n0.h{2 * g + k}"):
                            pe.wait_ge(*at(f"n0.h{2 * g + k}"))
                        ins = pe.matmul(b, H[:, 2 * g + k, tt * P:tt * P + P], w[:, k, :], start=k == 0, stop=k == 1)
                    did(T_, ins.then_inc(tensor_done, 1), f"f1.{tt}.{g}")
            marks["wf.dftC"] = (T_, count[T_])
            for s0, sn, tts, ws in ((TX, TC, (4, 5), ("dftTc",)), (0, TX, (0, 1, 2, 3), ("dftT.0", "dftT.1"))):
                for d in range(KT):
                    b = bank(pe, f"f2.{d}.{s0}")
                    for cs in range(2):
                        w = weight(pe, ws[cs % len(ws)])
                        for n, tt in enumerate(tts):
                            if later(pe, f"free.f1.{tt}.{d // 2}"):
                                pe.wait_ge(*at(f"free.f1.{tt}.{d // 2}"))
                            rhs = w[:, n, cs * TC:cs * TC + TC] if len(ws) == 1 else w[:, n, :]
                            o = cs * 256 + (d % 2) * P
                            ins = pe.matmul(b[:, 0:sn], Z[:, tt, d // 2, o:o + P], rhs,
                                            start=cs == 0 and n == 0, stop=cs == 1 and n == len(tts) - 1)
                    did(T_, ins.then_inc(tensor_done, 1), f"f2.{d}.{s0}")
                for wn in ws:
                    marks["wf." + wn] = (T_, count[T_])
            linear_tensor(pe, "fo", "fwo", lambda k, s0, sn: H[:, k, s0:s0 + sn], SEGS, lambda k: f"free.f2.{k}.0")

        def fnet_scalar(act):
            for tt in range(6):
                for g in range(1, 4, 2):
                    t = tile(act, f"f1.{tt}.{g}")
                    did(A_, act.activation(Z[:, tt, g, :], t, ACT.Copy).then_inc(scalar_done, 1), f"free.f1.{tt}.{g}")

        def fnet_vector(dve):
            for tt in range(6):
                for g in range(0, 4, 2):
                    t = tile(dve, f"f1.{tt}.{g}")
                    did(V, dve.tensor_copy(Z[:, tt, g, :], t).then_inc(vector_done, 1), f"free.f1.{tt}.{g}")
            for s0, sn in (SEGS[1], SEGS[0]):
                for d in range(KT):
                    t = tile(dve, f"f2.{d}.{s0}")
                    did(V, dve.tensor_copy(H[:, d, s0:s0 + sn], t[:, 0:sn]).then_inc(vector_done, 1), f"free.f2.{d}.{s0}")
            bo = vec[:, VEC["fnet_bo"]:VEC["fnet_bo"] + 8].unsqueeze(2).to_broadcast([P, KT, 2])
            did(V, dve.tensor_tensor(fb, ada[:, 16:24, :], bo, ALU.mult).then_inc(vector_done, 1))
            dve.wait_ge(*own(dve, V))
            for k in range(KT):
                for i, (s0, sn) in enumerate(SEGS):
                    did(V, dve.tensor_scalar(X[:, k, s0:s0 + sn], X[:, k, s0:s0 + sn], fb[:, k, i:i + 1], None, ALU.add).then_inc(vector_done, 1))
            dve.wait_ge(*own(dve, V))
            residual_vector(dve, "fo", SEGS, 16)

        HT = S(0, 6, D)
        YSX = S(6144, 8, D)
        YSC = S(14336, 4, D)
        HDC = S(18432, 256)
        HIC = S(18688, 2, P)
        GM = S(19200, 6, 256)
        WORK = scr[0:NE, 19200:19200 + TA]
        AT = scr[0:NE, 20736:20736 + TA]
        AFF = S(21504, 6, NE)
        POST = S(21600, 6, NE)
        HDX = S(21696, 512)
        HIX = S(22208, 4, P)
        MX = S(22720, 8)
        M8 = scr[0:NE, 22728:22736]
        RANK = scr[0:NE, 19200 + TA:19200 + 2 * TA]
        POSM = scr[32:32 + NE, 20736:20736 + TA]
        SMX = S(0, 8, TX)
        SMC = S(4096, 4, TC)
        AB = S(5120, 2, 512)
        sel = S(19200, 12, P)

        def XS(q):
            return H[:, :, :].rearrange("p k t -> p (k t)")[:, 3072 * q:3072 * q + 3072].rearrange(
                "p (k e c) -> p k e c", k=KT, c=96)

        def moe_segs(i):
            return SEGS if i == 0 else XSEG

        def experts_tensor(pe, i, gather, spread):
            def product(nm, e, stat_x, stat_c):
                bx = bank(pe, f"{nm}x{i}.{e}")
                bc = bank(pe, f"{nm}c{i}.{e}") if i == 0 else None
                for k in range(KT):
                    if nm != "d":
                        if later(pe, f"free.xs{i}.{e // 4}.{k}"):
                            pe.wait_ge(*at(f"free.xs{i}.{e // 4}.{k}"))
                    for n in range(2):
                        w = weight(pe, f"w{nm}{i}.{e}.{k // 4}.{n}")
                        ins = pe.matmul(bx[64 * n:64 * n + 64, :], stat_x(k), w[:, k % 4, :], start=k == 0, stop=k == KT - 1)
                    for n in range(4) if i == 0 else ():
                        w = weight(pe, f"w{nm}{i}.{e}.{k // 4}.{n // 2}")
                        o = 256 * (n % 2)
                        ins = pe.matmul(bc[32 * n:32 * n + 32, 0:256], stat_c(k), w[:, k % 4, o:o + 256],
                                        start=k == 0, stop=k == KT - 1)
                    if k == 3:
                        did(T_, ins.then_inc(tensor_done, 1))
                        for n in range(2):
                            marks[f"wf.w{nm}{i}.{e}.0.{n}"] = (T_, count[T_])
                did(T_, ins.then_inc(tensor_done, 1), f"{nm}x{i}.{e}")
                marks[f"{nm}c{i}.{e}"] = (T_, count[T_])
                for n in range(2):
                    marks[f"wf.w{nm}{i}.{e}.1.{n}"] = (T_, count[T_])

            def turn(e):
                if later(pe, f"hd{i}.{e}"):
                    pe.wait_ge(*at(f"hd{i}.{e}"))
                b = bank(pe, f"hx{i}.{e}")
                for f in range(4):
                    ins = pe.transpose(b[:, f * P:f * P + P], HDX[:, f * P:f * P + P], ident[:, :])
                did(T_, ins.then_inc(tensor_done, 1), f"hx{i}.{e}")
                if i == 0:
                    b = bank(pe, f"hc{i}.{e}")
                    for f in range(2):
                        ins = pe.transpose(b[:, f * P:f * P + P], HDC[:, f * P:f * P + P], ident[:, :])
                    did(T_, ins.then_inc(tensor_done, 1), f"hc{i}.{e}")

            def second(e):
                if later(pe, f"hi{i}.{e}"):
                    pe.wait_ge(*at(f"hi{i}.{e}"))
                product("d", e, lambda f: HIX[:, f % 4, 64 * (f // 4):64 * (f // 4) + 64],
                        lambda f: HIC[:, f % 2, 32 * (f // 2):32 * (f // 2) + 32])

            for e in range(NE):
                xs = XS((e // 4) % 2)

                def first(nm):
                    product(nm, e, lambda k: xs[:, k, e % 4, 0:64], lambda k: xs[:, k, e % 4, 64:96])
                if e:
                    turn(e - 1)
                first("g")
                if e:
                    second(e - 1)
                first("u")
                if e % 4 == 0 and e < 12:
                    gather(e // 4 + 1)
                if e >= 12:
                    spread(e - 12)
            turn(NE - 1)
            second(NE - 1)

        def experts_scalar(act, i, spread):
            def turned(e):
                t = tile(act, f"hx{i}.{e}")
                if e:
                    if later(act, f"dx{i}.{e - 1}"):
                        act.wait_ge(*at(f"dx{i}.{e - 1}"))
                did(A_, act.activation(HIX[:, :, :].rearrange("p f c -> p (f c)"), t, ACT.Copy).then_inc(scalar_done, 1), f"free.hx{i}.{e}")
                if i == 0:
                    t = tile(act, f"hc{i}.{e}")
                    did(A_, act.activation(HIC[:, :, :].rearrange("p f c -> p (f c)"), t[:, 0:256], ACT.Copy).then_inc(scalar_done, 1), f"free.hc{i}.{e}")
                marks[f"hi{i}.{e}"] = (A_, count[A_])

            def out(e):
                t = tile(act, f"dx{i}.{e}")
                for n in range(2):
                    o = 64 * (e % 2)
                    did(A_, act.activation(YSX[o:o + 64, e // 2, 512 * n:512 * n + 512], t[64 * n:64 * n + 64, :], ACT.Copy).then_inc(scalar_done, 1))
                marks[f"free.dx{i}.{e}"] = (A_, count[A_])
                if i == 0:
                    t = tile(act, f"dc{i}.{e}")
                    o = 32 * (e % 4)
                    for n in range(4):
                        did(A_, act.activation(YSC[o:o + 32, e // 4, 256 * n:256 * n + 256], t[32 * n:32 * n + 32, 0:256],
                                               ACT.Copy).then_inc(scalar_done, 1))
                    marks[f"free.dc{i}.{e}"] = (A_, count[A_])
            for e in range(NE):
                if e:
                    turned(e - 1)
                t = tile(act, f"gx{i}.{e}")
                did(A_, act.activation(HDX, t, ACT.Silu).then_inc(scalar_done, 1), f"free.gx{i}.{e}")
                if i == 0:
                    t = tile(act, f"gc{i}.{e}")
                    did(A_, act.activation(HDC, t[:, 0:256], ACT.Silu).then_inc(scalar_done, 1), f"free.gc{i}.{e}")
                if e:
                    out(e - 1)
                if e >= 12:
                    spread(e - 12)
            turned(NE - 1)
            out(NE - 1)
            marks[f"ys{i}"] = (A_, count[A_])

        def experts_vector(dve, i, onehot, take, spread):
            for e in range(NE):
                if e % 4 == 0 and e < 12:
                    onehot(e // 4 + 1)
                t = tile(dve, f"ux{i}.{e}")
                if later(dve, f"free.gx{i}.{e}"):
                    dve.wait_ge(*at(f"free.gx{i}.{e}"))
                did(V, dve.tensor_tensor(HDX, t, HDX, ALU.mult).then_inc(vector_done, 1), f"free.ux{i}.{e}")
                if i == 0:
                    t = tile(dve, f"uc{i}.{e}")
                    if later(dve, f"free.gc{i}.{e}"):
                        dve.wait_ge(*at(f"free.gc{i}.{e}"))
                    did(V, dve.tensor_tensor(HDC, t[:, 0:256], HDC, ALU.mult).then_inc(vector_done, 1), f"free.uc{i}.{e}")
                marks[f"hd{i}.{e}"] = (V, count[V])
                if e % 4 == 0 and e < 12:
                    take(e // 4 + 1)
                if e >= 12:
                    spread(e - 12)

        def spread_items(i, part):
            n = 2 if i == 1 else 3
            for j in range(n * part, n * part + n):
                yield (j, "", j) if j < 8 else (j, "c", j - 8)

        def moe_tensor(pe, i):
            segs = moe_segs(i)
            ntt = 6 if i == 0 else 4
            w = weight(pe, f"router{i}")
            b = bank(pe, f"rt{i}")
            for tt in range(ntt):
                for k in range(KT):
                    if later(pe, f"m{i}.h{k}"):
                        pe.wait_ge(*at(f"m{i}.h{k}"))
                    ins = pe.matmul(b[:, tt * NE:tt * NE + NE], H[:, k, tt * P:tt * P + P], w[:, k, :],
                                    start=k == 0, stop=k == KT - 1)
            did(T_, ins.then_inc(tensor_done, 1), f"rt{i}")
            marks[f"wf.router{i}"] = (T_, count[T_])
            for tt in range(ntt):
                for half in range(2):
                    b = bank(pe, f"ht{i}.{tt}.{half}")
                    for k in range(4):
                        ins = pe.transpose(b[:, k * P:k * P + P], H[:, 4 * half + k, tt * P:tt * P + P], ident[:, :])
                    did(T_, ins.then_inc(tensor_done, 1), f"ht{i}.{tt}.{half}")
            if later(pe, f"aff{i}"):
                pe.wait_ge(*at(f"aff{i}"))
            for n, (s0, sn) in enumerate(segs):
                b = bank(pe, f"at{i}.{s0}")
                for tt in range(sn // P):
                    ins = pe.transpose(b[0:NE, tt * P:tt * P + P], AFF[:, s0 // P + tt, :], ident[:, :])
                did(T_, ins.then_inc(tensor_done, 1), f"at{i}.{s0}")
            if later(pe, f"posm{i}"):
                pe.wait_ge(*at(f"posm{i}"))
            b = bank(pe, f"pt{i}")
            for tt in range(ntt):
                ins = pe.transpose(b[:, tt * NE:tt * NE + NE], POSM[:, tt * P:tt * P + P],
                                   ident[32:32 + NE, 32:32 + NE])
            did(T_, ins.then_inc(tensor_done, 1), f"pt{i}")

            def gather(q):
                if later(pe, f"gm{i}.{q}"):
                    pe.wait_ge(*at(f"gm{i}.{q}"))
                for step in [f"free.ht{i}.{tt}.{hf}" for tt in range(ntt) for hf in range(2)]:
                    if later(pe, step):
                        pe.wait_ge(*at(step))
                for k in range(KT):
                    b = bank(pe, f"xs{i}.{q}.{k}")
                    for tt in range(4):
                        ins = pe.matmul(b[:, 0:256], HT[:, tt, k * P:k * P + P], GM[:, tt, :], start=tt == 0, stop=tt == 3)
                    if i == 0:
                        for tt in (4, 5):
                            ins = pe.matmul(b[:, 256:384], HT[:, tt, k * P:k * P + P], GM[:, tt, 0:128],
                                            start=tt == 4, stop=tt == 5)
                    did(T_, ins.then_inc(tensor_done, 1), f"xs{i}.{q}.{k}")

            gather(0)

            def spread(part):
                if later(pe, f"sel{i}"):
                    pe.wait_ge(*at(f"sel{i}"))
                for n, pre, j in spread_items(i, part):
                    w, s0 = (TX, 0) if pre == "" else (TC, TX)
                    for nm, src, r in (("pb", POSM, 32), ("ab", AT, 0)):
                        b = bank(pe, f"{nm}{i}.{pre}{j}")
                        did(T_, pe.matmul(b[:, 0:w], sel[r:r + NE, n, :], src[:, s0:s0 + w], start=True, stop=True).then_inc(tensor_done, 1), f"{nm}{i}.{pre}{j}")
            experts_tensor(pe, i, gather, spread)
            if later(pe, f"ys{i}"):
                pe.wait_ge(*at(f"ys{i}"))
            for m in range(KT):
                for s0, sn in segs:
                    b = bank(pe, f"mo{i}.{m}.{s0}")
                    ys, sm, nj, pre = (YSX, SMX, 8, "") if s0 == 0 else (YSC, SMC, 4, "c")
                    for j in range(nj):
                        if later(pe, f"free.pb{i}.{pre}{j}"):
                            pe.wait_ge(*at(f"free.pb{i}.{pre}{j}"))
                        ins = pe.matmul(b[:, 0:sn], ys[:, j, m * P:m * P + P], sm[:, j, :], start=j == 0, stop=j == nj - 1)
                    did(T_, ins.then_inc(tensor_done, 1), f"mo{i}.{m}.{s0}")

        def moe_scalar(act, i):
            ntt = 6 if i == 0 else 4
            if later(act, f"lg{i}"):
                act.wait_ge(*at(f"lg{i}"))
            did(A_, act.activation(AFF[:, 0:ntt, :], AFF[:, 0:ntt, :], ACT.Exp).then_inc(scalar_done, 1), f"ex{i}")
            for tt in range(ntt):
                for half in range(2):
                    t = tile(act, f"ht{i}.{tt}.{half}")
                    did(A_, act.activation(HT[:, tt, 512 * half:512 * half + 512], t, ACT.Copy).then_inc(scalar_done, 1), f"free.ht{i}.{tt}.{half}")
            for s0, sn in moe_segs(i):
                t = tile(act, f"at{i}.{s0}")
                did(A_, act.activation(AT[:, s0:s0 + sn], t[0:NE, 0:sn], ACT.Copy).then_inc(scalar_done, 1), f"free.at{i}.{s0}")

            def spread(part):
                for n, pre, j in spread_items(i, part):
                    w = TX if pre == "" else TC
                    t = tile(act, f"ab{i}.{pre}{j}")
                    if n >= 2:
                        if later(act, f"free.pb{i}.{'' if n - 2 < 8 else 'c'}{n - 2 if n - 2 < 8 else n - 10}"):
                            act.wait_ge(*at(f"free.pb{i}.{'' if n - 2 < 8 else 'c'}{n - 2 if n - 2 < 8 else n - 10}"))
                    did(A_, act.activation(AB[:, n % 2, 0:w], t[:, 0:w], ACT.Copy).then_inc(scalar_done, 1), f"free.ab{i}.{pre}{j}")
            experts_scalar(act, i, spread)
            residual_scalar(act, f"mo{i}", moe_segs(i), NEXT[f"moe{i}"])

        def moe_vector(dve, i):
            segs = moe_segs(i)
            ntt = 6 if i == 0 else 4
            w = TA if i == 0 else TX
            t = tile(dve, f"rt{i}")[:, 0:ntt * NE].rearrange("p (t e) -> p t e", e=NE)
            did(V, dve.tensor_reduce(MX[:, 0:ntt], t, AX, ALU.max).then_inc(vector_done, 1))
            dve.wait_ge(*own(dve, V))
            did(V, dve.tensor_tensor(AFF[:, 0:ntt, :], t, MX[:, 0:ntt].unsqueeze(2).to_broadcast([P, ntt, NE]),
                                     ALU.subtract).then_inc(vector_done, 1), f"lg{i}")
            marks[f"free.rt{i}"] = marks[f"lg{i}"]
            if later(dve, f"ex{i}"):
                dve.wait_ge(*at(f"ex{i}"))
            did(V, dve.tensor_reduce(MX[:, 0:ntt], AFF[:, 0:ntt, :], AX, ALU.add).then_inc(vector_done, 1))
            dve.wait_ge(*own(dve, V))
            did(V, dve.reciprocal(MX[:, 0:ntt], MX[:, 0:ntt]).then_inc(vector_done, 1))
            dve.wait_ge(*own(dve, V))
            did(V, dve.tensor_tensor(AFF[:, 0:ntt, :], AFF[:, 0:ntt, :],
                                     MX[:, 0:ntt].unsqueeze(2).to_broadcast([P, ntt, NE]), ALU.mult).then_inc(vector_done, 1), f"aff{i}")
            for s0, sn in segs:
                if later(dve, f"free.at{i}.{s0}"):
                    dve.wait_ge(*at(f"free.at{i}.{s0}"))
                did(V, dve.tensor_copy(WORK[:, s0:s0 + sn], AT[:, s0:s0 + sn]).then_inc(vector_done, 1))
                dve.wait_ge(*own(dve, V))
                for r in range(2 * sn // NE // 8):
                    did(V, dve.max(M8, WORK[:, s0:s0 + sn]).then_inc(vector_done, 1))
                    dve.wait_ge(*own(dve, V))
                    did(V, dve.match_replace(WORK[:, s0:s0 + sn], M8, WORK[:, s0:s0 + sn], -1.0).then_inc(vector_done, 1))
                    dve.wait_ge(*own(dve, V))
            did(V, dve.tensor_scalar(WORK[:, 0:w], WORK[:, 0:w], 0.0, None, ALU.is_lt).then_inc(vector_done, 1))
            dve.wait_ge(*own(dve, V))
            for s0, sn in segs:
                did(V, dve.tensor_tensor_scan(RANK[:, s0:s0 + sn], ones[0:NE, 0:1].to_broadcast([NE, sn]),
                                              WORK[:, s0:s0 + sn], 0.0, ALU.mult, ALU.add).then_inc(vector_done, 1))
            dve.wait_ge(*own(dve, V))
            did(V, dve.tensor_tensor(RANK[:, 0:w], RANK[:, 0:w], WORK[:, 0:w], ALU.mult).then_inc(vector_done, 1))
            dve.wait_ge(*own(dve, V))
            did(V, dve.tensor_scalar(POSM[:, 0:w], RANK[:, 0:w], -1.0, None, ALU.add).then_inc(vector_done, 1), f"posm{i}")
            t = tile(dve, f"pt{i}")
            did(V, dve.tensor_copy(POST[:, 0:ntt, :], t[:, 0:ntt * NE].rearrange("p (t e) -> p t e", e=NE)).then_inc(vector_done, 1), f"free.pt{i}")
            dve.wait_ge(*own(dve, V))

            def onehot(q):
                if q:
                    if later(dve, f"xs{i}.{q - 1}.{KT - 1}"):
                        dve.wait_ge(*at(f"xs{i}.{q - 1}.{KT - 1}"))
                for tt in range(ntt):
                    c = CAPX if tt < 4 else CAPC
                    did(V, dve.tensor_tensor(
                        GM[:, tt, 0:4 * c].rearrange("p (e c) -> p e c", c=c),
                        iota[:, 0:c].unsqueeze(1).to_broadcast([P, 4, c]),
                        POST[:, tt, 4 * q:4 * q + 4].unsqueeze(2).to_broadcast([P, 4, c]), ALU.is_equal).then_inc(vector_done, 1))
                marks[f"gm{i}.{q}"] = (V, count[V])

            def take(q):
                xs = XS(q % 2)
                if q >= 2:
                    if later(dve, f"ux{i}.{4 * (q - 2) + 3}"):
                        dve.wait_ge(*at(f"ux{i}.{4 * (q - 2) + 3}"))
                else:
                    if later(dve, f"ht{i}.{ntt - 1}.1"):
                        dve.wait_ge(*at(f"ht{i}.{ntt - 1}.1"))
                for k in range(KT):
                    t = tile(dve, f"xs{i}.{q}.{k}")
                    did(V, dve.tensor_copy(xs[:, k, :, 0:64], t[:, 0:256].rearrange("p (e c) -> p e c", c=64)).then_inc(vector_done, 1), None if i == 0 else f"free.xs{i}.{q}.{k}")
                    if i == 0:
                        did(V, dve.tensor_copy(xs[:, k, :, 64:96], t[:, 256:384].rearrange("p (e c) -> p e c", c=32)).then_inc(vector_done, 1), f"free.xs{i}.{q}.{k}")

            onehot(0)
            take(0)

            def spread(part):
                for n, pre, j in spread_items(i, part):
                    sn, sm = (TX, SMX) if pre == "" else (TC, SMC)
                    t = tile(dve, f"pb{i}.{pre}{j}")
                    if later(dve, f"free.ab{i}.{pre}{j}"):
                        dve.wait_ge(*at(f"free.ab{i}.{pre}{j}"))
                    did(V, dve.scalar_tensor_tensor(sm[:, j, :], t[:, 0:sn], col("iop", 0 if pre == "" else 1),
                                                    AB[:, n % 2, 0:sn], ALU.is_equal, ALU.mult).then_inc(vector_done, 1), f"free.pb{i}.{pre}{j}")
            experts_vector(dve, i, onehot, take, spread)
            residual_vector(dve, f"mo{i}", segs, 40, NEXT[f"moe{i}"])

        def moe_pool(pool, i):
            if later(pool, f"xs{i}.3.{KT - 1}"):
                pool.wait_ge(*at(f"xs{i}.3.{KT - 1}"))
            for r in (0, 32):
                did("aux", pool.dma_start(sel[r:r + NE, :, :], a["sel"].rearrange("e (j p) -> e j p", p=P)).then_inc(constants_in, 16), f"sel{i}" if r else None, by=16)

        XX = S(0, KT, TA)
        XJ = S(6144, KT, TA)
        ST = [S(12288 + TA * n, TA) for n in range(10)]
        LH = S(12288 + 10 * TA, 2, TA)
        SQ, RN, AS0, AS1 = ST[5], ST[6], ST[8], ST[9]
        KS = [ST[7], S(12288 + 12 * TA, TA)]
        HALF = float(math.exp(-0.5))
        order = (1, 4, 2, 3, 0, 5)
        last_mm = {}

        def jsegs(j):
            return XSEG if j in (0, 5) else SEGS

        def rw_tensor(pe):
            def xj(j):
                return lambda k, s0, sn: XJ[:, k, s0:s0 + sn]

            def down(tag, wn, j, last_name):
                w = weight(pe, wn)
                for s0, sn in jsegs(j):
                    b = bank(pe, f"{tag}.{s0}")
                    for k in range(KT):
                        if later(pe, f"xj{j}.{k}"):
                            pe.wait_ge(*at(f"xj{j}.{k}"))
                        ins = pe.matmul(b[:, 0:sn], w[:, k, :], XJ[:, k, s0:s0 + sn], start=k == 0, stop=k == KT - 1)
                    did(T_, ins.then_inc(tensor_done, 1), f"{tag}.{s0}")
                marks["wf." + wn] = (T_, count[T_])
                marks[f"xjfree{j}"] = (T_, count[T_])

            down("lw", "w1", 1, None)
            w = weight(pe, "w2")
            for d in range(2):
                for m in range(KT):
                    for s0, sn in SEGS:
                        if later(pe, "free.lw.0"):
                            pe.wait_ge(*at("free.lw.0"))
                        if later(pe, "free.lw.512"):
                            pe.wait_ge(*at("free.lw.512"))
                        b = bank(pe, f"zw{d}.{m}.{s0}")
                        did(T_, pe.matmul(b[:, 0:sn], w[64 * d:64 * d + 64, 0, m * P:m * P + P],
                                          LH[64 * d:64 * d + 64, 0, s0:s0 + sn], start=True, stop=True).then_inc(tensor_done, 1), f"zw{d}.{m}.{s0}")
            marks["wf.w2"] = (T_, count[T_])
            down("la", "a1", 4, None)
            wa = weight(pe, "a2")
            for m in range(KT):
                w = weight(pe, f"wk.{m // 2}")
                for s0, sn in SEGS:
                    b = bank(pe, f"k.{m}.{s0}")
                    for k in range(KT):
                        if later(pe, f"xj2.{k}"):
                            pe.wait_ge(*at(f"xj2.{k}"))
                        ins = pe.matmul(b[:, 0:sn], w[:, k, (m % 2) * P:(m % 2) * P + P], XJ[:, k, s0:s0 + sn],
                                        start=k == 0, stop=k == KT - 1)
                    did(T_, ins.then_inc(tensor_done, 1), f"k.{m}.{s0}")
                if m % 2:
                    marks[f"wf.wk.{m // 2}"] = (T_, count[T_])
                for d in range(2):
                    for s0, sn in SEGS:
                        if later(pe, "free.la.0"):
                            pe.wait_ge(*at("free.la.0"))
                        if later(pe, "free.la.512"):
                            pe.wait_ge(*at("free.la.512"))
                        b = bank(pe, f"a{d}.{m}.{s0}")
                        did(T_, pe.matmul(b[:, 0:sn], wa[64 * d:64 * d + 64, 0, m * P:m * P + P],
                                          LH[64 * d:64 * d + 64, 1, s0:s0 + sn], start=True, stop=True).then_inc(tensor_done, 1), f"a{d}.{m}.{s0}")
                if m == KT - 1:
                    marks["xjfree2"] = (T_, count[T_])
                for s0, sn in SEGS:
                    if later(pe, f"ksq.{m}"):
                        pe.wait_ge(*at(f"ksq.{m}"))
                    b = bank(pe, f"kn.{m}.{s0}")
                    did(T_, pe.matmul(b[:, 0:sn], bones[:, :], SQ[:, s0:s0 + sn], start=True, stop=True).then_inc(tensor_done, 1), f"kn.{m}.{s0}")
            marks["wf.a2"] = (T_, count[T_])
            for tag, wn, j in (("v", "wv", 3), ("r", "wr", 0)):
                linear_tensor(pe, tag, wn, xj(j), jsegs(j), lambda k, j=j: f"xj{j}.{k}")
                marks[f"xjfree{j}"] = (T_, count[T_])
            down("lg", "g1", 5, None)
            w = weight(pe, "g2")
            for m in range(KT):
                if later(pe, "free.lg.0"):
                    pe.wait_ge(*at("free.lg.0"))
                b = bank(pe, f"g.{m}.0")
                did(T_, pe.matmul(b, w[:, 0, m * P:m * P + P], LH[:, 0, 0:TX], start=True, stop=True).then_inc(tensor_done, 1), f"g.{m}.0")
            marks["wf.g2"] = (T_, count[T_])

        def rw_vector(dve):

            def sub(k, o0, n, i0):
                did(V, dve.tensor_tensor(XX[:, k, o0:o0 + n], H[:, k, i0:i0 + n], H[:, k, o0:o0 + n], ALU.subtract).then_inc(vector_done, 1))

            def neg(out_, in_):
                did(V, dve.tensor_scalar(out_, in_, -1.0, None, ALU.mult).then_inc(vector_done, 1))
            for k in range(KT):
                if later(dve, f"n1.h{k}"):
                    dve.wait_ge(*at(f"n1.h{k}"))
                hx = H[:, k, 0:TX].rearrange("p (r c) -> p r c", c=64)
                xx = XX[:, k, 0:TX].rearrange("p (r c) -> p r c", c=64)
                if k < 2:
                    did(V, dve.tensor_tensor(xx[:, :, 1:64], hx[:, :, 0:63], hx[:, :, 1:64], ALU.subtract).then_inc(vector_done, 1))
                    neg(xx[:, :, 0:1], hx[:, :, 0:1])
                elif k < 4:
                    did(V, dve.tensor_tensor(xx[:, :, 0:63], hx[:, :, 1:64], hx[:, :, 0:63], ALU.subtract).then_inc(vector_done, 1))
                    neg(xx[:, :, 63:64], hx[:, :, 63:64])
                elif k < 6:
                    sub(k, 64, TX - 64, 0)
                    neg(XX[:, k, 0:64], H[:, k, 0:64])
                else:
                    sub(k, 0, TX - 64, 64)
                    neg(XX[:, k, TX - 64:TX], H[:, k, TX - 64:TX])
                if k < 4:
                    sub(k, TX + 1, TC - 1, TX)
                    neg(XX[:, k, TX:TX + 1], H[:, k, TX:TX + 1])
                else:
                    sub(k, TX, TC - 1, TX + 1)
                    neg(XX[:, k, TA - 1:TA], H[:, k, TA - 1:TA])
            dve.wait_ge(*own(dve, V))

            def mix(n):
                j = order[n]
                if n:
                    if later(dve, f"xjfree{order[n - 1]}"):
                        dve.wait_ge(*at(f"xjfree{order[n - 1]}"))
                w = TX if j in (0, 5) else TA
                for k in range(KT):
                    did(V, dve.scalar_tensor_tensor(XJ[:, k, 0:w], XX[:, k, 0:w], col("mix", 8 * j + k), H[:, k, 0:w],
                                                    ALU.mult, ALU.add).then_inc(vector_done, 1), f"xj{j}.{k}")
            mix(0)
            for d in range(2):
                for m in range(KT):
                    s = (d * KT + m) % 4
                    if later(dve, f"zs{d}.{m}"):
                        dve.wait_ge(*at(f"zs{d}.{m}"))
                    did(V, dve.tensor_scalar(ST[s], ST[s], -HALF, None, ALU.mult).then_inc(vector_done, 1), f"lw{d}.{m}")
                    if d == 0 and m == 0:
                        mix(1)
            mix(2)
            for m in range(KT):
                if m == KT - 1:
                    mix(3)
                if later(dve, f"as.{m}"):
                    dve.wait_ge(*at(f"as.{m}"))
                if later(dve, f"ks.{m}"):
                    dve.wait_ge(*at(f"ks.{m}"))
                if m:
                    for step in [f"s.{x}.{m - 1}" for x in ("kk", "kka0", "kka1", "kd0", "kd1")]:
                        if later(dve, step):
                            dve.wait_ge(*at(step))
                else:
                    if later(dve, "s.lw1.4"):
                        dve.wait_ge(*at("s.lw1.4"))
                    if later(dve, "s.lw1.5"):
                        dve.wait_ge(*at("s.lw1.5"))
                    if later(dve, "s.lw1.6"):
                        dve.wait_ge(*at("s.lw1.6"))
                    if later(dve, "s.lw1.7"):
                        dve.wait_ge(*at("s.lw1.7"))
                for d, AS in ((0, AS0), (1, AS1)):
                    did(V, dve.tensor_scalar(ST[3 + d], AS, col("ka", m), small[:, 32 + m:33 + m], ALU.mult, ALU.add).then_inc(vector_done, 1))
                dve.wait_ge(*own(dve, V))
                for d in range(2):
                    did(V, dve.tensor_tensor(ST[3 + d], ST[3 + d], KS[m % 2], ALU.mult).then_inc(vector_done, 1))
                if later(dve, f"rn.{m}"):
                    dve.wait_ge(*at(f"rn.{m}"))
                did(V, dve.reciprocal(RN, RN).then_inc(vector_done, 1))
                dve.wait_ge(*own(dve, V))
                did(V, dve.scalar_tensor_tensor(ST[0], KS[m % 2], col("kk", m), RN, ALU.mult, ALU.mult).then_inc(vector_done, 1))
                dve.wait_ge(*own(dve, V))
                for d, AS in ((0, AS0), (1, AS1)):
                    did(V, dve.tensor_tensor(ST[1 + d], ST[0], AS, ALU.mult).then_inc(vector_done, 1))
                marks[f"kout.{m}"] = (V, count[V])
            mix(4)
            mix(5)

        def stored(stream, m, s, w):
            return dram[stream][:, m, 0:w], ST[s][:, 0:w]

        def rw_scalar(act):
            def store_decay(n):
                d, m = divmod(n, KT)
                if later(act, f"lw{d}.{m}"):
                    act.wait_ge(*at(f"lw{d}.{m}"))
                did(f"sa{n % 4}", act.dma_start(*stored(f"lw{d}", m, n % 4, TA)).then_inc(sems[f"sa{n % 4}"], 16), f"s.lw{d}.{m}", by=16)

            def store_keys(m):
                if later(act, f"kout.{m}"):
                    act.wait_ge(*at(f"kout.{m}"))
                for s, stream in enumerate(("kk", "kka0", "kka1", "kd0", "kd1")):
                    did(f"sa{s}", act.dma_start(*stored(stream, m, s, TA)).then_inc(sems[f"sa{s}"], 16), f"s.{stream}.{m}", by=16)

            def lora(tag, row, func, segs):
                for s0, sn in segs:
                    t = tile(act, f"{tag}.{s0}")
                    did(A_, act.activation(LH[:, row, s0:s0 + sn], t[:, 0:sn], func).then_inc(scalar_done, 1), f"free.{tag}.{s0}")

            lora("lw", 0, ACT.Tanh, SEGS)
            for d in range(2):
                for m in range(KT):
                    n = d * KT + m
                    s = n % 4
                    if n >= 4:
                        if later(act, f"s.lw{(n - 4) // KT}.{(n - 4) % KT}"):
                            act.wait_ge(*at(f"s.lw{(n - 4) // KT}.{(n - 4) % KT}"))
                    for s0, sn in SEGS:
                        t = tile(act, f"zw{d}.{m}.{s0}")
                        did(A_, act.activation(ST[s][:, s0:s0 + sn], t[:, 0:sn], ACT.Sigmoid, bias=col("w0", 8 * d + m)).then_inc(scalar_done, 1), f"free.zw{d}.{m}.{s0}")
                    marks[f"zs{d}.{m}"] = (A_, count[A_])
                    if n % 2:
                        store_decay(n - 1)
            lora("la", 1, ACT.Copy, SEGS)
            for m in range(KT):
                if m >= 2:
                    if later(act, f"kout.{m - 2}"):
                        act.wait_ge(*at(f"kout.{m - 2}"))
                for s0, sn in SEGS:
                    t = tile(act, f"k.{m}.{s0}")
                    did(A_, act.activation(KS[m % 2][:, s0:s0 + sn], t[:, 0:sn], ACT.Copy).then_inc(scalar_done, 1), f"free.k.{m}.{s0}")
                marks[f"ks.{m}"] = (A_, count[A_])
                act.wait_ge(*own(act, A_))
                if m:
                    for step in [f"kn.{m - 1}.{s0}" for s0, _ in SEGS]:
                        if later(act, step):
                            act.wait_ge(*at(step))
                did(A_, act.activation(SQ, KS[m % 2], ACT.Square, scale=col("kk", m)).then_inc(scalar_done, 1), f"ksq.{m}")
                if m:
                    store_keys(m - 1)
                for d, AS in ((0, AS0), (1, AS1)):
                    for s0, sn in SEGS:
                        t = tile(act, f"a{d}.{m}.{s0}")
                        did(A_, act.activation(AS[:, s0:s0 + sn], t[:, 0:sn], ACT.Sigmoid, bias=col("a0", 8 * d + m)).then_inc(scalar_done, 1), f"free.a{d}.{m}.{s0}")
                marks[f"as.{m}"] = (A_, count[A_])
                for s0, sn in SEGS:
                    t = tile(act, f"kn.{m}.{s0}")
                    did(A_, act.activation(RN[:, s0:s0 + sn], t[:, 0:sn], ACT.Sqrt, bias=eps[:, 2:3]).then_inc(scalar_done, 1), f"free.kn.{m}.{s0}")
                marks[f"rn.{m}"] = (A_, count[A_])
            store_keys(KT - 1)
            if later(act, f"s.kd1.{KT - 1}"):
                act.wait_ge(*at(f"s.kd1.{KT - 1}"))
            if later(act, f"s.kd0.{KT - 1}"):
                act.wait_ge(*at(f"s.kd0.{KT - 1}"))
            if later(act, f"s.kka1.{KT - 1}"):
                act.wait_ge(*at(f"s.kka1.{KT - 1}"))
            if later(act, f"s.kka0.{KT - 1}"):
                act.wait_ge(*at(f"s.kka0.{KT - 1}"))
            if later(act, f"s.kk.{KT - 1}"):
                act.wait_ge(*at(f"s.kk.{KT - 1}"))
            n = 0
            for tag in ("v", "r", "g"):
                if tag == "g":
                    lora("lg", 0, ACT.Sigmoid, XSEG)
                for m in range(KT):
                    s = n % 4
                    if n >= 4:
                        if later(act, f"s.{'vrg'[(n - 4) // KT]}.{(n - 4) % KT}"):
                            act.wait_ge(*at(f"s.{'vrg'[(n - 4) // KT]}.{(n - 4) % KT}"))
                    for s0, sn in SEGS if tag == "v" else XSEG:
                        t = tile(act, f"{tag}.{m}.{s0}")
                        did(A_, act.activation(ST[s][:, s0:s0 + sn], t[:, 0:sn], ACT.Copy).then_inc(scalar_done, 1), f"free.{tag}.{m}.{s0}")
                    marks[f"{tag}o.{m}"] = (A_, count[A_])
                    n += 1

        def rw_pool(pool):
            def store(stream, m, s, w, after):
                if later(pool, after):
                    pool.wait_ge(*at(after))
                did(f"st{s}", pool.dma_start(*stored(stream, m, s, w)).then_inc(sems[f"st{s}"], 16), f"s.{stream}.{m}", by=16)
            for n in range(1, 2 * KT, 2):
                d, m = divmod(n, KT)
                store(f"lw{d}", m, n % 4, TA, f"lw{d}.{m}")
            n = 0
            for tag in ("v", "r", "g"):
                for m in range(KT):
                    store(tag, m, n % 4, TA if tag == "v" else TX, f"{tag}o.{m}")
                    n += 1
            for s in range(4):
                pool.wait_ge(sems[f"st{s}"], count[f"st{s}"])
            for step in [f"s.{x}.{KT - 1}" for x in ("kk", "kka0", "kka1", "kd0", "kd1")]:
                if later(pool, step):
                    pool.wait_ge(*at(step))

        LD = H[:, :, :].rearrange("p k t -> p (k t)").rearrange("p (b s n) -> p b s n", b=2, s=6)
        off = 0

        def take_scr(*dims):
            nonlocal off
            t = S(off, *dims)
            off += int(np.prod(dims))
            return t
        YA = take_scr(KT, TX)
        EP, EN, EM, CS = (take_scr(512) for _ in range(4))
        BK = [take_scr(KT, 2, CH) for _ in range(2)]
        AR = [[take_scr(KT, 2, CH) for _ in range(2)],
              [X[:, :, TX + 128 * d:TX + 128 * d + 128].rearrange("p k (s t) -> p k s t", s=2) for d in range(2)]]

        def held(n, off, *dims):
            t = ring[:, place[f"hold.{n}"][0], off:off + int(np.prod(dims))]
            return t.rearrange("p (a b) -> p a b", b=dims[1])
        SC = [take_scr(NE, 128), held(0, 0, NE, 128)]
        NM4 = [take_scr(LEVELS * 8, CH), None]
        NM = [[NM4[0][:, 8 * l:8 * l + 8, :] for l in range(LEVELS)],
              [held(1 + l // 4, (l % 4) * 512, 8, CH) for l in range(LEVELS)]]
        XI, XT, GT, QB = ([take_scr(8, CH), held(3, 512 * n, 8, CH)] for n in range(4))
        BKT = [take_scr(NE, CH), held(2, 1024, NE, CH)]
        SV = [take_scr(NE, CH), held(4, 0, NE, CH)]
        ZS = [take_scr(8, CH) for _ in range(2)]
        MD = take_scr(2, 128)
        LM = take_scr(2, LEVELS * CH)
        RST = take_scr(512)
        PT = take_scr(4, 8)

        def units():
            for step in range(NCH):
                pair = []
                for d in range(2):
                    s = step - NCHC
                    if s < 0:
                        c = NCHX + (step if d == 0 else NCHC - 1 - step)
                    else:
                        c = s if d == 0 else NCHX - 1 - s
                    pair.append((2 * step + d, d, c, s >= 0, s < NCHX // 2))
                yield pair

        def rows(q):
            return slice(64 * q, 64 * q + 64)

        def odd(t, q):
            return t.rearrange("p (j q) c -> p j q c", q=2)[:, :, q, :]

        def pairs(t):
            return t[:, 0:256].rearrange("p (j c) -> p j c", c=CH)

        def chunk_streams(d, img):
            names = [f"kd{d}", "v", "kk", f"kka{d}", f"lw{d}"] + (["r"] if img else [])
            return sorted(enumerate(names), key=lambda x: x[0] != 4)

        def wkv_pool(pool):
            def loads(u, d, c, img, first):
                if u >= 2:
                    if later(pool, f"til{u - 2}"):
                        pool.wait_ge(*at(f"til{u - 2}"))
                    if later(pool, f"V{u - 2}.1"):
                        pool.wait_ge(*at(f"V{u - 2}.1"))
                for n, s in chunk_streams(d, img):
                    did(f"ld{d}", pool.dma_start(LD[:, d, n, :].rearrange("p (k t) -> p k t", t=CH),
                                                          dram[s][:, :, c * CH:c * CH + CH]).then_inc(sems[f"ld{d}"], 16), by=16)
                marks[f"ld{u}"] = (f"ld{d}", count[f"ld{d}"])
            steps = list(units())
            if later(pool, "wkvc"):
                pool.wait_ge(*at("wkvc"))
            for n, pair in enumerate(steps):
                for l in range(LEVELS):
                    for u, d, c, img, first in pair:
                        if later(pool, f"sc{u}.3"):
                            pool.wait_ge(*at(f"sc{u}.3"))
                        for q in range(2):
                            did(G_, pool.tensor_tensor(
                                NM[d][l][rows(1 - q)], odd(SC[d][rows(1 - q)], q)[:, :, 0:CH],
                                LM[rows(1 - q), d, l * CH:l * CH + CH].unsqueeze(1).to_broadcast([64, 8, CH]), ALU.mult).then_inc(pool_done, 1))
                        marks[f"nm{u}.{l}"] = (G_, count[G_])
                    if n + 1 < len(steps) and l in (2, 3):
                        loads(*steps[n + 1][l - 2])

        def wkv_scalar(act):
            def exps(u, d, c, img, first):
                if u:
                    if later(act, f"til{u - 1}"):
                        act.wait_ge(*at(f"til{u - 1}"))
                if later(act, f"cs{u}"):
                    act.wait_ge(*at(f"cs{u}"))
                did(A_, act.activation(EM, EM, ACT.Exp).then_inc(scalar_done, 1))
                did(A_, act.activation(EN, CS, ACT.Exp, scale=-1.0).then_inc(scalar_done, 1))
                did(A_, act.activation(EP, CS, ACT.Exp).then_inc(scalar_done, 1), f"exps{u}")
            steps = list(units())
            did("sa0", act.dma_start(RST, a["rst"]).then_inc(sems["sa0"], 16), by=16)
            did("sa0", act.dma_start(MD[:, :, :], a["md"].rearrange("p (d c) -> p d c", d=2)).then_inc(sems["sa0"], 16), by=16)
            did("sa0", act.dma_start(LM[:, :, :], a["lm"].rearrange("p (d c) -> p d c", d=2)).then_inc(sems["sa0"], 16), "wkvc", by=16)
            for u, d, c, img, first in steps[0]:
                for n, s in chunk_streams(d, False):
                    did(f"sa{1 + d}", act.dma_start(LD[:, d, n, :].rearrange("p (k t) -> p k t", t=CH),
                                                dram[s][:, :, c * CH:c * CH + CH]).then_inc(sems[f"sa{1 + d}"], 16), by=16)
                marks[f"ld{u}"] = (f"sa{1 + d}", count[f"sa{1 + d}"])
            exps(*steps[0][0])
            exps(*steps[0][1])
            for n, pair in enumerate(steps):
                for u, d, c, img, first in pair:
                    for q in range(2):
                        t = tile(act, f"T{u}.{q}")
                        did(A_, act.activation(odd(BKT[d], q), t.rearrange("p (h c) -> p h c", c=CH), ACT.Copy).then_inc(scalar_done, 1), f"free.T{u}.{q}")
                for l in range(1, LEVELS):
                    for u, d, c, img, first in pair:
                        for g in range(2):
                            t = tile(act, f"G{u}.{l}.{g}")
                            did(A_, act.activation(GT[d][:, 4 * g:4 * g + 4, :], pairs(t), ACT.Copy).then_inc(scalar_done, 1), f"free.G{u}.{l}.{g}")
                    if n + 1 < len(steps) and l >= 4:
                        exps(*steps[n + 1][l - 4])
                for u, d, c, img, first in pair:
                    for g in range(2):
                        t = tile(act, f"Q{u}.{g}")
                        did(A_, act.activation(QB[d][:, 4 * g:4 * g + 4, :], pairs(t), ACT.Copy).then_inc(scalar_done, 1), f"free.Q{u}.{g}")
                for u, d, c, img, first in pair:
                    for g in range(2):
                        t = pairs(tile(act, f"S{u}.{g}"))
                        for q in range(2):
                            did(A_, act.activation(odd(SV[d][rows(1 - q), 8 * g:8 * g + 8, :], q), t[rows(1 - q)], ACT.Copy).then_inc(scalar_done, 1))
                        marks[f"free.S{u}.{g}"] = (A_, count[A_])

        def wkv_vector(dve):
            did(V, dve.memset(ZS[0][:, :, :], 0.0).then_inc(vector_done, 1))
            did(V, dve.memset(ZS[1][:, :, :], 0.0).then_inc(vector_done, 1), "z0")
            if later(dve, "wkvc"):
                dve.wait_ge(*at("wkvc"))
            dve.wait_ge(*own(dve, V))

            def v3(t):
                return t.rearrange("p (j t) -> p j t", t=CH)

            def flat(t):
                return t.rearrange("p j t -> p (j t)")

            def scan(u, d, c, img, first):
                if later(dve, f"ld{u}"):
                    dve.wait_ge(*at(f"ld{u}"))
                ld = LD[:, d]
                cs, lw = (CS, ld[:, 4, :]) if d == 0 else (CS[:, ::-1], ld[:, 4, ::-1])
                did(V, dve.tensor_tensor_scan(cs, RST, lw, 0.0, ALU.mult, ALU.add).then_inc(vector_done, 1))
                dve.wait_ge(*own(dve, V))
                did(V, dve.tensor_tensor(EM, CS, ld[:, 4, :], ALU.subtract).then_inc(vector_done, 1), f"cs{u}")

            def tildes(u, d, c, img, first):
                ld = LD[:, d]
                if later(dve, f"exps{u}"):
                    dve.wait_ge(*at(f"exps{u}"))
                if u >= 2:
                    if later(dve, f"T{u - 2}.1"):
                        dve.wait_ge(*at(f"T{u - 2}.1"))
                b, r = BK[d], AR[(u // 2) % 2][d]
                did(V, dve.scalar_tensor_tensor(r[:, :, 0, :], v3(ld[:, 2, :]), -1.0, v3(EM), ALU.mult, ALU.mult).then_inc(vector_done, 1))
                if img:
                    did(V, dve.tensor_tensor(r[:, :, 1, :], v3(ld[:, 5, :]), v3(EP), ALU.mult).then_inc(vector_done, 1))
                for q in range(2):
                    did(V, dve.tensor_tensor(b[rows(q), :, 1 - q, :], v3(ld[rows(q), 3, :]), v3(EN[rows(q)]), ALU.mult).then_inc(vector_done, 1))
                    did(V, dve.tensor_tensor(b[rows(q), :, q, :], v3(ld[rows(q), 0, :]), v3(EN[rows(q)]), ALU.mult).then_inc(vector_done, 1))
                e = CH - 1 if d == 0 else 0
                did(V, dve.tensor_copy(PT[:, u % 4, :], v3(EP)[:, :, e]).then_inc(vector_done, 1), f"til{u}")

            steps = list(units())
            for un in steps[0]:
                scan(*un)
                tildes(*un)
            idb = id64[:, :].unsqueeze(1).to_broadcast([P, 8, CH])
            for n, pair in enumerate(steps):
                for u, d, c, img, first in pair:
                    for b4 in range(4):
                        t = tile(dve, f"A{u}.{b4}").rearrange("p (h c) -> p h c", c=128)
                        w = 128 if img else CH
                        g, q = divmod(b4, 2)
                        did(V, dve.tensor_tensor(odd(SC[d][:, 8 * g:8 * g + 8, :], q)[:, :, 0:w], t[:, :, 0:w],
                                                 MD[:, d, 0:w].unsqueeze(1).to_broadcast([P, 4, w]), ALU.mult).then_inc(vector_done, 1), f"sc{u}.{b4}")
                        marks[f"free.A{u}.{b4}"] = (V, count[V])
                for u, d, c, img, first in pair:
                    if later(dve, f"nm{u}.0"):
                        dve.wait_ge(*at(f"nm{u}.0"))
                    did(V, dve.tensor_tensor(XI[d][:, :, :], NM[d][0], idb, ALU.add).then_inc(vector_done, 1), f"xi{u}.0.0")
                    marks[f"xi{u}.0.1"] = marks[f"xi{u}.0.0"]
                    dve.wait_ge(*own(dve, V))
                    did(V, dve.transpose(flat(XT[d][:, :, :]), flat(XI[d][:, :, :])).then_inc(vector_done, 1), f"xt{u}.0.0")
                    marks[f"xt{u}.0.1"] = marks[f"xt{u}.0.0"]
                for u, d, c, img, first in pair:
                    for g in range(2):
                        t = tile(dve, f"V{u}.{g}")[0:64, :].rearrange("p (j q c) -> p j q c", q=2, c=CH)
                        for q in range(2):
                            did(V, dve.tensor_copy(odd(SV[d][rows(q), 8 * g:8 * g + 8, :], q), t[:, :, q, :]).then_inc(vector_done, 1))
                        marks[f"free.V{u}.{g}"] = (V, count[V])
                for l in range(1, LEVELS):
                    for u, d, c, img, first in pair:
                        for g in range(2):
                            t = pairs(tile(dve, f"P{u}.{l}.{g}"))
                            x = XI[d][:, 4 * g:4 * g + 4, :]
                            did(V, dve.tensor_tensor(x, t, x, ALU.add).then_inc(vector_done, 1), f"xi{u}.{l}.{g}")
                            marks[f"free.P{u}.{l}.{g}"] = (V, count[V])
                        if l < LEVELS - 1:
                            dve.wait_ge(*own(dve, V))
                            for g in range(2):
                                did(V, dve.transpose(flat(XT[d][:, 4 * g:4 * g + 4, :]),
                                                     flat(XI[d][:, 4 * g:4 * g + 4, :])).then_inc(vector_done, 1), f"xt{u}.{l}.{g}")
                    if n + 1 < len(steps):
                        if l >= 4:
                            tildes(*steps[n + 1][l - 4])
                        if l in (3, 4):
                            scan(*steps[n + 1][l - 3])
                if img:
                    for u, d, c, img, first in pair:
                        for g in range(2):
                            t = pairs(tile(dve, f"Y{u}.{g}"))
                            y = YA[:, 4 * g:4 * g + 4, c * CH:c * CH + CH]
                            ins = dve.tensor_copy(y, t) if first else dve.tensor_tensor(y, t, y, ALU.add)
                            did(V, ins.then_inc(vector_done, 1), f"free.Y{u}.{g}")
                for u, d, c, img, first in pair:
                    for g in range(2):
                        t = pairs(tile(dve, f"Z{u}.{g}"))
                        z = ZS[d][:, 4 * g:4 * g + 4, :]
                        did(V, dve.tensor_tensor(z, t, z, ALU.add).then_inc(vector_done, 1), f"free.Z{u}.{g}")
                dve.wait_ge(*own(dve, V))
                for u, d, c, img, first in pair:
                    z = ZS[d][:, :, :]
                    did(V, dve.tensor_tensor(z, z, PT[:, u % 4, :].unsqueeze(2).to_broadcast([P, 8, CH]), ALU.mult).then_inc(vector_done, 1), f"zn{u}")

        def wkv_tensor(pe):
            def each(g):
                return [(j, q, slice((j % 4) * CH, (j % 4) * CH + CH)) for j in range(4 * g, 4 * g + 4) for q in range(2)]

            for pair in units():
                for u, d, c, img, first in pair:
                    bk, ar = BK[d], AR[(u // 2) % 2][d]
                    if later(pe, f"til{u}"):
                        pe.wait_ge(*at(f"til{u}"))
                    if later(pe, "z0"):
                        pe.wait_ge(*at("z0"))
                    w = 128 if img else CH
                    for g in range(2):
                        for q in range(2):
                            b = bank(pe, f"A{u}.{2 * g + q}")
                            for n, j in enumerate(range(4 * g, 4 * g + 4)):
                                ins = pe.matmul(b[:, n * 128:n * 128 + w], bk[rows(q), j, :, :],
                                                ar[rows(q), j, :, :] if img else ar[rows(q), j, 0, :], start=True, stop=True)
                            did(T_, ins.then_inc(tensor_done, 1), f"A{u}.{2 * g + q}")
                for u, d, c, img, first in pair:
                    for q in range(2):
                        b = bank(pe, f"T{u}.{q}")
                        for j in range(8):
                            ins = pe.transpose(b[:, j * CH:j * CH + CH], BK[d][rows(q), j, :, :], ident[rows(q), rows(q)])
                        did(T_, ins.then_inc(tensor_done, 1), f"T{u}.{q}")
                for u, d, c, img, first in pair:
                    for g in range(2):
                        b = bank(pe, f"V{u}.{g}")
                        for j in range(4):
                            o = (4 * g + j) * CH
                            ins = pe.transpose(b[0:64, j * P:j * P + P], LD[:, d, 1, o:o + CH], ident[:, :])
                        did(T_, ins.then_inc(tensor_done, 1), f"V{u}.{g}")
                for l in range(1, LEVELS):
                    for u, d, c, img, first in pair:
                        if later(pe, f"nm{u}.{l}"):
                            pe.wait_ge(*at(f"nm{u}.{l}"))
                        for g in range(2):
                            b = bank(pe, f"G{u}.{l}.{g}")
                            if later(pe, f"xt{u}.{l - 1}.{g}"):
                                pe.wait_ge(*at(f"xt{u}.{l - 1}.{g}"))
                            for j, q, o in each(g):
                                ins = pe.matmul(b[rows(q), o], NM[d][l][rows(q), j, :], XT[d][rows(q), j, :],
                                                start=True, stop=True)
                            did(T_, ins.then_inc(tensor_done, 1), f"G{u}.{l}.{g}")
                    for u, d, c, img, first in pair:
                        for g in range(2):
                            b = bank(pe, f"P{u}.{l}.{g}")
                            if later(pe, f"free.G{u}.{l}.{g}"):
                                pe.wait_ge(*at(f"free.G{u}.{l}.{g}"))
                            if later(pe, f"xi{u}.{l - 1}.{g}"):
                                pe.wait_ge(*at(f"xi{u}.{l - 1}.{g}"))
                            for j, q, o in each(g):
                                ins = pe.matmul(b[rows(q), o], GT[d][rows(q), j, :], XI[d][rows(q), j, :],
                                                start=True, stop=True)
                            did(T_, ins.then_inc(tensor_done, 1), f"P{u}.{l}.{g}")
                for u, d, c, img, first in pair:
                    ar = AR[(u // 2) % 2][d]
                    if later(pe, f"free.V{u}.0"):
                        pe.wait_ge(*at(f"free.V{u}.0"))
                    if later(pe, f"free.V{u}.1"):
                        pe.wait_ge(*at(f"free.V{u}.1"))
                    for step in [f"zn{u - 2}"] if u >= 2 else []:
                        if later(pe, step):
                            pe.wait_ge(*at(step))
                    for g in range(2):
                        b = bank(pe, f"Q{u}.{g}")
                        for j, q, o in each(g):
                            pe.matmul(b[rows(1 - q), o], ar[rows(q), j, 0, :], ZS[d][rows(q), j, :], start=True, stop=False)
                            ins = pe.matmul(b[rows(1 - q), o], SC[d][rows(q), 2 * j + q, 0:CH],
                                            SV[d][rows(q), 2 * j + q, :], start=False, stop=True)
                        did(T_, ins.then_inc(tensor_done, 1), f"Q{u}.{g}")
                for u, d, c, img, first in pair:
                    for g in range(2):
                        b = bank(pe, f"S{u}.{g}")
                        if later(pe, f"free.Q{u}.{g}"):
                            pe.wait_ge(*at(f"free.Q{u}.{g}"))
                        if later(pe, f"xi{u}.{LEVELS - 1}.{g}"):
                            pe.wait_ge(*at(f"xi{u}.{LEVELS - 1}.{g}"))
                        for j, q, o in each(g):
                            ins = pe.matmul(b[rows(q), o], XI[d][rows(q), j, :], QB[d][rows(q), j, :], start=True, stop=True)
                        did(T_, ins.then_inc(tensor_done, 1), f"S{u}.{g}")
                if img:
                    for u, d, c, img, first in pair:
                        ar = AR[(u // 2) % 2][d]
                        for g in range(2):
                            b = bank(pe, f"Y{u}.{g}")
                            if later(pe, f"free.S{u}.{g}"):
                                pe.wait_ge(*at(f"free.S{u}.{g}"))
                            for j, q, o in each(g):
                                pe.matmul(b[rows(q), o], ZS[d][rows(q), j, :], ar[rows(q), j, 1, :], start=True, stop=False)
                                ins = pe.matmul(b[rows(q), o], SV[d][:, 2 * j + q, :], SC[d][:, 2 * j + q, CH:2 * CH],
                                                start=False, stop=True)
                            did(T_, ins.then_inc(tensor_done, 1), f"Y{u}.{g}")
                for u, d, c, img, first in pair:
                    for g in range(2):
                        b = bank(pe, f"Z{u}.{g}")
                        if later(pe, f"free.S{u}.{g}"):
                            pe.wait_ge(*at(f"free.S{u}.{g}"))
                        if later(pe, f"free.T{u}.1"):
                            pe.wait_ge(*at(f"free.T{u}.1"))
                        for j, q, o in each(g):
                            ins = pe.matmul(b[rows(q), o], BKT[d][:, 2 * j + q, :], SV[d][:, 2 * j + q, :],
                                            start=True, stop=True)
                        did(T_, ins.then_inc(tensor_done, 1), f"Z{u}.{g}")
            for n in range(5):
                marks[f"wf.hold.{n}"] = (T_, count[T_])

        PL = [S(4096 + 2560 * b, 5, 512) for b in range(4)]
        PW = [[S(14336 + 2560 * b + 512 * n, 512) for n in range(5)] for b in range(2)]

        def post_pool(pool):
            for m in range(KT):
                YC, BV = PW[m % 2][1], PW[m % 2][4]
                if later(pool, f"pl.{m}"):
                    pool.wait_ge(*at(f"pl.{m}"))
                if later(pool, f"yn.{m}"):
                    pool.wait_ge(*at(f"yn.{m}"))
                if later(pool, f"free.bo.{m}"):
                    pool.wait_ge(*at(f"free.bo.{m}"))
                did(G_, pool.tensor_tensor(YC, YC, BV, ALU.add).then_inc(pool_done, 1))
                pool.wait_ge(*own(pool, G_))
                did(G_, pool.tensor_tensor(YA[:, m, :], YC, PL[m % 4][:, 4, :], ALU.mult).then_inc(pool_done, 1), f"yo.{m}")

        def post_vector(dve):
            def centre(m):
                BS, YC, YQ, SD, BV = PW[m % 2]
                t = tile(dve, f"mu.{m}")
                if m >= 2:
                    if later(dve, f"yo.{m - 2}"):
                        dve.wait_ge(*at(f"yo.{m - 2}"))
                did(V, dve.scalar_tensor_tensor(YC, t, -1.0 / 64, YA[:, m, :], ALU.mult, ALU.add).then_inc(vector_done, 1), f"free.mu.{m}")
                t = tile(dve, f"bo.{m}")
                did(V, dve.tensor_tensor(BV, t, PL[m % 4][:, 3, :], ALU.mult).then_inc(vector_done, 1), f"free.bo.{m}")

            def bonus(m):
                if later(dve, f"pl.{m}"):
                    dve.wait_ge(*at(f"pl.{m}"))
                if m >= 2:
                    if later(dve, f"bo.{m - 2}"):
                        dve.wait_ge(*at(f"bo.{m - 2}"))
                pl = PL[m % 4]
                did(V, dve.tensor_tensor(pl[:, 1, :], pl[:, 1, :], pl[:, 2, :], ALU.add).then_inc(vector_done, 1))
                dve.wait_ge(*own(dve, V))
                did(V, dve.scalar_tensor_tensor(PW[m % 2][0], PL[m % 4][:, 1, :], col("rk", m), PL[m % 4][:, 0, :],
                                                ALU.mult, ALU.mult).then_inc(vector_done, 1), f"bs.{m}")
            bonus(0)
            bonus(1)
            centre(0)
            for m in range(KT):
                BS, YC, YQ, SD, BV = PW[m % 2]
                if m + 1 < KT:
                    centre(m + 1)
                if m + 2 < KT:
                    bonus(m + 2)
                if later(dve, f"free.va.{m}"):
                    dve.wait_ge(*at(f"free.va.{m}"))
                did(V, dve.reciprocal(SD, SD).then_inc(vector_done, 1))
                dve.wait_ge(*own(dve, V))
                did(V, dve.tensor_tensor(YC, YC, SD, ALU.mult).then_inc(vector_done, 1), f"yd.{m}")
            residual_vector(dve, "wo", XSEG, 16, NEXT["post"])

        def post_scalar(act):
            def loads(m):
                for n, s in enumerate(("r", "kd0", "kd1", "v", "g")):
                    did(f"sa{m % 4}", act.dma_start(PL[m % 4][:, n, :], dram[s][:, m, 0:TX]).then_inc(sems[f"sa{m % 4}"], 16), by=16)
                marks[f"pl.{m}"] = (f"sa{m % 4}", count[f"sa{m % 4}"])

            def square(m):
                if later(act, f"free.mu.{m}"):
                    act.wait_ge(*at(f"free.mu.{m}"))
                if m >= 2:
                    if later(act, f"va.{m - 2}"):
                        act.wait_ge(*at(f"va.{m - 2}"))
                did(A_, act.activation(PW[m % 2][2], PW[m % 2][1], ACT.Square).then_inc(scalar_done, 1), f"yq.{m}")

            def root(m):
                t = tile(act, f"va.{m}")
                if m >= 2:
                    if later(act, f"yd.{m - 2}"):
                        act.wait_ge(*at(f"yd.{m - 2}"))
                did(A_, act.activation(PW[m % 2][3], t, ACT.Sqrt, bias=eps[:, 1:2], scale=1.0 / 64).then_inc(scalar_done, 1), f"free.va.{m}")
            for m in range(4):
                loads(m)
            square(0)
            root(0)
            for m in range(KT):
                if m + 1 < KT:
                    square(m + 1)
                YC = PW[m % 2][1]
                if later(act, f"yd.{m}"):
                    act.wait_ge(*at(f"yd.{m}"))
                did(A_, act.activation(YC, YC, ACT.Identity, bias=col("lnb", m), scale=col("lnw", m)).then_inc(scalar_done, 1), f"yn.{m}")
                if 0 < m < KT - 3:
                    if later(act, f"yo.{m - 1}"):
                        act.wait_ge(*at(f"yo.{m - 1}"))
                    loads(m + 3)
                if m + 1 < KT:
                    root(m + 1)
            residual_scalar(act, "wo", XSEG, NEXT["post"])

        def post_tensor(pe):
            def one(key, src, after=None):
                b = bank(pe, key)
                if after:
                    if later(pe, after):
                        pe.wait_ge(*at(after))
                did(T_, pe.matmul(b, bones[:, :], src, start=True, stop=True).then_inc(tensor_done, 1), key)
            one("mu.0", YA[:, 0, :])
            one("bo.0", PW[0][0], "bs.0")
            for m in range(KT):
                if m + 1 < KT:
                    one(f"mu.{m + 1}", YA[:, m + 1, :])
                    one(f"bo.{m + 1}", PW[(m + 1) % 2][0], f"bs.{m + 1}")
                one(f"va.{m}", PW[m % 2][2], f"yq.{m}")
            linear_tensor(pe, "wo", "wo", lambda k, s0, sn: YA[:, k, s0:s0 + sn], XSEG, lambda k: f"yo.{k}")

        MIX = S(0, KT, TX)
        CQ = S(4096, 3, TX)
        CKV = S(5632, 2, TX)
        QT = S(6656, 6, TX)
        KTT = S(9728, 6, TX)
        VT = S(12800, 4, 384)
        PB = S(14336, 2, 512)
        PTT = S(15360, 2, 512)
        TR = S(16384, 2, 512)
        TQ = S(17408, 5, 512)
        RC = S(19968, 2, 512)
        KW = S(20992, 512)
        NEG = S(21504, P)
        AST = S(21632, 4, 24)
        SCALE = 1.0 / math.sqrt(96.0)
        HR = slice(64, 96)
        ORDER = [(h, i) for h in range(6) for i in range(4)]

        def mla_pool(pool, l):
            did("aux", pool.dma_start(TR[HR, :, :], a["rope"].rearrange("p (s t) -> p s t", s=2)).then_inc(constants_in, 16), by=16)
            did("aux", pool.dma_start(NEG, a["neg"]).then_inc(constants_in, 16), f"mlac{l}", by=16)

        def mla_tensor(pe, l):
            t0 = f"i{l}."
            hk = f"n2{l}"
            for m in range(3):
                w = weight(pe, f"{t0}cq.{m // 2}")
                b = bank(pe, f"{t0}cq{m}")
                for k in range(KT):
                    if later(pe, f"{hk}.h{k}"):
                        pe.wait_ge(*at(f"{hk}.h{k}"))
                    ins = pe.matmul(b, w[:, k, (m % 2) * P:(m % 2) * P + P], H[:, k, 0:TX], start=k == 0, stop=k == KT - 1)
                did(T_, ins.then_inc(tensor_done, 1), f"{t0}cq{m}")
                if m:
                    marks[f"wf.{t0}cq.{m // 2}"] = (T_, count[T_])
            marks[f"wf.{t0}cq.0"] = marks[f"wf.{t0}cq.0"] if f"wf.{t0}cq.0" in marks else (T_, count[T_])
            w = weight(pe, f"{t0}ckv")
            for m in range(2):
                b = bank(pe, f"{t0}ckv{m}")
                for k in range(KT):
                    ins = pe.matmul(b, w[:, k, m * P:m * P + P], H[:, k, 0:TX], start=k == 0, stop=k == KT - 1)
                did(T_, ins.then_inc(tensor_done, 1), f"{t0}ckv{m}")
            marks[f"wf.{t0}ckv"] = (T_, count[T_])
            w = weight(pe, f"{t0}kr")
            for s in range(2):
                b = bank(pe, f"{t0}kr{s}")
                for k in range(KT):
                    ins = pe.matmul(b[HR, :], w[:, k, 32 * s:32 * s + 32], H[:, k, 0:TX], start=k == 0, stop=k == KT - 1)
                did(T_, ins.then_inc(tensor_done, 1), f"{t0}kr{s}")
            marks[f"wf.{t0}kr"] = (T_, count[T_])
            for nm, n in (("cq", 3), ("ckv", 2)):
                b = bank(pe, f"{t0}s{nm}")
                for m in range(n):
                    if later(pe, f"{t0}q{nm}{m}"):
                        pe.wait_ge(*at(f"{t0}q{nm}{m}"))
                    ins = pe.matmul(b, ones[:, :], TQ[:, m + (3 if nm == "ckv" else 0), :], start=m == 0, stop=m == n - 1)
                did(T_, ins.then_inc(tensor_done, 1), f"{t0}s{nm}")
            w = weight(pe, f"{t0}qb")
            w2 = weight(pe, f"{t0}qs")
            for h in range(6):
                b = bank(pe, f"{t0}q{h}")
                b2 = bank(pe, f"{t0}qw{h}")
                if later(pe, f"{t0}ncq"):
                    pe.wait_ge(*at(f"{t0}ncq"))
                for k in range(3):
                    ins = pe.matmul(b[0:96, :], w[:, k, 96 * h:96 * h + 96], CQ[:, k, :], start=k == 0, stop=k == 2)
                did(T_, ins.then_inc(tensor_done, 1), f"{t0}q{h}")
                for k in range(3):
                    ins = pe.matmul(b2[HR, :], w2[:, k, 32 * h:32 * h + 32], CQ[:, k, :], start=k == 0, stop=k == 2)
                did(T_, ins.then_inc(tensor_done, 1), f"{t0}qw{h}")
            marks[f"wf.{t0}qb"] = (T_, count[T_])
            marks[f"wf.{t0}qs"] = (T_, count[T_])
            w = weight(pe, f"{t0}kvb")
            if later(pe, f"{t0}nckv"):
                pe.wait_ge(*at(f"{t0}nckv"))
            for h in range(6):
                b = bank(pe, f"{t0}k{h}")
                for k in range(2):
                    ins = pe.matmul(b[0:64, :], w[:, k, 128 * h:128 * h + 64], CKV[:, k, :], start=k == 0, stop=k == 1)
                did(T_, ins.then_inc(tensor_done, 1), f"{t0}k{h}")
            for tt in range(4):
                b = bank(pe, f"{t0}vt{tt}")
                for k in range(2):
                    rhs = w[:, k, :].rearrange("p (h s c) -> p h s c", s=2, c=64)[:, :, 1, :]
                    ins = pe.matmul(b[:, 0:384].rearrange("p (h c) -> p h c", c=64), CKV[:, k, tt * P:tt * P + P], rhs,
                                    start=k == 0, stop=k == 1)
                did(T_, ins.then_inc(tensor_done, 1), f"{t0}vt{tt}")
            marks[f"wf.{t0}kvb"] = (T_, count[T_])

            def score(n):
                h, i = ORDER[n]
                if later(pe, f"{t0}qt{h}"):
                    pe.wait_ge(*at(f"{t0}qt{h}"))
                if later(pe, f"{t0}kt{h}"):
                    pe.wait_ge(*at(f"{t0}kt{h}"))
                if later(pe, f"mlac{l}"):
                    pe.wait_ge(*at(f"mlac{l}"))
                b = bank(pe, f"{t0}sc{n}")
                w = (i + 1) * P
                pe.matmul(b[:, 0:w], QT[0:96, h, i * P:i * P + P], KTT[0:96, h, 0:w], start=True, stop=False)
                did(T_, pe.matmul(b[:, i * P:w], ident[:, :], NEG, start=False, stop=True).then_inc(tensor_done, 1), f"{t0}sc{n}")

            def turn(n):
                h, i = ORDER[n]
                if later(pe, f"{t0}pn{n}"):
                    pe.wait_ge(*at(f"{t0}pn{n}"))
                b = bank(pe, f"{t0}pt{n}")
                for j in range(i + 1):
                    ins = pe.transpose(b[:, j * P:j * P + P], PB[:, n % 2, j * P:j * P + P], ident[:, :])
                did(T_, ins.then_inc(tensor_done, 1), f"{t0}pt{n}")

            def value(n):
                h, i = ORDER[n]
                if later(pe, f"free.{t0}pt{n}"):
                    pe.wait_ge(*at(f"free.{t0}pt{n}"))
                if later(pe, f"free.{t0}vt3"):
                    pe.wait_ge(*at(f"free.{t0}vt3"))
                b = bank(pe, f"{t0}o{n}")
                for j in range(i + 1):
                    ins = pe.matmul(b[rows(h % 2), 0:P], VT[:, j, 64 * h:64 * h + 64], PTT[:, n % 2, j * P:j * P + P],
                                    start=j == 0, stop=j == i)
                did(T_, ins.then_inc(tensor_done, 1), f"{t0}o{n}")
            N = len(ORDER)
            for n in range(N + 2):
                if n < N:
                    score(n)
                if 1 <= n <= N:
                    turn(n - 1)
                if n >= 2:
                    value(n - 2)

        def mla_scalar(act, l):
            t0 = f"i{l}."
            for nm, n, o in (("cq", 3, CQ), ("ckv", 2, CKV)):
                for m in range(n):
                    t = tile(act, f"{t0}{nm}{m}")
                    did(A_, act.activation(o[:, m, :], t, ACT.Copy).then_inc(scalar_done, 1), f"{t0}c{nm}{m}")
                    did(A_, act.activation(TQ[:, m + (3 if nm == "ckv" else 0), :], t, ACT.Square).then_inc(scalar_done, 1), f"{t0}q{nm}{m}")
                    marks[f"free.{t0}{nm}{m}"] = (A_, count[A_])
            for nm, n, c in (("cq", 384, 0), ("ckv", 256, 1)):
                t = tile(act, f"{t0}s{nm}")
                did(A_, act.activation(RC[:, c, :], t, ACT.Sqrt, bias=eps[:, 0:1], scale=1.0 / n).then_inc(scalar_done, 1), f"free.{t0}s{nm}")
            for h in range(6):
                t = tile(act, f"{t0}k{h}")
                did(A_, act.activation(KTT[0:64, h, :], t[0:64, :], ACT.Copy).then_inc(scalar_done, 1), f"free.{t0}k{h}")
            for tt in range(4):
                t = tile(act, f"{t0}vt{tt}")
                did(A_, act.activation(VT[:, tt, :], t[:, 0:384], ACT.Copy).then_inc(scalar_done, 1), f"free.{t0}vt{tt}")

            def soft(n):
                h, i = ORDER[n]
                w = (i + 1) * P
                t = tile(act, f"{t0}sc{n}")
                if later(act, f"{t0}mx{n}"):
                    act.wait_ge(*at(f"{t0}mx{n}"))
                if n >= 2:
                    if later(act, f"{t0}pt{n - 2}"):
                        act.wait_ge(*at(f"{t0}pt{n - 2}"))
                did(A_, act.activation(PB[:, n % 2, 0:w], t[:, 0:w], ACT.Exp, bias=AST[:, 1, n:n + 1], scale=SCALE,
                                       accum_out=AST[:, 2, n:n + 1]).then_inc(scalar_done, 1), f"free.{t0}sc{n}")

            def turned(n):
                h, i = ORDER[n]
                w = (i + 1) * P
                t = tile(act, f"{t0}pt{n}")
                if n >= 2:
                    if later(act, f"{t0}o{n - 2}"):
                        act.wait_ge(*at(f"{t0}o{n - 2}"))
                did(A_, act.activation(PTT[:, n % 2, 0:w], t[:, 0:w], ACT.Copy).then_inc(scalar_done, 1), f"free.{t0}pt{n}")
            N = len(ORDER)
            for n in range(N + 1):
                if n < N:
                    soft(n)
                if n >= 1:
                    turned(n - 1)

        def mla_vector(dve, l):
            t0 = f"i{l}."
            if later(dve, f"mlac{l}"):
                dve.wait_ge(*at(f"mlac{l}"))
            for s in range(2):
                t = tile(dve, f"{t0}kr{s}")
                did(V, dve.tensor_tensor(TQ[HR, s, :] if False else KTT[HR, s, :], t[HR, :], TR[HR, s, :], ALU.mult).then_inc(vector_done, 1), f"free.{t0}kr{s}")
            dve.wait_ge(*own(dve, V))
            did(V, dve.tensor_tensor(KW[HR, :], KTT[HR, 0, :], KTT[HR, 1, :], ALU.add).then_inc(vector_done, 1))
            dve.wait_ge(*own(dve, V))
            did(V, dve.tensor_copy(KTT[HR, :, :], KW[HR, :].unsqueeze(1).to_broadcast([32, 6, TX])).then_inc(vector_done, 1))
            for nm, n, c, o, g in (("cq", 3, 0, CQ, "qg"), ("ckv", 2, 1, CKV, "kvg")):
                if later(dve, f"free.{t0}s{nm}"):
                    dve.wait_ge(*at(f"free.{t0}s{nm}"))
                did(V, dve.reciprocal(RC[:, c, :], RC[:, c, :]).then_inc(vector_done, 1))
                dve.wait_ge(*own(dve, V))
                for m in range(n):
                    if later(dve, f"{t0}c{nm}{m}"):
                        dve.wait_ge(*at(f"{t0}c{nm}{m}"))
                    did(V, dve.scalar_tensor_tensor(o[:, m, :], o[:, m, :], col(g, n * l + m), RC[:, c, :],
                                                    ALU.mult, ALU.mult).then_inc(vector_done, 1))
                marks[f"{t0}n{nm}"] = (V, count[V])
            for h in range(6):
                t = tile(dve, f"{t0}q{h}")
                did(V, dve.tensor_copy(QT[0:64, h, :], t[0:64, :]).then_inc(vector_done, 1))
                did(V, dve.tensor_tensor(QT[HR, h, :], t[HR, :], TR[HR, 0, :], ALU.mult).then_inc(vector_done, 1), f"free.{t0}q{h}")
                t = tile(dve, f"{t0}qw{h}")
                if h:
                    dve.wait_ge(*own(dve, V))
                did(V, dve.tensor_tensor(KW[HR, :], t[HR, :], TR[HR, 1, :], ALU.mult).then_inc(vector_done, 1), f"free.{t0}qw{h}")
                dve.wait_ge(*own(dve, V))
                did(V, dve.tensor_tensor(QT[HR, h, :], QT[HR, h, :], KW[HR, :], ALU.add).then_inc(vector_done, 1), f"{t0}qt{h}")
            for h in range(6):
                marks[f"{t0}kt{h}"] = (A_, 0)
            N = len(ORDER)

            def mx(n):
                h, i = ORDER[n]
                w = (i + 1) * P
                t = tile(dve, f"{t0}sc{n}")
                did(V, dve.tensor_reduce(AST[:, 0, n:n + 1], t[:, 0:w], AX, ALU.max).then_inc(vector_done, 1))
                dve.wait_ge(*own(dve, V))
                did(V, dve.tensor_scalar(AST[:, 1, n:n + 1], AST[:, 0, n:n + 1], -SCALE, None, ALU.mult).then_inc(vector_done, 1), f"{t0}mx{n}")

            def norm(n):
                h, i = ORDER[n]
                w = (i + 1) * P
                if later(dve, f"free.{t0}sc{n}"):
                    dve.wait_ge(*at(f"free.{t0}sc{n}"))
                did(V, dve.reciprocal(AST[:, 3, n:n + 1], AST[:, 2, n:n + 1]).then_inc(vector_done, 1))
                dve.wait_ge(*own(dve, V))
                did(V, dve.tensor_scalar(PB[:, n % 2, 0:w], PB[:, n % 2, 0:w], AST[:, 3, n:n + 1], None, ALU.mult).then_inc(vector_done, 1), f"{t0}pn{n}")

            def outv(n):
                h, i = ORDER[n]
                t = tile(dve, f"{t0}o{n}")
                did(V, dve.tensor_copy(MIX[rows(h % 2), 5 + h // 2, i * P:i * P + P], t[rows(h % 2), 0:P]).then_inc(vector_done, 1), f"free.{t0}o{n}")
            for n in range(N + 2):
                if n < N:
                    mx(n)
                    norm(n)
                if n >= 2:
                    outv(n - 2)

        UU = S(4096, 2, TX)
        VG = S(5120, 4, 256)
        VN = S(6144, 4, 256)
        WST = S(7168, 4, P)
        GBC = S(7680, 256)
        GB = S(7936, 2, P)
        CAUS = S(8192, P)
        VS = S(8320, 2, 4)
        GSQ = S(8328, 256)

        def gmlp_pool(pool, l):
            did("aux", pool.dma_start(WST, a["wsT"][l].rearrange("h s t -> s h t")).then_inc(constants_in, 16), by=16)
            did("aux", pool.dma_start(GBC, a["vng"][l]).then_inc(constants_in, 16), by=16)
            did("aux", pool.dma_start(GB, a["gbs"][l].rearrange("p (m t) -> p m t", t=P)).then_inc(constants_in, 16), by=16)
            did("aux", pool.dma_start(CAUS, a["caus"]).then_inc(constants_in, 16), f"gmc{l}", by=16)

        def gmlp_tensor(pe, l):
            t0 = f"i{l}."
            w = weight(pe, f"{t0}v")
            for tt in range(4):
                b = bank(pe, f"{t0}gv{tt}")
                for k in range(KT):
                    ins = pe.matmul(b[:, 0:256], H[:, k, tt * P:tt * P + P], w[:, k, :], start=k == 0, stop=k == KT - 1)
                did(T_, ins.then_inc(tensor_done, 1), f"{t0}gv{tt}")
            marks[f"wf.{t0}v"] = (T_, count[T_])
            w = weight(pe, f"{t0}u")
            for m in range(2):
                b = bank(pe, f"{t0}gu{m}")
                for k in range(KT):
                    ins = pe.matmul(b, w[:, k, m * P:m * P + P], H[:, k, 0:TX], start=k == 0, stop=k == KT - 1)
                did(T_, ins.then_inc(tensor_done, 1), f"{t0}gu{m}")
            marks[f"wf.{t0}u"] = (T_, count[T_])
            if later(pe, f"{t0}wst"):
                pe.wait_ge(*at(f"{t0}wst"))
            if later(pe, f"{t0}vn"):
                pe.wait_ge(*at(f"{t0}vn"))
            for m in range(2):
                b = bank(pe, f"{t0}gm{m}")
                for q in range(2):
                    h = 2 * m + q
                    for c in range(4):
                        ins = pe.matmul(b[rows(q), c * P:c * P + P], VN[:, c, 64 * h:64 * h + 64], WST[:, h, :],
                                        start=True, stop=True)
                did(T_, ins.then_inc(tensor_done, 1), f"{t0}gm{m}")

        def gmlp_scalar(act, l):
            t0 = f"i{l}."
            for tt in range(4):
                t = tile(act, f"{t0}gv{tt}")
                did(A_, act.activation(VG[:, tt, :], t[:, 0:256], ACT.Gelu_apprx_tanh).then_inc(scalar_done, 1), f"free.{t0}gv{tt}")
            for m in range(2):
                t = tile(act, f"{t0}gu{m}")
                did(A_, act.activation(UU[:, m, :], t, ACT.Gelu_apprx_tanh).then_inc(scalar_done, 1), f"free.{t0}gu{m}")
            if later(act, f"{t0}vs"):
                act.wait_ge(*at(f"{t0}vs"))
            did(A_, act.activation(VS[:, 1, :], VS[:, 0, :], ACT.Sqrt, bias=eps[:, 0:1], scale=1.0 / 256).then_inc(scalar_done, 1), f"{t0}vsq")

        def gmlp_vector(dve, l):
            t0 = f"i{l}."
            if later(dve, f"gmc{l}"):
                dve.wait_ge(*at(f"gmc{l}"))
            did(V, dve.tensor_tensor(WST[:, :, :], WST[:, :, :], CAUS.unsqueeze(1).to_broadcast([P, 4, P]), ALU.mult).then_inc(vector_done, 1), f"{t0}wst")
            for tt in range(4):
                if later(dve, f"free.{t0}gv{tt}"):
                    dve.wait_ge(*at(f"free.{t0}gv{tt}"))
                if tt:
                    dve.wait_ge(*own(dve, V))
                did(V, dve.scalar_tensor_tensor(GSQ, VG[:, tt, :], 1.0, VG[:, tt, :], ALU.mult, ALU.mult,
                                                accum_out=VS[:, 0, tt:tt + 1]).then_inc(vector_done, 1))
            marks[f"{t0}vs"] = (V, count[V])
            if later(dve, f"{t0}vsq"):
                dve.wait_ge(*at(f"{t0}vsq"))
            did(V, dve.reciprocal(VS[:, 1, :], VS[:, 1, :]).then_inc(vector_done, 1))
            dve.wait_ge(*own(dve, V))
            for tt in range(4):
                did(V, dve.scalar_tensor_tensor(VN[:, tt, :], VG[:, tt, :], VS[:, 1, tt:tt + 1], GBC, ALU.mult, ALU.mult).then_inc(vector_done, 1))
            marks[f"{t0}vn"] = (V, count[V])
            for m in range(2):
                t = tile(dve, f"{t0}gm{m}").rearrange("p (c t) -> p c t", t=P)
                mm = MIX[:, m, :].rearrange("p (c t) -> p c t", t=P)
                did(V, dve.tensor_tensor(mm, t, GB[:, m, :].unsqueeze(1).to_broadcast([P, 4, P]), ALU.add).then_inc(vector_done, 1), f"free.{t0}gm{m}")
                dve.wait_ge(*own(dve, V))
                if later(dve, f"free.{t0}gu{m}"):
                    dve.wait_ge(*at(f"free.{t0}gu{m}"))
                did(V, dve.tensor_tensor(MIX[:, m, :], MIX[:, m, :], UU[:, m, :], ALU.mult).then_inc(vector_done, 1))

        SZ = S(4096, 3, TX)
        RAW = S(5632, 5, TX)
        XBC = S(8192, 5, TX)
        TOK = S(10752, 4, 512)
        XW = S(12800, 24, 64)
        ABS = S(14336, 6, TX)
        WW = S(17408, 6, TX)
        RG = S(17408, 2, TX)
        YQ = S(18432, 3, TX)
        CB = S(20480, 2, 512)
        HS = S(12800, 4, 192)
        DTW = [scr[0:6, 5632 + 512 * n:6144 + 512 * n] for n in range(5)]
        SEL6 = scr[0:6, 8192 - 2560:8192 - 2560 + 768]
        AC2 = S(21504, 2, 24)
        DEC = S(21552, 2, 24)
        STT_ = S(21600, 192)
        SM6 = small[0:6, 64:68]
        CAU2 = S(21792, P)
        SE = S(5632 + 2560 - 1024, 2, 512)

        def ssd_pool(pool, l):
            did("aux", pool.dma_start(SM6, a["sm6"]).then_inc(constants_in, 16), by=16)
            did("aux", pool.dma_start(CAU2, a["caus"]).then_inc(constants_in, 16), by=16)
            did("aux", pool.dma_start(small[0:6, 72:74], a["sm6"][:, 0:2]).then_inc(constants_in, 16), f"ssc{l}", by=16)
            if later(pool, f"i{l}.sdt"):
                pool.wait_ge(*at(f"i{l}.sdt"))
            did("aux", pool.dma_start(H[0:6, 0, 0:768], a["sel6"]).then_inc(constants_in, 16), by=16)
            did("aux", pool.dma_start(H[0:6, 1, 0:512], a["rst128"]).then_inc(constants_in, 16), f"ssd2{l}", by=16)

        HF = H[:, :, :].rearrange("p k t -> p (k t)")
        DT = [HF[0:6, 2 * TA + 512 * n:2 * TA + 512 * n + 512] for n in range(5)]
        SELH = HF[0:6, 0:768].rearrange("p (h c) -> p h c", c=P)
        RS6 = HF[0:6, TA:TA + 512]
        SEH = HF[:, 5120:6144].rearrange("p (b n) -> p b n", b=2)

        def ssd_tensor(pe, l):
            t0 = f"i{l}."
            w = weight(pe, f"{t0}dt")
            b = bank(pe, f"{t0}dt")
            for k in range(KT):
                ins = pe.matmul(b[0:6, :], w[:, k, :], H[:, k, 0:TX], start=k == 0, stop=k == KT - 1)
            did(T_, ins.then_inc(tensor_done, 1), f"{t0}dt")
            marks[f"wf.{t0}dt"] = (T_, count[T_])
            for nm, n in (("xbc", 5), ("z", 3)):
                for m in range(n):
                    w = weight(pe, f"{t0}{nm}.{m // 2}")
                    b = bank(pe, f"{t0}{nm}{m}")
                    for k in range(KT):
                        ins = pe.matmul(b, w[:, k, (m % 2) * P:(m % 2) * P + P], H[:, k, 0:TX], start=k == 0, stop=k == KT - 1)
                    did(T_, ins.then_inc(tensor_done, 1), f"{t0}{nm}{m}")
                    if m % 2 or m == n - 1:
                        marks[f"wf.{t0}{nm}.{m // 2}"] = (T_, count[T_])
            marks[f"{t0}sdt"] = (T_, count[T_])
            if later(pe, f"ssd2{l}"):
                pe.wait_ge(*at(f"ssd2{l}"))
            if later(pe, f"{t0}ac"):
                pe.wait_ge(*at(f"{t0}ac"))
            for h in range(6):
                b = bank(pe, f"{t0}ab{h}")
                did(T_, pe.matmul(b, SELH[:, h, :], DT[4], start=True, stop=True).then_inc(tensor_done, 1), f"{t0}ab{h}")
            b = bank(pe, f"{t0}tk")
            for n, src in enumerate((DT[4], DT[3])):
                for c in range(4):
                    o = 24 * n + 6 * c
                    ins = pe.transpose(b[:, o:o + 6], src[:, c * P:c * P + P], ident[0:6, 0:6])
            did(T_, ins.then_inc(tensor_done, 1), f"{t0}tk")
            for c in range(4):
                b = bank(pe, f"{t0}tok{c}")
                for m in range(4):
                    if later(pe, f"{t0}xc{m}"):
                        pe.wait_ge(*at(f"{t0}xc{m}"))
                    ins = pe.transpose(b[:, m * P:m * P + P], XBC[:, m, c * P:c * P + P], ident[:, :])
                did(T_, ins.then_inc(tensor_done, 1), f"{t0}tok{c}")
            if later(pe, f"{t0}xc4"):
                pe.wait_ge(*at(f"{t0}xc4"))
            for g in range(2):
                b = bank(pe, f"{t0}cb{g}")
                for c in range(4):
                    ins = pe.matmul(b[:, c * P:c * P + P], XBC[rows(g), 3, c * P:c * P + P], XBC[rows(g), 4, c * P:c * P + P],
                                    start=True, stop=True)
                did(T_, ins.then_inc(tensor_done, 1), f"{t0}cb{g}")
            for c in range(4):
                b = bank(pe, f"{t0}st{c}")
                if later(pe, f"{t0}xw"):
                    pe.wait_ge(*at(f"{t0}xw"))
                for g in range(2):
                    ins = pe.matmul(b[rows(g), 0:192], TOK[:, c, 384 + 64 * g:448 + 64 * g], XW[:, 6 * c + 3 * g:6 * c + 3 * g + 3, :],
                                    start=True, stop=True)
                did(T_, ins.then_inc(tensor_done, 1), f"{t0}st{c}")
            for m in range(3):
                b = bank(pe, f"{t0}ya{m}")
                for q in range(2):
                    h = 2 * m + q
                    if later(pe, f"{t0}w{h}"):
                        pe.wait_ge(*at(f"{t0}w{h}"))
                    for c in range(4):
                        ins = pe.matmul(b[rows(q), c * P:c * P + P], TOK[:, c, 64 * h:64 * h + 64], WW[:, h, c * P:c * P + P],
                                        start=True, stop=True)
                did(T_, ins.then_inc(tensor_done, 1), f"{t0}ya{m}")
                b = bank(pe, f"{t0}yo{m}")
                if later(pe, f"{t0}hs"):
                    pe.wait_ge(*at(f"{t0}hs"))
                for q in range(2):
                    h = 2 * m + q
                    g = h // 3
                    for c in range(4):
                        ins = pe.matmul(b[rows(q), c * P:c * P + P], HS[rows(g), c, 64 * (h % 3):64 * (h % 3) + 64],
                                        XBC[rows(g), 4, c * P:c * P + P], start=True, stop=True)
                did(T_, ins.then_inc(tensor_done, 1), f"{t0}yo{m}")
            if later(pe, f"{t0}yq"):
                pe.wait_ge(*at(f"{t0}yq"))
            b = bank(pe, f"{t0}sg0")
            pe.matmul(b, ones[:, :], YQ[:, 0, :], start=True, stop=False)
            did(T_, pe.matmul(b, ones[0:64, :], YQ[0:64, 1, :], start=False, stop=True).then_inc(tensor_done, 1), f"{t0}sg0")
            b = bank(pe, f"{t0}sg1")
            pe.matmul(b, ones[:, :], YQ[:, 2, :], start=True, stop=False)
            did(T_, pe.matmul(b, ones[64:128, :], YQ[64:128, 1, :], start=False, stop=True).then_inc(tensor_done, 1), f"{t0}sg1")

        def ssd_scalar(act, l):
            t0 = f"i{l}."
            if later(act, f"{t0}ady"):
                act.wait_ge(*at(f"{t0}ady"))
            did(A_, act.activation(DTB(l)[1], DTB(l)[1], ACT.Exp, scale=-1.0).then_inc(scalar_done, 1))
            act.wait_ge(*own(act, A_))
            did(A_, act.activation(DTB(l)[1], DTB(l)[1], ACT.Ln, bias=1.0).then_inc(scalar_done, 1))
            if later(act, f"ssc{l}"):
                act.wait_ge(*at(f"ssc{l}"))
            did(A_, act.activation(small[0:6, 70:71], SM6[:, 2 + l:3 + l], ACT.Exp).then_inc(scalar_done, 1), f"{t0}ln")
            for m in range(5):
                if later(act, f"{t0}cv{m}"):
                    act.wait_ge(*at(f"{t0}cv{m}"))
                did(A_, act.activation(XBC[:, m, :], XBC[:, m, :], ACT.Silu).then_inc(scalar_done, 1), f"{t0}xc{m}")
            for m in range(3):
                t = tile(act, f"{t0}z{m}")
                did(A_, act.activation(SZ[:, m, :], t, ACT.Silu).then_inc(scalar_done, 1), f"free.{t0}z{m}")
            for h in range(6):
                t = tile(act, f"{t0}ab{h}")
                did(A_, act.activation(ABS[:, h, :], t, ACT.Copy).then_inc(scalar_done, 1), f"free.{t0}ab{h}")
            for c in range(4):
                t = tile(act, f"{t0}tok{c}")
                did(A_, act.activation(TOK[:, c, :], t, ACT.Copy).then_inc(scalar_done, 1), f"free.{t0}tok{c}")
            if later(act, f"{t0}dc"):
                act.wait_ge(*at(f"{t0}dc"))
            did(A_, act.activation(DEC[:, :, :], DEC[:, :, :], ACT.Exp).then_inc(scalar_done, 1), f"{t0}dce")
            for h in range(6):
                if later(act, f"{t0}sg_{h}"):
                    act.wait_ge(*at(f"{t0}sg_{h}"))
                if h >= 2:
                    if later(act, f"{t0}w{h - 2}"):
                        act.wait_ge(*at(f"{t0}w{h - 2}"))
                did(A_, act.activation(SEH[:, h % 2, :], WW[:, h, :], ACT.Exp).then_inc(scalar_done, 1), f"{t0}se{h}")
            for h in range(6):
                did(A_, act.activation(ABS[:, h, :], ABS[:, h, :], ACT.Exp).then_inc(scalar_done, 1), f"{t0}ea{h}")
            for g in range(2):
                t = tile(act, f"{t0}sg{g}")
                did(A_, act.activation(RG[:, g, :], t, ACT.Sqrt, bias=eps[:, 0:1], scale=1.0 / 192).then_inc(scalar_done, 1), f"free.{t0}sg{g}")

        def DTB(l):
            return [scr[0:6, 17408 + 512 * n:17920 + 512 * n] for n in range(2)]

        def ssd_vector(dve, l):
            t0 = f"i{l}."
            y0, y1 = DTB(l)
            if later(dve, f"ssc{l}"):
                dve.wait_ge(*at(f"ssc{l}"))
            t = tile(dve, f"{t0}dt")
            did(V, dve.tensor_scalar(y0, t[0:6, :], SM6[:, l:l + 1], None, ALU.add).then_inc(vector_done, 1), f"free.{t0}dt")
            dve.wait_ge(*own(dve, V))
            did(V, dve.scalar_tensor_tensor(y1, y0, -1.0, y0, ALU.mult, ALU.max).then_inc(vector_done, 1), f"{t0}ady")
            for m in range(5):
                t = tile(dve, f"{t0}xbc{m}")
                did(V, dve.tensor_copy(RAW[:, m, :], t).then_inc(vector_done, 1), f"free.{t0}xbc{m}")
                dve.wait_ge(*own(dve, V))
                cw = [col("convw", 20 * l + 5 * j + m) for j in range(4)]
                did(V, dve.tensor_scalar(XBC[:, m, :], RAW[:, m, :], cw[3], col("convb", 5 * l + m), ALU.mult, ALU.add).then_inc(vector_done, 1))
                for j in (2, 1, 0):
                    s = 3 - j
                    dve.wait_ge(*own(dve, V))
                    did(V, dve.scalar_tensor_tensor(XBC[:, m, s:TX], RAW[:, m, 0:TX - s], cw[j], XBC[:, m, s:TX],
                                                    ALU.mult, ALU.add).then_inc(vector_done, 1))
                marks[f"{t0}cv{m}"] = (V, count[V])
            if later(dve, f"{t0}ln"):
                dve.wait_ge(*at(f"{t0}ln"))
            if later(dve, f"{t0}sdt"):
                dve.wait_ge(*at(f"{t0}sdt"))
            if later(dve, f"ssd2{l}"):
                dve.wait_ge(*at(f"ssd2{l}"))
            did(V, dve.scalar_tensor_tensor(DT[3], y0, 0.0, y1, ALU.max, ALU.add).then_inc(vector_done, 1))
            dve.wait_ge(*own(dve, V))
            did(V, dve.tensor_scalar(DT[0], DT[3], small[0:6, 70:71], -1.0, ALU.mult, ALU.mult).then_inc(vector_done, 1))
            dve.wait_ge(*own(dve, V))
            did(V, dve.tensor_tensor_scan(DT[4], RS6, DT[0], 0.0, ALU.mult, ALU.add).then_inc(vector_done, 1), f"{t0}ac")
            t = tile(dve, f"{t0}tk")
            did(V, dve.tensor_copy(AC2[:, :, :], t[:, 0:48].rearrange("p (n c) -> p n c", n=2)).then_inc(vector_done, 1), f"free.{t0}tk")
            for step in [f"free.{t0}ab{h}" for h in range(6)]:
                if later(dve, step):
                    dve.wait_ge(*at(step))
            dve.wait_ge(*own(dve, V))
            ends = ABS[:, :, :].rearrange("p h (c t) -> p c h t", t=P)[:, :, :, P - 1]
            a2 = AC2[:, 0, :].rearrange("p (c h) -> p c h", h=6)
            did(V, dve.tensor_tensor(DEC[:, 0, :].rearrange("p (c h) -> p c h", h=6), ends, a2, ALU.subtract).then_inc(vector_done, 1))
            did(V, dve.tensor_copy(DEC[:, 1, :].rearrange("p (c h) -> p c h", h=6), ends).then_inc(vector_done, 1), f"{t0}dc")
            for g in range(2):
                t = tile(dve, f"{t0}cb{g}")
                did(V, dve.tensor_tensor(CB[:, g, :].rearrange("p (c t) -> p c t", t=P), t.rearrange("p (c t) -> p c t", t=P),
                                         CAU2.unsqueeze(1).to_broadcast([P, 4, P]), ALU.mult).then_inc(vector_done, 1), f"free.{t0}cb{g}")
            if later(dve, f"{t0}dce"):
                dve.wait_ge(*at(f"{t0}dce"))
            did(V, dve.tensor_tensor(DEC[:, 0, :], DEC[:, 0, :], AC2[:, 1, :], ALU.mult).then_inc(vector_done, 1))
            dve.wait_ge(*own(dve, V))
            if later(dve, f"free.{t0}tok3"):
                dve.wait_ge(*at(f"free.{t0}tok3"))
            for c in range(4):
                did(V, dve.tensor_tensor(XW[:, 6 * c:6 * c + 6, :], TOK[:, c, 0:384].rearrange("p (h c) -> p h c", c=64),
                                         DEC[:, 0, 6 * c:6 * c + 6].unsqueeze(2).to_broadcast([P, 6, 64]), ALU.mult).then_inc(vector_done, 1))
            marks[f"{t0}xw"] = (V, count[V])
            for h in range(6):
                for c in range(4):
                    did(V, dve.tensor_scalar(WW[:, h, c * P:c * P + P], ABS[:, h, c * P:c * P + P],
                                             AC2[:, 0, 6 * c + h:6 * c + h + 1], 0.0, ALU.subtract, ALU.min).then_inc(vector_done, 1))
                marks[f"{t0}sg_{h}"] = (V, count[V])
            for h in range(6):
                if later(dve, f"{t0}se{h}"):
                    dve.wait_ge(*at(f"{t0}se{h}"))
                for c in range(4):
                    did(V, dve.scalar_tensor_tensor(WW[:, h, c * P:c * P + P], CB[:, h // 3, c * P:c * P + P],
                                                    AC2[:, 1, 6 * c + h:6 * c + h + 1], SEH[:, h % 2, c * P:c * P + P],
                                                    ALU.mult, ALU.mult).then_inc(vector_done, 1))
                marks[f"{t0}w{h}"] = (V, count[V])
            if later(dve, f"{t0}st3"):
                dve.wait_ge(*at(f"{t0}st3"))
            did(V, dve.memset(HS[:, 0, :], 0.0).then_inc(vector_done, 1))
            dve.wait_ge(*own(dve, V))
            for c in range(4):
                t = tile(dve, f"{t0}st{c}")
                if c == 3:
                    did(V, dve.tensor_copy(STT_[:, 0:1], t[:, 0:1]).then_inc(vector_done, 1), f"free.{t0}st{c}")
                    continue
                for g in range(2):
                    dd = DEC[rows(g), 1, 6 * c + 3 * g:6 * c + 3 * g + 3].unsqueeze(2).to_broadcast([64, 3, 64])
                    did(V, dve.tensor_tensor(STT_[rows(g), :].rearrange("p (h c) -> p h c", c=64),
                                             HS[rows(g), c, :].rearrange("p (h c) -> p h c", c=64), dd, ALU.mult).then_inc(vector_done, 1))
                dve.wait_ge(*own(dve, V))
                did(V, dve.tensor_tensor(HS[:, c + 1, :], t[:, 0:192], STT_, ALU.add).then_inc(vector_done, 1), f"free.{t0}st{c}")
                dve.wait_ge(*own(dve, V))
            marks[f"{t0}hs"] = (V, count[V])
            for m in range(3):
                to = tile(dve, f"{t0}yo{m}")
                ta = tile(dve, f"{t0}ya{m}")
                y = MIX[:, 2 + m, :]
                for q in range(2):
                    if later(dve, f"{t0}ea{2 * m + q}"):
                        dve.wait_ge(*at(f"{t0}ea{2 * m + q}"))
                    did(V, dve.tensor_tensor(MIX[rows(q), 2 + m, :], to[rows(q), :], ABS[rows(q), 2 * m + q, :], ALU.mult).then_inc(vector_done, 1))
                marks[f"free.{t0}yo{m}"] = (V, count[V])
                dve.wait_ge(*own(dve, V))
                did(V, dve.tensor_tensor(y, ta, y, ALU.add).then_inc(vector_done, 1), f"free.{t0}ya{m}")
                dve.wait_ge(*own(dve, V))
                did(V, dve.scalar_tensor_tensor(y, XBC[:, m, :], col("ssdd", 3 * l + m), y, ALU.mult, ALU.add).then_inc(vector_done, 1))
                dve.wait_ge(*own(dve, V))
                did(V, dve.tensor_tensor(y, y, SZ[:, m, :], ALU.mult).then_inc(vector_done, 1), f"{t0}yg{m}")
            if later(dve, f"{t0}yo2"):
                dve.wait_ge(*at(f"{t0}yo2"))
            dve.wait_ge(*own(dve, V))
            for m in range(3):
                did(V, dve.tensor_tensor(YQ[:, m, :], MIX[:, 2 + m, :], MIX[:, 2 + m, :], ALU.mult).then_inc(vector_done, 1))
            marks[f"{t0}yq"] = (V, count[V])
            if later(dve, f"free.{t0}sg0"):
                dve.wait_ge(*at(f"free.{t0}sg0"))
            if later(dve, f"free.{t0}sg1"):
                dve.wait_ge(*at(f"free.{t0}sg1"))
            did(V, dve.reciprocal(RG[:, :, :], RG[:, :, :]).then_inc(vector_done, 1))
            dve.wait_ge(*own(dve, V))
            for m, rr, g in ((0, slice(0, P), 0), (1, rows(0), 0), (1, rows(1), 1), (2, slice(0, P), 1)):
                did(V, dve.scalar_tensor_tensor(MIX[rr, 2 + m, :], MIX[rr, 2 + m, :],
                                                vec[rr, VEC["ssdg"] + 3 * l + m:VEC["ssdg"] + 3 * l + m + 1],
                                                RG[rr, g, :], ALU.mult, ALU.mult).then_inc(vector_done, 1))
            marks[f"{t0}mix"] = (V, count[V])

        HHI = S(0, KT, TX, of=scr_r)
        WHI = [S(4096 + 2048 * n, 2048, of=scr_r) for n in range(2)]
        HBH = S(8192, 16, TX, of=scr_r)
        HBL = S(16384, 8, TX, of=scr_r)
        RL = S(20480, 2, TX)

        def low_tile(f):
            if f < 8:
                return HBL[:, f, :].rearrange("p (a b) -> p a b", a=2)
            t = X_r if f < 12 else H_r
            return t[:, 2 * (f % 4):2 * (f % 4) + 2, TX:TA]

        def halves(t):
            return t.rearrange("p (a b) -> p a b", a=2)

        def mlp_slots(l):
            out = []
            for half in range(2):
                out += [(half, 1, i, 0, f"i{l}.m1.{8 * half + i}") for i in range(8)]
                out += [(half, 2, r, n, f"i{l}.m2.{n}.{4 * half + r}") for n in range(2) for r in range(4)]
            return out

        def mlp_tensor(pe, l):
            t0 = f"i{l}."
            for j, (half, kind, i, n, name) in enumerate(mlp_slots(l)):
                low = weight(pe, name, ring_r)
                high = WHI[j % 2].rearrange("p (k c) -> p k c", k=low.shape[1])
                if later(pe, "ws." + name):
                    pe.wait_ge(*at("ws." + name))
                if kind == 1:
                    for m in range(2):
                        f = 16 * half + 2 * i + m
                        b = bank(pe, f"{t0}m1.{f}")
                        for k in range(KT):
                            if later(pe, f"{t0}hl{k}"):
                                pe.wait_ge(*at(f"{t0}hl{k}"))
                            o = slice(m * P, m * P + P)
                            hh, hl = HHI[:, k, :], H_r[:, k, 0:TX]
                            pe.matmul(b, low[:, k, o], hh, start=k == 0, stop=False)
                            pe.matmul(b, high[:, k, o], hl, start=False, stop=False)
                            ins = pe.matmul(b, high[:, k, o], hh, start=False, stop=k == KT - 1)
                        did(T_, ins.then_inc(tensor_done, 1), f"{t0}m1.{f}")
                else:
                    if i == 0:
                        banks = [bank(pe, f"{t0}m2{half}.{4 * n + m}.0") for m in range(4)]
                    for m in range(4):
                        o = slice(m * P, m * P + P)
                        for k in range(4):
                            f = 4 * i + k
                            if later(pe, f"{t0}hb{16 * half + f}"):
                                pe.wait_ge(*at(f"{t0}hb{16 * half + f}"))
                            b3 = halves(banks[m])
                            hh, hl = HBH[:, f, :], low_tile(f)
                            pe.matmul(banks[m], low[:, k, o], hh, start=f == 0, stop=False)
                            pe.matmul(b3, high[:, k, o], hl, start=False, stop=False)
                            ins = pe.matmul(banks[m], high[:, k, o], hh, start=False, stop=f == 15)
                        if i == 3:
                            did(T_, ins.then_inc(tensor_done, 1), f"{t0}m2{half}.{4 * n + m}.0")
                    if i < 3:
                        did(T_, ins.then_inc(tensor_done, 1))
                marks["wf." + name] = (T_, count[T_])

        def mlp_scalar(act, l):
            t0 = f"i{l}."
            slots = mlp_slots(l)

            def high_weights(j):
                name = slots[j][4]
                if later(act, "w." + name):
                    act.wait_ge(*at("w." + name))
                if j >= 2:
                    if later(act, "wf." + slots[j - 2][4]):
                        act.wait_ge(*at("wf." + slots[j - 2][4]))
                did(A_, act.activation(WHI[j % 2], ring[:, place[name][0], :], ACT.Copy).then_inc(scalar_done, 1), f"wh.{name}")
            high_weights(0)
            for k in range(KT):
                did(A_, act.activation(HHI[:, k, :], H[:, k, 0:TX], ACT.Copy).then_inc(scalar_done, 1), f"{t0}hh{k}")
            high_weights(1)
            for j, (half, kind, i, n, name) in enumerate(slots):
                if kind == 1:
                    for f in (16 * half + 2 * i, 16 * half + 2 * i + 1):
                        t = tile(act, f"{t0}m1.{f}")
                        if f >= 2:
                            if later(act, f"{t0}hb{f - 2}"):
                                act.wait_ge(*at(f"{t0}hb{f - 2}"))
                        did(A_, act.activation(RL[:, f % 2, :], t, ACT.Relu).then_inc(scalar_done, 1), f"free.{t0}m1.{f}")
                    for f in (16 * half + 2 * i, 16 * half + 2 * i + 1):
                        if later(act, f"{t0}rl{f}"):
                            act.wait_ge(*at(f"{t0}rl{f}"))
                        if half and f == 16:
                            if later(act, f"wf.{slots[15][4]}"):
                                act.wait_ge(*at(f"wf.{slots[15][4]}"))
                        did(A_, act.activation(HBH[:, f % 16, :], RL[:, f % 2, :], ACT.Copy).then_inc(scalar_done, 1), f"{t0}hbh{f}")
                if j + 2 < len(slots):
                    high_weights(j + 2)
                if half and kind == 2 and i == 3:
                    residual_scalar(act, f"{t0}m21", XSEG, NEXT[f"mlp{l}"], range(4 * n, 4 * n + 4))

        def mlp_vector(dve, l):
            t0 = f"i{l}."
            slots = mlp_slots(l)

            def low_weights(j):
                name = slots[j][4]
                at_slot = place[name][0]
                if later(dve, f"wh.{name}"):
                    dve.wait_ge(*at(f"wh.{name}"))
                did(V, dve.tensor_tensor(ring_r[:, at_slot, :], ring[:, at_slot, :], WHI[j % 2].bitcast(F32), ALU.subtract).then_inc(vector_done, 1), f"ws.{name}")
            low_weights(0)
            for k in range(KT):
                if later(dve, f"{t0}hh{k}"):
                    dve.wait_ge(*at(f"{t0}hh{k}"))
                did(V, dve.tensor_tensor(H_r[:, k, 0:TX], H[:, k, 0:TX], HHI[:, k, :].bitcast(F32), ALU.subtract).then_inc(vector_done, 1), f"{t0}hl{k}")
            low_weights(1)
            for j, (half, kind, i, n, name) in enumerate(slots):
                if kind == 1:
                    for f in (16 * half + 2 * i, 16 * half + 2 * i + 1):
                        if later(dve, f"free.{t0}m1.{f}"):
                            dve.wait_ge(*at(f"free.{t0}m1.{f}"))
                        did(V, dve.tensor_tensor(RL[:, f % 2, :], RL[:, f % 2, :], RL[:, f % 2, :], ALU.mult).then_inc(vector_done, 1), f"{t0}rl{f}")
                    for f in (16 * half + 2 * i, 16 * half + 2 * i + 1):
                        if later(dve, f"{t0}hbh{f}"):
                            dve.wait_ge(*at(f"{t0}hbh{f}"))
                        did(V, dve.tensor_tensor(low_tile(f % 16), halves(RL[:, f % 2, :]),
                                                 halves(HBH[:, f % 16, :].bitcast(F32)), ALU.subtract).then_inc(vector_done, 1), f"{t0}hb{f}")
                elif i == 3:
                    residual_vector(dve, f"{t0}m2{half}", XSEG, None, NEXT[f"mlp{l}"] if half else None,
                                    range(4 * n, 4 * n + 4))
                if j + 2 < len(slots):
                    low_weights(j + 2)

        def stages():
            names = ["ada0", "n0", "fnet", "m0", "moe0", "ada1", "n1", "rw", "wkv", "post", "m1", "moe1", "fg"]
            for l in range(2):
                names += [f"n2{l}", f"mla{l}", f"gmlp{l}", f"ssd{l}", f"wout{l}", f"n3{l}", f"mlp{l}"]
            names = names[:names.index(STOP) + 1] if STOP else names
            return names + ["end"]

        def vgain(name, i):
            return lambda s, k: col(name, 8 * i + k)

        def again(n):
            return lambda s, k: gsc[:, n, k, s:s + 1]

        @block.tensor
        def _(pe):
            if later(pe, "const"):
                pe.wait_ge(*at("const"))
            for st in stages():
                if st in ("ada0", "ada1"):
                    ada_tensor(pe, int(st[3]))
                elif st in ("n0", "m0", "n1"):
                    norm_tensor(pe, st, SEGS)
                elif st == "m1" or st == "fg" or st[:2] in ("n2", "n3") or st == "end":
                    norm_tensor(pe, st, XSEG)
                elif st == "fnet":
                    fnet_tensor(pe)
                elif st[:3] == "moe":
                    moe_tensor(pe, int(st[3]))
                elif st == "rw":
                    rw_tensor(pe)
                elif st == "wkv":
                    wkv_tensor(pe)
                elif st == "post":
                    post_tensor(pe)
                elif st[:3] == "mla":
                    mla_tensor(pe, int(st[3]))
                elif st[:4] == "gmlp":
                    gmlp_tensor(pe, int(st[4]))
                elif st[:3] == "ssd":
                    ssd_tensor(pe, int(st[3]))
                elif st[:4] == "wout":
                    l = int(st[4])
                    linear_tensor(pe, f"wo{l}", f"i{l}.wout", lambda k, s0, sn: MIX[:, k, s0:s0 + sn], XSEG,
                                  lambda k: f"i{l}.mix")
                elif st[:3] == "mlp":
                    mlp_tensor(pe, int(st[3]))
                if st not in ("ada0", "ada1", "end"):
                    phase(pe, T_, st)

        @block.vector
        def _(dve):
            did(V, dve.memset(csil[:, :, :], 0.0).then_inc(vector_done, 1))
            did(V, dve.memset(ones[:, :], 1.0).then_inc(vector_done, 1))
            did(V, dve.memset(eps[:, 0:1], 1e-6).then_inc(vector_done, 1))
            did(V, dve.memset(eps[:, 1:2], 64e-5).then_inc(vector_done, 1))
            did(V, dve.memset(eps[:, 2:3], 1e-12).then_inc(vector_done, 1), "eps")
            if later(dve, "const"):
                dve.wait_ge(*at("const"))
            did(V, dve.tensor_scalar(small[:, 32:40], vec[:, VEC["ka"]:VEC["ka"] + 8], -1.0, 1.0, ALU.mult, ALU.add).then_inc(vector_done, 1))
            for st in stages():
                if st in ("ada0", "ada1"):
                    ada_vector(dve, int(st[3]))
                elif st in ("n0", "m0", "n1"):
                    norm_vector(dve, st, SEGS, again(0 if st[0] == "n" else 1), True)
                elif st == "m1":
                    norm_vector(dve, st, XSEG, again(1), True)
                elif st == "fg":
                    norm_vector(dve, st, XSEG, vgain("final_g", 0), False)
                    dve.wait_ge(*own(dve, V))
                    for k in range(KT):
                        did(V, dve.tensor_copy(X[:, k, 0:TX], H[:, k, 0:TX]).then_inc(vector_done, 1))
                elif st[:2] == "n2":
                    norm_vector(dve, st, XSEG, vgain("nmix", int(st[2])), False)
                elif st[:2] == "n3":
                    norm_vector(dve, st, XSEG, vgain("nmlp", int(st[2])), False)
                elif st == "end":
                    if STOP is None:
                        norm_vector(dve, st, XSEG, vgain("fin2", 0), False)
                    else:
                        if later(dve, "end.sq7"):
                            dve.wait_ge(*at("end.sq7"))
                        did(V, dve.tensor_copy(small[:, 0:1], small[:, 1:2]).then_inc(vector_done, 1), "end.sum")
                        if later(dve, "end.ss0"):
                            dve.wait_ge(*at("end.ss0"))
                        did(V, dve.tensor_copy(H[:, :, 0:TX], X[:, :, 0:TX]).then_inc(vector_done, 1))
                    marks["final"] = (V, count[V])
                elif st == "fnet":
                    fnet_vector(dve)
                elif st[:3] == "moe":
                    moe_vector(dve, int(st[3]))
                elif st == "rw":
                    rw_vector(dve)
                elif st == "wkv":
                    wkv_vector(dve)
                elif st == "post":
                    post_vector(dve)
                elif st[:3] == "mla":
                    mla_vector(dve, int(st[3]))
                elif st[:4] == "gmlp":
                    gmlp_vector(dve, int(st[4]))
                elif st[:3] == "ssd":
                    ssd_vector(dve, int(st[3]))
                elif st[:4] == "wout":
                    residual_vector(dve, f"wo{st[4]}", XSEG, None, NEXT[st])
                elif st[:3] == "mlp":
                    mlp_vector(dve, int(st[3]))
                if st not in ("ada0", "ada1", "end"):
                    phase(dve, V, st)
                    dve.wait_ge(*own(dve, V))

        @block.scalar
        def _(act):
            if later(act, "const"):
                act.wait_ge(*at("const"))
            if later(act, "eps"):
                act.wait_ge(*at("eps"))
            did(A_, act.activation(csil[:, :, 0:2], vec[:, VEC["c"]:VEC["c"] + 16].rearrange("p (k c) -> p k c", c=2),
                                   ACT.Silu).then_inc(scalar_done, 1), "csil")
            for st in stages():
                if st in ("n0", "m0", "n1"):
                    norm_scalar(act, st, SEGS, KT, (0,) if st[0] == "n" else (24,))
                elif st == "m1":
                    norm_scalar(act, st, XSEG, KT, (24,))
                elif st == "fg" or st[:2] in ("n2", "n3") or st == "end":
                    norm_scalar(act, st, XSEG, KT, None)
                elif st == "fnet":
                    fnet_scalar(act)
                elif st[:3] == "moe":
                    moe_scalar(act, int(st[3]))
                elif st == "rw":
                    rw_scalar(act)
                elif st == "wkv":
                    wkv_scalar(act)
                elif st == "post":
                    post_scalar(act)
                elif st[:3] == "mla":
                    mla_scalar(act, int(st[3]))
                elif st[:4] == "gmlp":
                    gmlp_scalar(act, int(st[4]))
                elif st[:3] == "ssd":
                    ssd_scalar(act, int(st[3]))
                elif st[:4] == "wout":
                    residual_scalar(act, f"wo{st[4]}", XSEG, NEXT[st])
                elif st[:3] == "mlp":
                    mlp_scalar(act, int(st[3]))
                if st not in ("ada0", "ada1", "end"):
                    phase(act, A_, st)
                    act.wait_ge(*own(act, A_))

        @block.gpsimd
        def _(pool):
            for st in stages():
                if st[:3] == "moe":
                    moe_pool(pool, int(st[3]))
                elif st == "rw":
                    rw_pool(pool)
                elif st == "wkv":
                    wkv_pool(pool)
                elif st == "post":
                    post_pool(pool)
                elif st[:3] == "mla":
                    mla_pool(pool, int(st[3]))
                elif st[:4] == "gmlp":
                    gmlp_pool(pool, int(st[4]))
                elif st[:3] == "ssd":
                    ssd_pool(pool, int(st[3]))
                if st not in ("ada0", "ada1", "end"):
                    phase(pool, G_, st)
                    if count[G_]:
                        pool.wait_ge(*own(pool, G_))
    return marks


def feature_cols(v):
    v = np.asarray(v)
    v = v.reshape(-1, v.shape[-1] // P, P)
    return v.transpose(2, 0, 1).reshape(P, -1)


def constants():
    f = np.float32
    c = {}

    def dft(n):
        ang = 2 * np.pi * (np.outer(np.arange(n), np.arange(n)) % n) / n
        return np.cos(ang) / np.sqrt(n), np.sin(ang) / np.sqrt(n)
    cs, sn = dft(256)
    c["dftC"] = np.concatenate([cs, sn], 1)
    c["dftTc"] = np.concatenate([cs, -sn], 1)
    cs, sn = dft(TX)
    c["dftT"] = np.concatenate([cs, -sn], 1)
    c["ident"] = np.eye(P)
    i = np.arange(P)
    c["bones"] = (i[:, None] // 64 == i[None] // 64)
    c["id64"] = (i[:, None] % 64 == np.arange(64)[None])
    c["iota"] = np.tile(np.arange(64), (P, 1))
    e = np.arange(NE)[:, None, None]
    pair = 2 * np.arange(8)[None, :, None] + (i // 64)[None, None]
    four = 4 * np.arange(4)[None, :, None] + (i // 32)[None, None]
    c["sel"] = np.concatenate([(e == pair), (e == four)], 1).reshape(NE, -1)
    s, t = np.arange(64)[:, None], np.arange(64)[None]
    md, lm = [], []
    for d in range(2):
        strict, incl = (s < t, s <= t) if d == 0 else (s > t, s >= t)
        md.append(np.tile(np.concatenate([strict, incl], 1), (2, 1)))
        for l in range(LEVELS):
            lo, hi = (s >> l, t >> l) if d == 0 else (t >> l, s >> l)
            lm.append(np.tile((lo % 2 == 0) & (hi == lo + 1), (2, 1)))
    c["md"] = np.concatenate(md, 1)
    c["lm"] = np.concatenate(lm, 1)
    c["rst"] = np.tile((np.arange(512) % 64 != 0), (P, 1))
    c["rst128"] = np.tile((np.arange(512) % 128 != 0), (6, 1))
    c["neg"] = np.where(i[None] <= i[:, None], 0.0, -1e30)
    c["caus"] = (i[:, None] <= i[None])
    c["sel6"] = (np.arange(6)[:, None, None] == np.arange(6)[None, :, None]) * np.ones((1, 1, P))
    c["sel6"] = c["sel6"].reshape(6, -1)
    inv = np.power(np.float32(10000.0), -np.arange(16, dtype=f) / np.float32(16))
    ang = np.arange(TX, dtype=f)[None] * inv[:, None].astype(f)
    co, si = np.cos(ang.astype(np.float64)), np.sin(ang.astype(np.float64))
    c["rope"] = np.concatenate([np.concatenate([co, co], 0), np.concatenate([-si, si], 0)], 1)
    c["iop"] = np.stack([i % 64, i % 32], 1)
    c["selc"] = np.stack([i % 32 == 0, i % 32 == 1], 1)
    return {k: np.ascontiguousarray(v, dtype=f) for k, v in c.items()}


def layout(x):
    c = constants()
    n = {k: np.asarray(v) for k, v in x.items()}
    parts = {
        "norm_g": feature_cols(n["norm_g"].reshape(4, D)), "fnet_bo": feature_cols(n["fnet_bo"]),
        "mix": feature_cols(n["rw_mix"][0]), "w0": feature_cols(n["rw_w0"][0]), "a0": feature_cols(n["rw_a0"][0]),
        "kk": feature_cols(n["rw_kk"]), "ka": feature_cols(n["rw_ka"]), "rk": feature_cols(n["rw_rk"].reshape(1, D)),
        "lnw": feature_cols(n["rw_lnx_w"]), "lnb": feature_cols(n["rw_lnx_b"]), "final_g": feature_cols(n["final_g"][None]),
        "nmix": feature_cols(n["norm_mix_g_2"]), "nmlp": feature_cols(n["norm_mlp_g_2"]),
        "fin2": feature_cols(n["final_norm_g_2"][None]), "ada_b": feature_cols(n["ada_b"]),
        "convw": feature_cols(n["ssd_conv_w_2"].reshape(8, 640)), "convb": feature_cols(n["ssd_conv_b_2"]),
        "ssdg": feature_cols(n["ssd_norm_g_2"]), "qg": feature_cols(n["mla_q_norm_g_2"]),
        "kvg": feature_cols(n["mla_kv_norm_g_2"]), "ssdd": feature_cols(np.repeat(n["ssd_d_2"], 64, axis=1)),
        "c": np.stack([feature_cols(n["c"]), feature_cols(n["c_ctx"][None])], 2).reshape(P, 16), "iop": c.pop("iop"), "selc": c.pop("selc"),
    }
    vecs = np.zeros((P, NVEC), np.float32)
    for k, v in parts.items():
        vecs[:, VEC[k]:VEC[k] + v.shape[1]] = v
    w_in, qb = n["w_in_2"], n["mla_w_qb_2"].reshape(2, 384, 6, 96)
    kr = w_in[:, :, 2182:2214]
    arrays = {
        "vecs": vecs, "xT": n["x"][0].T, "ctxT": n["ctx"][0].T,
        "w1cat": n["rw_w1"][0].transpose(1, 0, 2).reshape(D, P), "a1cat": n["rw_a1"][0].transpose(1, 0, 2).reshape(D, P),
        "w2cat": n["rw_w2"][0].reshape(P, D), "a2cat": n["rw_a2"][0].reshape(P, D),
        "krcat": np.concatenate([kr, kr[:, :, 16:], kr[:, :, :16]], 2),
        "qbsw": np.concatenate([qb[..., 80:96], qb[..., 64:80]], 3).reshape(2, 384, 192),
        "wsT": n["gmlp_w_s_2"].transpose(0, 1, 3, 2),
        "vng": np.repeat(n["gmlp_v_norm_g_2"][:, None, :], P, axis=1),
        "gbs": np.repeat(n["gmlp_b_s_2"].reshape(2, 2, 2, 128).transpose(0, 2, 1, 3).reshape(2, 2, 256), 64, axis=1),
        "sm6": np.concatenate([n["ssd_dt_bias_2"].T, n["ssd_a_log_2"].T], 1),
    }
    for k in ("ada_w", "fnet_wo", "rw_wr", "rw_wk", "rw_wv", "rw_wo", "rw_g1", "rw_g2", "moe_router", "moe_wg",
              "moe_wu", "moe_wd", "w_in_2", "mla_w_qb_2", "mla_w_kvb_2", "w_out_2", "mlp_w1_2", "mlp_w2_2"):
        arrays[k] = n[k]
    arrays.update(c)
    return {k: np.ascontiguousarray(v) for k, v in arrays.items()}


def kernel(**inputs):
    import concourse.bacc as bacc
    from concourse.bass_utils import run_bass_kernel_spmd

    arrays = layout(inputs)
    table = {}
    for _ in range(2):
        nc = bacc.Bacc("TRN2", target_bir_lowering=False, num_devices=1)
        aps = {k: nc.dram_tensor(f"in_{k}", v.shape, mybir.dt.from_np(v.dtype), kind="ExternalInput").ap()
               for k, v in arrays.items()}
        out = nc.dram_tensor("outT", (D, TX), F32, kind="ExternalOutput").ap()
        table = build(nc, aps, out, table)
    r = run_bass_kernel_spmd(nc, [{f"in_{k}": v for k, v in arrays.items()}], core_ids=[0])
    return np.ascontiguousarray(r.results[0]["outT"].T)[None]
```
